# Optimizing a Trainium2 kernel written in Bass

```python
import math
import jax, jax.numpy as jnp
from jax import lax
import numpy as np

D_MODEL = 1024
BATCH = 1
SEQ = 512
DEPTH = 1
DEC_BATCH = 8
DEC_SEQ = 8
PAST_LEN = 4096
PAGE_SIZE = 128

N_META = 16
NORM_EPS = 1e-6
CONV_A_DIM = D_MODEL
CONV_A_W = 3
SSD_INNER = 2 * D_MODEL
SSD_HEADDIM = 64
SSD_HEADS = SSD_INNER // SSD_HEADDIM
SSD_STATE = 128
SSD_GROUPS = 4
SSD_HPG = SSD_HEADS // SSD_GROUPS
SSD_CONV_W = 4
SSD_CONV_DIM = SSD_INNER + 2 * SSD_GROUPS * SSD_STATE
SSD_CHUNK = 128
IN_DIM = 3 * CONV_A_DIM + SSD_INNER + SSD_CONV_DIM + SSD_HEADS + 2 * D_MODEL
PEER_HEADS = 8
N_KEYS = 128
N_EXPERTS = N_KEYS * N_KEYS
PEER_TOPK = 16
PEER_QDIM = 256
PEER_HALF = PEER_QDIM // 2
PEER_BLOCK = 256

kernel_name = 'hybrid_shortconv_ssd_peer_step'

def rmsnorm(x, w):
    xf = x.astype(jnp.float32)
    inv = lax.rsqrt(jnp.mean(xf * xf, axis=-1, keepdims=True) + NORM_EPS)
    return (xf * inv).astype(x.dtype) * w.astype(x.dtype)

def causal_dwconv(x_padded, w):
    c = x_padded.shape[-1]
    return lax.conv_general_dilated(
        x_padded, w.astype(x_padded.dtype)[:, None, :], window_strides=(1,), padding='VALID',
        dimension_numbers=('NWC', 'WIO', 'NWC'), feature_group_count=c)

def split_in_proj(proj):
    sizes = (CONV_A_DIM, CONV_A_DIM, CONV_A_DIM, SSD_INNER, SSD_CONV_DIM, SSD_HEADS, D_MODEL, D_MODEL)
    points = np.cumsum(np.array(sizes))[:-1].tolist()
    return jnp.split(proj, points, axis=-1)

def ssd_chunked(x, dt, a, bm, cm, state0, chunk):
    b, L = x.shape[0], x.shape[1]
    nc = L // chunk
    x = x.reshape(b, nc, chunk, SSD_GROUPS, SSD_HPG, SSD_HEADDIM)
    dt = dt.reshape(b, nc, chunk, SSD_GROUPS, SSD_HPG)
    bm = bm.reshape(b, nc, chunk, SSD_GROUPS, SSD_STATE)
    cm = cm.reshape(b, nc, chunk, SSD_GROUPS, SSD_STATE)
    cum = jnp.cumsum(dt * a, axis=2)
    causal = jnp.tril(jnp.ones((chunk, chunk), dtype=bool))[:, :, None, None]
    seg = cum[:, :, :, None] - cum[:, :, None, :]
    decay = jnp.exp(jnp.where(causal, seg, -jnp.inf))
    cb = jnp.einsum('bcqgn,bckgn->bcqkg', cm, bm)
    w_qk = cb[..., None] * decay * dt[:, :, None]
    y_diag = jnp.einsum('bcqkgh,bckghp->bcqghp', w_qk, x)
    decay_end = jnp.exp(cum[:, :, -1:] - cum)
    chunk_states = jnp.einsum('bckgn,bckgh,bckghp->bcghpn', bm, decay_end * dt, x)
    chunk_decay = jnp.exp(cum[:, :, -1])

    def step(s, inp):
        d, cs = inp
        return d[..., None, None] * s + cs, s

    final, prev = lax.scan(step, state0, (jnp.moveaxis(chunk_decay, 1, 0), jnp.moveaxis(chunk_states, 1, 0)))
    prev = jnp.moveaxis(prev, 0, 1)
    y_off = jnp.einsum('bcqgn,bcghpn,bcqgh->bcqghp', cm, prev, jnp.exp(cum))
    y = (y_diag + y_off).reshape(b, L, SSD_GROUPS, SSD_HPG, SSD_HEADDIM)
    return y, final

def token_mixers(h, conv_a_prev, conv_ssd_prev, ssm_prev, segments,
                 w_in, conv_a_w, w_a_out, ssd_conv_w, ssd_conv_b, ssd_dt_bias, ssd_a_log,
                 ssd_d, ssd_norm_w, w_ssd_out, w_o):
    b, L, _ = h.shape
    dty = h.dtype
    a_b, a_c, a_x, z, xbc, dt_raw, g_a, g_b = split_in_proj(h @ w_in)
    u = a_c * a_x
    u_full = jnp.concatenate([conv_a_prev.astype(dty), u], axis=1)
    br_a = (a_b * causal_dwconv(u_full, conv_a_w)) @ w_a_out
    new_conv_a = u_full[:, u_full.shape[1] - (CONV_A_W - 1):]
    xbc_full = jnp.concatenate([conv_ssd_prev.astype(dty), xbc], axis=1)
    xbc_c = jax.nn.silu(causal_dwconv(xbc_full, ssd_conv_w) + ssd_conv_b.astype(dty))
    new_conv_ssd = xbc_full[:, xbc_full.shape[1] - (SSD_CONV_W - 1):]
    xs, bm, cm = jnp.split(xbc_c, [SSD_INNER, SSD_INNER + SSD_GROUPS * SSD_STATE], axis=-1)
    xh = xs.astype(jnp.float32).reshape(b, L, SSD_GROUPS, SSD_HPG, SSD_HEADDIM)
    bm = bm.astype(jnp.float32).reshape(b, L, SSD_GROUPS, SSD_STATE)
    cm = cm.astype(jnp.float32).reshape(b, L, SSD_GROUPS, SSD_STATE)
    dt = jax.nn.softplus(dt_raw.astype(jnp.float32) + ssd_dt_bias.astype(jnp.float32))
    dt = dt.reshape(b, L, SSD_GROUPS, SSD_HPG)
    a = -jnp.exp(ssd_a_log.astype(jnp.float32)).reshape(SSD_GROUPS, SSD_HPG)
    state = ssm_prev.astype(jnp.float32).reshape(b, SSD_GROUPS, SSD_HPG, SSD_HEADDIM, SSD_STATE)
    ys = []
    start = 0
    for length, chunk in segments:
        y_seg, state = ssd_chunked(xh[:, start:start + length], dt[:, start:start + length], a,
                                   bm[:, start:start + length], cm[:, start:start + length], state, chunk)
        ys.append(y_seg)
        start += length
    y = jnp.concatenate(ys, axis=1) + ssd_d.astype(jnp.float32).reshape(SSD_GROUPS, SSD_HPG, 1) * xh
    gated = (y.reshape(b, L, SSD_INNER) * jax.nn.silu(z.astype(jnp.float32))).reshape(b, L, SSD_GROUPS, -1)
    gated = gated * lax.rsqrt(jnp.mean(gated * gated, axis=-1, keepdims=True) + NORM_EPS)
    yn = gated.reshape(b, L, SSD_INNER).astype(dty) * ssd_norm_w.astype(dty)
    br_b = yn @ w_ssd_out
    merged = jax.nn.sigmoid(g_a) * br_a + jax.nn.sigmoid(g_b) * br_b
    new_ssm = state.reshape(b, SSD_HEADS, SSD_HEADDIM, SSD_STATE).astype(ssm_prev.dtype)
    return merged @ w_o, new_conv_a, new_conv_ssd, new_ssm

def peer(h, w_q, sub_keys, u_tab, v_tab):
    b, L, d = h.shape
    t = h.reshape(-1, d)
    n_tok = t.shape[0]
    n_blk = -(-n_tok // PEER_BLOCK)
    tp = jnp.pad(t, ((0, n_blk * PEER_BLOCK - n_tok), (0, 0))).reshape(n_blk, PEER_BLOCK, d)

    def block(tb):
        q = (tb @ w_q).reshape(PEER_BLOCK, PEER_HEADS, 2, PEER_HALF)
        s = jnp.einsum('thik,hink->thin', q, sub_keys.astype(q.dtype)).astype(jnp.float32)
        s_top, i_top = lax.top_k(s, PEER_TOPK)
        cand = (s_top[:, :, 0, :, None] + s_top[:, :, 1, None, :]).reshape(PEER_BLOCK, PEER_HEADS, PEER_TOPK * PEER_TOPK)
        best_s, best_c = lax.top_k(cand, PEER_TOPK)
        i1 = jnp.take_along_axis(i_top[:, :, 0], best_c // PEER_TOPK, axis=-1)
        i2 = jnp.take_along_axis(i_top[:, :, 1], best_c % PEER_TOPK, axis=-1)
        eid = i1 * N_KEYS + i2
        g = jax.nn.softmax(best_s, axis=-1)
        act = jax.nn.gelu(jnp.einsum('thkd,td->thk', u_tab[eid], tb).astype(jnp.float32), approximate=False)
        return jnp.einsum('thk,thkd->td', (g * act).astype(tb.dtype), v_tab[eid])

    out = lax.map(block, tp).reshape(-1, d)[:n_tok]
    return out.reshape(b, L, d)

def layer(x, conv_a_prev, conv_ssd_prev, ssm_prev, segments, lw):
    (norm_mix_w, w_in, conv_a_w, w_a_out, ssd_conv_w, ssd_conv_b, ssd_dt_bias, ssd_a_log, ssd_d,
     ssd_norm_w, w_ssd_out, w_o, norm_ffn_w, peer_w_q, peer_sub_keys, peer_u, peer_v) = lw
    mix, ca, cs, ss = token_mixers(rmsnorm(x, norm_mix_w), conv_a_prev, conv_ssd_prev, ssm_prev, segments,
                                   w_in, conv_a_w, w_a_out, ssd_conv_w, ssd_conv_b, ssd_dt_bias,
                                   ssd_a_log, ssd_d, ssd_norm_w, w_ssd_out, w_o)
    x = x + mix
    x = x + peer(rmsnorm(x, norm_ffn_w), peer_w_q, peer_sub_keys, peer_u, peer_v)
    return x, ca, cs, ss

def setup_inputs(seed: int = 0) -> dict:
    key = jax.random.key(seed)
    ks = jax.random.split(key, 32)
    f32 = jnp.float32
    nrm = lambda k, shape, scale: jax.random.normal(k, shape, f32) * scale
    dt_init = jnp.exp(jax.random.uniform(ks[10], (DEPTH, SSD_HEADS), f32, math.log(1e-3), math.log(1e-1)))
    return {
        'x_prompt': nrm(ks[0], (BATCH, SEQ, D_MODEL), 1.0),
        'x_sample': nrm(ks[1], (DEC_BATCH, DEC_SEQ, D_MODEL), 1.0),
        'state_conv_a': nrm(ks[2], (DEPTH, DEC_BATCH, CONV_A_W - 1, CONV_A_DIM), 1.0),
        'state_conv_ssd': nrm(ks[3], (DEPTH, DEC_BATCH, SSD_CONV_W - 1, SSD_CONV_DIM), 1.0),
        'state_ssm': nrm(ks[4], (DEPTH, DEC_BATCH, SSD_HEADS, SSD_HEADDIM, SSD_STATE), 0.1),
        'meta_tokens': nrm(ks[5], (N_META, D_MODEL), 1.0),
        'norm_mix_w': 1.0 + nrm(ks[6], (DEPTH, D_MODEL), 0.02),
        'w_in': nrm(ks[7], (DEPTH, D_MODEL, IN_DIM), D_MODEL ** -0.5),
        'conv_a_w': nrm(ks[8], (DEPTH, CONV_A_W, CONV_A_DIM), CONV_A_W ** -0.5),
        'w_a_out': nrm(ks[9], (DEPTH, CONV_A_DIM, D_MODEL), CONV_A_DIM ** -0.5),
        'ssd_conv_w': nrm(ks[11], (DEPTH, SSD_CONV_W, SSD_CONV_DIM), SSD_CONV_W ** -0.5),
        'ssd_conv_b': nrm(ks[12], (DEPTH, SSD_CONV_DIM), 0.01),
        'ssd_dt_bias': dt_init + jnp.log(-jnp.expm1(-dt_init)),
        'ssd_a_log': jnp.log(jax.random.uniform(ks[13], (DEPTH, SSD_HEADS), f32, 1.0, 16.0)),
        'ssd_d': 1.0 + nrm(ks[14], (DEPTH, SSD_HEADS), 0.1),
        'ssd_norm_w': 1.0 + nrm(ks[15], (DEPTH, SSD_INNER), 0.02),
        'w_ssd_out': nrm(ks[16], (DEPTH, SSD_INNER, D_MODEL), SSD_INNER ** -0.5),
        'w_o': nrm(ks[17], (DEPTH, D_MODEL, D_MODEL), D_MODEL ** -0.5),
        'norm_ffn_w': 1.0 + nrm(ks[18], (DEPTH, D_MODEL), 0.02),
        'peer_w_q': nrm(ks[19], (DEPTH, D_MODEL, PEER_HEADS * PEER_QDIM), D_MODEL ** -0.5),
        'peer_sub_keys': nrm(ks[20], (DEPTH, PEER_HEADS, 2, N_KEYS, PEER_HALF), PEER_HALF ** -0.5),
        'peer_u': nrm(ks[21], (DEPTH, N_EXPERTS, D_MODEL), D_MODEL ** -0.5),
        'peer_v': nrm(ks[22], (DEPTH, N_EXPERTS, D_MODEL), PEER_HEADS ** -0.5),
        'norm_final_w': 1.0 + nrm(ks[23], (D_MODEL,), 0.02),
    }

def reference(x_prompt, x_sample, state_conv_a, state_conv_ssd, state_ssm, meta_tokens,
              norm_mix_w, w_in, conv_a_w, w_a_out, ssd_conv_w, ssd_conv_b, ssd_dt_bias, ssd_a_log,
              ssd_d, ssd_norm_w, w_ssd_out, w_o, norm_ffn_w, peer_w_q, peer_sub_keys, peer_u, peer_v,
              norm_final_w):
    bp, s_len = x_prompt.shape[0], x_prompt.shape[1]
    bs, ds_len = x_sample.shape[0], x_sample.shape[1]
    dty = x_prompt.dtype
    meta = jnp.broadcast_to(meta_tokens.astype(dty)[None], (bp, N_META, D_MODEL))
    xp = jnp.concatenate([meta, x_prompt], axis=1)
    xs = x_sample
    seg_prompt = ((N_META, N_META), (s_len, SSD_CHUNK))
    seg_sample = ((ds_len, ds_len),)
    ca_p, cs_p, ss_p, ca_s, cs_s, ss_s = [], [], [], [], [], []
    for l in range(DEPTH):
        lw = (norm_mix_w[l], w_in[l], conv_a_w[l], w_a_out[l], ssd_conv_w[l], ssd_conv_b[l],
              ssd_dt_bias[l], ssd_a_log[l], ssd_d[l], ssd_norm_w[l], w_ssd_out[l], w_o[l],
              norm_ffn_w[l], peer_w_q[l], peer_sub_keys[l], peer_u[l], peer_v[l])
        zero_ca = jnp.zeros((bp, CONV_A_W - 1, CONV_A_DIM), dty)
        zero_cs = jnp.zeros((bp, SSD_CONV_W - 1, SSD_CONV_DIM), dty)
        zero_ss = jnp.zeros((bp, SSD_HEADS, SSD_HEADDIM, SSD_STATE), jnp.float32)
        xp, a1, a2, a3 = layer(xp, zero_ca, zero_cs, zero_ss, seg_prompt, lw)
        xs, b1, b2, b3 = layer(xs, state_conv_a[l], state_conv_ssd[l], state_ssm[l], seg_sample, lw)
        ca_p.append(a1); cs_p.append(a2); ss_p.append(a3)
        ca_s.append(b1); cs_s.append(b2); ss_s.append(b3)
    y_prompt = rmsnorm(xp[:, N_META:], norm_final_w)
    y_sample = rmsnorm(xs, norm_final_w)
    return (y_prompt, y_sample, jnp.stack(ca_p), jnp.stack(cs_p), jnp.stack(ss_p),
            jnp.stack(ca_s), jnp.stack(cs_s), jnp.stack(ss_s))


_drawn_inputs = setup_inputs


def setup_inputs(seed=0):
    import zlib

    import numpy as np

    out = dict(_drawn_inputs(seed))
    spreads = {}
    factors = {'ssd_conv_b': 3.666, 'ssd_norm_w': 8.775, 'norm_final_w': 24.361, 'norm_ffn_w': 12.853}
    for name, (base, spread) in spreads.items():
        noise = np.random.default_rng([zlib.crc32(name.encode()), seed]).standard_normal(out[name].shape)
        drawn = base * np.exp(spread * noise) if base else spread * noise
        out[name] = __import__('jax').numpy.asarray(drawn.astype(out[name].dtype))
    for name, factor in factors.items():
        out[name] = (out[name] * factor).astype(out[name].dtype)
    return out
```

```python
from contextlib import ExitStack

import concourse.bass as bass
from concourse import mybir

ALU = mybir.AluOpType
ACT = mybir.ActivationFunctionType
AX = mybir.AxisListType
F32 = mybir.dt.float32
F32R = mybir.dt.float32r
U32 = mybir.dt.uint32

P = 128
D = 1024
KT = D // P
N_META, SEQ = 16, 512
DEC_B, DEC_L = 8, 8
TP = N_META + SEQ
TS = DEC_B * DEC_L
T = TP + TS
HF = T // 2
HP = TP - HF
EPS = 1e-6
HEADS, HEADDIM, STATE = 32, 64, 128
GROUPS, HPG = 4, 8
GW = HPG * HEADDIM
XT = 2 * D // P
CT = XT + 2 * GROUPS
HA, HS = 2, 3
LA = HA + TP + DEC_B * (HA + DEC_L)
LS = HS + TP + DEC_B * (HS + DEC_L)
CHUNKS = [(0, N_META)] + [(N_META + P * c, P) for c in range(SEQ // P)] + [(TP, TS)]
NC = len(CHUNKS)
PH, NKEYS, TOPK = 8, 128, 16
TT = [(t, min(P, T - t)) for t in range(0, T, P)]
TB = 16
NB = T // TB
GI = 8
NG = NKEYS // GI
LOWEST = -3.0e38

N_DT, N_XBC, N_A, N_AO, N_GB, N_Z, N_SO, N_WO, N_WQ = 1, CT, 3 * KT, 2 * KT, KT, XT, 2 * KT, KT, 2 * KT
U_DT = 0
U_XBC = U_DT + N_DT
U_A = U_XBC + N_XBC
U_AO = U_A + N_A
U_GB = U_AO + N_AO
U_Z = U_GB + N_GB
U_SO = U_Z + N_Z
U_WO = U_SO + N_SO
U_WQ = U_WO + N_WO
U_PEER = U_WQ + N_WQ
UNITS = U_PEER + 2 * NKEYS
L_WO = U_SO + KT
L_SHIFT = U_WO - L_WO
RAW = 4
COLS = dict(mix=0, ffn=8, fin=16, ca=24, cs=48, cb=144, sn=168, dd=184)
NCOLS = 200


def trunk(nc, xT, units, keys, cols, heads, hist_a, hist_s, ssm_in,
          yT, new_a, new_s, ssm_p, ssm_s):
    gate_dram = nc.dram_tensor("gate_scratch", [NG, P, NB, GI, TB], F32).ap()
    base = ((nc.sbuf_base + 63) // 64) * 64
    end = nc.sbuf_usable_end
    with ExitStack() as ctx:
        def at(name, off, shape, dt=F32):
            n = 4
            for s in shape[1:]:
                n *= s
            assert base + off + n <= end, (name, off + n, end - base)
            return nc.alloc_sbuf_tensor_at(name, shape, dt, offset=base + off)

        def sem(name):
            return ctx.enter_context(nc.semaphore(name))

        TW = 4 * T
        LSB, LAB = ((4 * w + 31) // 32 * 32 for w in (LS, LA))
        pos = [0]

        def const(name, shape, dt=F32):
            n = 4
            for s in shape[1:]:
                n *= s
            r = at(name, pos[0], shape, dt)
            pos[0] += (n + 31) // 32 * 32
            return r

        ident = const("ident", [P, P])
        causal = const("causal", [P, P])
        smask = const("smask", [TS, DEC_B, DEC_L])
        rowmask = const("rowmask", [TS, DEC_B])
        iota_i = const("iota_i", [P, P], mybir.dt.int32)
        iota = const("iota", [P, P])
        ones = const("ones", [P, P])
        col = const("col", [P, NCOLS])
        hd = const("hd", [HEADS, 4])
        hista = const("hista", [P, KT, DEC_B, HA])
        hists = const("hists", [P, CT, DEC_B, HS])
        newa = const("newa", [P, KT, 1 + DEC_B, HA])
        news = const("news", [P, CT, 1 + DEC_B, HS])
        R_HT = pos[0]
        R_RING = R_HT + 2 * KT * TW
        R_XS = R_RING + (RAW + 4) * 4 * D
        R1 = R_XS + XT * TW
        R_TMP = R1 + 2 * KT * TW
        R_X = R_TMP + 18400
        R_MA = R_X + KT * TW
        h_hi = at("h_hi", R_HT, [P, KT, T], F32R)
        h_lo = at("h_lo", R_HT + KT * TW, [P, KT, T], F32R)
        m_hi = at("m_hi", R_HT, [P, KT, T], F32R)
        m_lo = at("m_lo", R_HT + KT * TW, [P, KT, T], F32R)
        g_hi = at("g_hi", R_HT, [P, KT, T], F32R)
        g_lo = at("g_lo", R_HT + KT * TW, [P, KT, T], F32R)
        raw = at("raw", R_RING, [P, RAW, D])
        w_hi = at("w_hi", R_RING + RAW * 4 * D, [P, 2, D], F32R)
        w_lo = at("w_lo", R_RING + (RAW + 2) * 4 * D, [P, 2, D], F32R)
        x = at("x", R_X, [P, KT, T])
        xs = at("xs", R_XS, [P, XT, T])
        bc = at("bc", R1, [P, 2 * GROUPS, T])
        tmp = [at(f"tmp{i}", R_TMP + i * TW, [P, T]) for i in range(7)]
        sq, hf, var, inv, nw = tmp[0:2], tmp[2:4], tmp[4], tmp[5], tmp[6]
        R_C = R1 + 2 * GROUPS * TW
        line_s = [at(f"line_s{i}", R_C + i * LSB, [P, LS]) for i in range(2)]
        cv_s = [at(f"cv_s{i}", R_C + (2 + i) * LSB, [P, LS]) for i in range(2)]
        spos = [R_C + 4 * LSB]

        def scr(name, shape):
            n = 4
            for s in shape[1:]:
                n *= s
            r = at(name, spos[0], shape)
            spos[0] += (n + 31) // 32 * 32
            return r

        dq = scr("dq", [P, T])
        sp = [at(f"sp{i}", R_C + i * TW, [HEADS, T]) for i in range(4)]
        reset = scr("reset", [HEADS, T])
        dqT = scr("dqT", [P, NC, P])
        NE = NC - 1 + DEC_B
        bde = scr("bde", [HEADS, HEADS, NE])
        dend = scr("dend", [P, HEADS, NE])
        bd = scr("bd", [HEADS, HPG, P])
        wT = scr("wT", [P, HPG, P])
        xdt = scr("xdt", [P, GW])
        xde = scr("xde", [P, GW])
        ysb = scr("ysb", [P, GW])
        state = scr("state", [P, GROUPS, GW])
        bT = scr("bT", [P, P])
        cbm = scr("cbm", [P, P])
        bTm = scr("bTm", [TS, DEC_B, P])
        cm = scr("cm", [P, DEC_B, TS + DEC_L])
        seg = at("seg", R_C, [P, HPG, P])
        prev = scr("prev", [P, DEC_B, GW])
        v_hi = at("v_hi", R1, [P, KT, T], F32R)
        v_lo = at("v_lo", R1 + KT * TW, [P, KT, T], F32R)
        line_a = at("line_a", R_TMP, [P, LA])
        cv_a = at("cv_a", R_TMP + LAB, [P, LA])
        c_sb = at("c_sb", R_TMP + 2 * LAB, [P, T])
        v_f = at("v_f", R_TMP + 2 * LAB + TW, [P, T])
        bra = [at(f"bra{i}", R_TMP + i * TW, [P, T]) for i in range(2)]
        sga = [at(f"sga{i}", R_TMP + (2 + i) * TW, [P, T]) for i in range(2)]
        ma = at("ma", R_MA, [P, KT, T])
        sgb = at("sgb", R_X, [P, KT, T])
        n_hi = at("n_hi", R_XS, [P, XT, T], F32R)
        n_lo = at("n_lo", R1, [P, XT, T], F32R)
        mt = [at(f"mt{i}", R_TMP + i * TW, [P, T]) for i in range(2)]
        q = at("q", R_XS, [P, 2 * PH, T])
        tpos = [R1]

        def tk(name, shape, dt=F32):
            n = 4
            for s in shape[1:]:
                n *= s
            r = at(name, tpos[0], shape, dt)
            tpos[0] += (n + 31) // 32 * 32
            assert tpos[0] <= R_X
            return r

        sc = tk("sc", [P, 2 * PH, NKEYS])
        sc2 = tk("sc2", [P, 2 * PH, NKEYS])
        cand = tk("cand", [P, PH, TOPK * TOPK])
        cand2 = tk("cand2", [P, PH, TOPK * TOPK])
        key_sb = tk("key_sb", [P, 2 * PH, NKEYS])
        top = tk("top", [P, 2 * PH, TOPK])
        topi = tk("topi", [P, 2 * PH, TOPK], U32)
        topf = tk("topf", [P, 2 * PH, TOPK])
        best = tk("best", [P, PH, TOPK])
        besti = tk("besti", [P, PH * TOPK], U32)
        bsel = tk("bsel", [P, 2, PH * TOPK], U32)
        bself = tk("bself", [P, 2, PH * TOPK])
        sm = tk("sm", [P, 2, PH])
        pick = tk("pick", [P, 3, PH * TOPK])
        pickT = at("pickT", R_MA, [P, 3, T])
        oh_g = at("oh_g", R_XS, [P, 2, TB, P])
        oh_2 = at("oh_2", R_XS + 4 * 2 * TB * P, [P, 2, TB, P])
        gt = at("gt", R1, [P, 2, NKEYS, TB])
        p_hi = [at("p_hi0", R_XS, [P, GI, T], F32R), at("p_hi1", R1, [P, GI, T], F32R)]
        p_lo = [at("p_lo0", R_XS + GI * TW, [P, GI, T], F32R), at("p_lo1", R1 + GI * TW, [P, GI, T], F32R)]
        gbuf = at("gbuf", R_MA, [P, 2, NB, GI // 2, TB])
        ge = [at(f"ge{i}", R_TMP + i * TW, [P, T]) for i in range(2)]
        yo = [at(f"yo{i}", R1 + i * TW, [P, T]) for i in range(2)]

        ps = ctx.enter_context(nc.psum_tensor("ps", [P, 8, 512], F32))
        acc = [ps[:, 0:2, 0:HF], ps[:, 2:4, 0:HF]]
        ssp = ps[:, 4:6, 0:HF]
        S0, S1, S2, S3 = (ps[:, 4 + i, :] for i in range(4))

        ld = [sem(f"unit_loaded{i}") for i in range(RAW)]
        s_wbeg = sem("split_begun")
        s_whi = sem("weights_hi")
        s_w = sem("weights_split")
        s_unit = sem("unit_used")
        s_accf = [sem("acc0_read"), sem("acc1_read")]
        s_x = sem("x_loaded")
        s_in = sem("small_inputs_loaded")
        s_c = sem("constants_made")
        s_pc = sem("pool_chain")
        s_dc = sem("vector_chain")
        s_ac = sem("scalar_chain")
        s_sq = sem("squares_ready")
        s_ss = sem("squares_summed")
        s_var = sem("variance_ready")
        s_std = sem("deviation_ready")
        s_hf = sem("normed_ready")
        s_hhi = sem("normed_hi")
        s_h = sem("normed_split")
        s_line = sem("conv_line_ready")
        s_cv = sem("conv_done")
        s_xbc = sem("xbc_ready")
        s_sp = sem("dt_for_exp")
        s_spe = sem("dt_exp_done")
        s_ds = sem("decays_ready")
        s_de = sem("decay_exp_done")
        s_dT = sem("decays_transposed")
        s_dTs = sem("decays_copied")
        s_bd = sem("head_rows_ready")
        s_pre = sem("chunk_products")
        s_seg = sem("segments_ready")
        s_exp = sem("segments_exp")
        s_wT = sem("mix_weights_ready")
        s_y = sem("chunk_outputs")
        s_ysb = sem("chunk_output_ready")
        s_st = sem("chunk_states")
        s_state = sem("state_updated")
        s_yT = sem("output_turned")
        s_y2 = sem("output_merged")
        s_pl = sem("sample_state_loaded")
        s_sst = sem("sample_state_product")
        s_snew = sem("sample_state_updated")
        s_po = sem("sample_state_stored")
        s_cc = sem("c_ready")
        s_vf = sem("v_ready")
        s_vhi = sem("v_hi_ready")
        s_v = sem("v_split")
        s_bra = sem("branch_a_gated_inputs")
        s_ma = sem("branch_a_merged")
        s_gb = sem("gate_b_ready")
        s_z = sem("silu_z_ready")
        s_gz = sem("gated_ready")
        s_nf = sem("group_normed_ready")
        s_nhi = sem("group_normed_hi")
        s_n = sem("group_normed_split")
        s_mf = sem("merge_ready")
        s_mhi = sem("merge_hi")
        s_m = sem("merge_split")
        s_xr = sem("x_reloaded")
        s_x1 = sem("x_after_mixer")
        s_q = sem("queries_ready")
        s_key = sem("keys_loaded")
        s_sc = sem("scores_ready")
        s_scs = sem("scores_copied")
        s_be = sem("softmax_shifted")
        s_bx = sem("softmax_exp")
        s_pk = sem("picks_ready")
        s_pkT = sem("picks_turned")
        s_pks = sem("picks_copied")
        s_oh = sem("one_hots_ready")
        s_gm = sem("gates_built")
        s_gt = sem("gates_copied")
        s_gs = [sem("gates_stored0"), sem("gates_stored1")]
        s_gl = [sem("gates_loaded0"), sem("gates_loaded1")]
        s_pm = sem("expert_gated")
        s_phi = sem("expert_hi")
        s_p = sem("expert_split")
        s_x2 = sem("x_after_experts")
        s_yo = sem("y_ready")
        s_yd = [sem("y_stored0"), sem("y_stored1")]
        s_out = sem("states_stored")

        block = ctx.enter_context(nc.Block())

        def halves(a):
            return a.rearrange("p (a t) -> p a t", a=2)

        def pieces(a, line, h):
            tail = line[:, h + TP:].rearrange("p (b r) -> p b r", b=DEC_B)
            return [(a[:, 0, :], line[:, h:h + HF]), (a[:, 1, 0:HP], line[:, h + HF:h + TP]),
                    (a[:, 1, HP:HF].rearrange("p (b r) -> p b r", b=DEC_B), tail[:, :, h:])]

        def sample_view(a):
            return a.rearrange("p (b r) -> p b r", b=DEC_B)

        def line_out(cv, h):
            return sample_view(cv[:, h + TP:])[:, :, 0:DEC_L]

        def sz(j):
            return hf[j % 2]

        def c_(name, i):
            return col[:, COLS[name] + i:COLS[name] + i + 1]

        @block.sync
        def _(sp_):
            sp_.dma_start(x[:], xT).then_inc(s_x, 16)
            sp_.dma_start(col[:], cols).then_inc(s_in, 16)
            sp_.dma_start(hd[:, 0:2], heads).then_inc(s_in, 16)
            sp_.dma_start(hista[:], hist_a).then_inc(s_in, 16)
            sp_.dma_start(hists[:], hist_s).then_inc(s_in, 16)
            for n in range(RAW):
                sp_.dma_start(raw[:, n, :], units[n]).then_inc(ld[n], 16)

            def stream(n, r):
                sp_.wait_ge(s_w, n - RAW + 1)
                sp_.dma_start(raw[:, r, :], units[bass.ds(n, 1)].rearrange("a p k -> (a p) k")).then_inc(ld[r], 16)

            with sp_.Fori(1, UNITS // RAW) as i:
                for r in range(RAW):
                    stream(i * RAW + r, r)
            for n in range(UNITS // RAW * RAW, UNITS):
                sp_.wait_ge(s_w, n - RAW + 1)
                sp_.dma_start(raw[:, n % RAW, :], units[n]).then_inc(ld[n % RAW], 16)

        @block.gpsimd
        def _(pool):
            chain = [0]

            def link(ins):
                chain[0] += 1
                ins.then_inc(s_pc, 1)
                pool.wait_ge(s_pc, chain[0])

            pool.memset(ones[:], 1.0)
            pool.memset(ident[:], 0.0)
            pool.memset(causal[:], 1.0)
            pool.memset(smask[:], 1.0)
            pool.iota(iota_i[:], [[1, P]], base=0, channel_multiplier=0)
            link(pool.memset(rowmask[:], 1.0))
            pool.affine_select(out=ident[:], in_=ident[:], compare_op=ALU.not_equal, fill=1.0, base=0,
                               pattern=[[-1, P]], channel_multiplier=1)
            pool.affine_select(out=causal[:], in_=causal[:], compare_op=ALU.is_ge, fill=0.0, base=0,
                               pattern=[[1, P]], channel_multiplier=-1)
            pool.affine_select(out=smask[:], in_=smask[:], compare_op=ALU.is_ge, fill=0.0, base=0,
                               pattern=[[DEC_L, DEC_B], [1, DEC_L]], channel_multiplier=-1)
            link(pool.affine_select(out=rowmask[:], in_=rowmask[:], compare_op=ALU.is_ge, fill=0.0, base=0,
                                    pattern=[[-DEC_L, DEC_B]], channel_multiplier=1))
            pool.affine_select(out=smask[:], in_=smask[:], compare_op=ALU.is_ge, fill=0.0, base=0,
                               pattern=[[-DEC_L, DEC_B], [0, DEC_L]], channel_multiplier=1)
            pool.tensor_copy(iota[:], iota_i[:])
            pool.affine_select(out=rowmask[:], in_=rowmask[:], compare_op=ALU.is_ge, fill=0.0,
                               base=DEC_L - 1, pattern=[[DEC_L, DEC_B]], channel_multiplier=-1)\
                .then_inc(s_c, 1)

            def split_unit(r, s, landed, used, hi_done):
                pool.wait_ge(ld[r], landed)
                if used is not None:
                    pool.wait_ge(s_unit, used)
                pool.sem_inc(s_wbeg, 1)
                pool.tensor_copy(w_hi[:, s, :], raw[:, r, :]).then_inc(s_whi, 1)
                pool.wait_ge(s_whi, hi_done)
                pool.tensor_tensor(w_lo[:, s, :], raw[:, r, :], w_hi[:, s, :].bitcast(F32), ALU.subtract)\
                    .then_inc(s_w, 1)

            for n in range(RAW):
                split_unit(n, n % 2, 16, n - 1 if n >= 2 else None, n + 1)
            with pool.Fori(1, UNITS // RAW) as i:
                for r in range(RAW):
                    split_unit(r, r % 2, i * 16 + 16, i * RAW + r - 1, i * RAW + r + 1)
            for n in range(UNITS // RAW * RAW, UNITS):
                split_unit(n % RAW, n % 2, 16 * (n // RAW + 1), n - 1, n + 1)

        @block.tensor
        def _(pe):
            mm = pe.matmul

            def unit(n, L, mov_hi, mov_lo, k0=0, start=True, stop=True, slot=None, par=None):
                s = n % 2 if slot is None else slot
                a = acc[L % 2 if par is None else par]
                for k in range(KT):
                    wh, wl = (w[:, s, k * P:(k + 1) * P] for w in (w_hi, w_lo))
                    for i, (w, m) in enumerate(((wh, mov_hi), (wh, mov_lo), (wl, mov_hi))):
                        for h in range(2):
                            last = mm(a[:, h, :], w, m[:, k0 + k, h * HF:(h + 1) * HF],
                                      start=start and k == 0 and i == 0, stop=stop and k == KT - 1 and i == 2)
                last.then_inc(s_unit, 1)

            def tile(n, L, mov_hi, mov_lo, units_=1):
                if L >= 2:
                    pe.wait_ge(s_accf[L % 2], L // 2)
                for u in range(units_):
                    pe.wait_ge(s_w, n + u + 1)
                    unit(n + u, L, mov_hi, mov_lo, u * KT, u == 0, u == units_ - 1)

            def square_sums(r):
                for k in range(KT):
                    pe.wait_ge(s_sq, KT * r + k + 1)
                    for h in range(2):
                        last = mm(ssp[:, h, :], ones[:], sq[k % 2][:, h * HF:(h + 1) * HF],
                                  start=k == 0, stop=k == KT - 1)
                    last.then_inc(s_ss, 1)

            pe.wait_ge(s_c, 1)
            square_sums(0)
            pe.wait_ge(s_h, KT)
            for n in range(U_DT, U_A):
                tile(n, n, h_hi, h_lo)

            pe.wait_ge(s_ds, 1)
            for c, (t0, n) in enumerate(CHUNKS):
                if c:
                    pe.wait_ge(s_dTs, c)
                pe.transpose(S0[0:n, 0:P], dq[:, t0:t0 + n], ident[:]).then_inc(s_dT, 1)
            pe.wait_ge(s_dTs, NC)
            mm(S0[:, 0:HEADS * NE], ones[0:HEADS, :], bde[:].rearrange("p h e -> p (h e)"),
               start=True, stop=True).then_inc(s_dT, 1)
            pe.wait_ge(s_xbc, CT)
            for c, (t0, n) in enumerate(CHUNKS):
                sample = c == NC - 1
                for g in range(GROUPS):
                    s = c * GROUPS + g
                    ch = slice(t0, t0 + n)
                    Bg, Cg = bc[:, g, ch], bc[:, GROUPS + g, ch]
                    pe.wait_ge(s_bd, s + 1)
                    if s:
                        pe.wait_ge(s_y2, s)
                        pe.wait_ge(s_state, s)
                    else:
                        pe.wait_ge(s_dTs, NC + 1)
                    for hh in range(2):
                        mm((S1, S2)[hh][0:n, 0:4 * n].rearrange("p (h q) -> p h q", h=4), ones[0:HEADS, 0:n],
                           bd[:, 4 * hh:4 * hh + 4, 0:n], start=True, stop=True)
                    mm(S0[0:n, 0:n], Bg, Cg, start=True, stop=True)
                    pe.transpose(S0[0:n, P:2 * P], Bg, ident[:])
                    for j in range(4):
                        last = pe.transpose(S3[0:n, j * P:(j + 1) * P], xs[:, 4 * g + j, ch], ident[:])
                    last.then_inc(s_pre, 1)
                    pe.wait_ge(s_wT, s + 1)
                    for h in range(HPG):
                        last = mm(S1[0:n, h * HEADDIM:(h + 1) * HEADDIM], wT[0:n, h, 0:n],
                                  xdt[0:n, h * HEADDIM:(h + 1) * HEADDIM], start=True, stop=True)
                    if sample:
                        pe.wait_ge(s_pl, 16 * (g + 1))
                        cmf = cm[:].rearrange("p b r -> p (b r)")
                        for b in range(DEC_B):
                            last = mm(S2[0:n, :], cmf[:, b * TS:(b + 1) * TS], prev[:, b, :],
                                      start=b == 0, stop=b == DEC_B - 1)
                    elif c:
                        last = mm(S2[0:n, :], Cg, state[:, g, :], start=True, stop=True)
                    last.then_inc(s_y, 1)
                    if sample:
                        pe.wait_ge(s_ysb, s + 1)
                        for b in range(DEC_B):
                            k = g * DEC_B + b
                            if b >= 2:
                                pe.wait_ge(s_snew, k - 1)
                            mm((S3, S1)[b % 2], bTm[:, b, :], xde[0:n, :], start=True, stop=True)\
                                .then_inc(s_sst, 1)
                    else:
                        mm(S3, bT[0:n, :], xde[0:n, :], start=True, stop=True).then_inc(s_st, 1)
                        pe.wait_ge(s_ysb, s + 1)
                    for j in range(4):
                        last = pe.transpose(S0[:, j * n:(j + 1) * n], ysb[0:n, j * P:(j + 1) * P],
                                            ident[0:n, 0:n])
                    last.then_inc(s_yT, 1)

            for n in range(U_A, U_AO):
                tile(n, n, h_hi, h_lo)
            for i in range(KT):
                n = U_AO + 2 * i
                if i == 0:
                    pe.wait_ge(s_v, KT)
                tile(n, n, v_hi, v_lo)
                tile(n + 1, n + 1, h_hi, h_lo)
            for n in range(U_GB, U_Z):
                tile(n, n, h_hi, h_lo)
            for j in range(XT + 1):
                if j < XT:
                    tile(U_Z + j, U_Z + j, h_hi, h_lo)
                if j:
                    i = j - 1
                    pe.wait_ge(s_sq, KT + i + 1)
                    if i % 4 == 0 and i:
                        pe.wait_ge(s_var, 1 + i // 4)
                    for h in range(2):
                        last = mm(ssp[:, h, :], ones[:], sq[i % 2][:, h * HF:(h + 1) * HF],
                                  start=i % 4 == 0, stop=i % 4 == 3)
                    last.then_inc(s_ss, 1)
            pe.wait_ge(s_n, XT)
            for j in range(KT):
                tile(U_SO + 2 * j, U_SO + j, n_hi, n_lo, 2)
            pe.wait_ge(s_m, KT)
            for j in range(KT):
                tile(U_WO + j, L_WO + j, m_hi, m_lo)
            for k in range(KT):
                pe.wait_ge(s_sq, KT + XT + k + 1)
                for h in range(2):
                    last = mm(ssp[:, h, :], ones[:], sq[k % 2][:, h * HF:(h + 1) * HF],
                              start=k == 0, stop=k == KT - 1)
                last.then_inc(s_ss, 1)
            pe.wait_ge(s_h, 2 * KT)
            for j in range(N_WQ):
                tile(U_WQ + j, U_WQ - L_SHIFT + j, g_hi, g_lo)
            pe.wait_ge(s_q, N_WQ)
            pe.wait_ge(s_key, 16)
            for tt, (t0, n) in enumerate(TT):
                if tt:
                    pe.wait_ge(s_pks, tt)
                for i in range(2 * PH):
                    last = mm(ps[0:n, 4 + i // 4, i % 4 * P:(i % 4 + 1) * P], q[:, i, t0:t0 + n],
                              key_sb[:, i, :], start=True, stop=True)
                last.then_inc(s_sc, 1)
                pe.wait_ge(s_pk, tt + 1)
                for i in range(3):
                    last = pe.transpose(S0[:, i * P:i * P + n], pick[0:n, i, :], ident[0:n, 0:n])
                last.then_inc(s_pkT, 1)

            def gates(b, par, first):
                pe.wait_ge(s_oh, b + 1)
                if not first:
                    pe.wait_ge(s_gt, b - 1)
                for j in range(TB):
                    last = mm(ps[:, 4 * par + j // 4, j % 4 * P:(j % 4 + 1) * P], oh_g[:, par, j, :],
                              oh_2[:, par, j, :], start=True, stop=True)
                last.then_inc(s_gm, 1)

            pe.wait_ge(s_pks, len(TT))
            for b in range(2):
                gates(b, b, True)
            with pe.Fori(1, NB // 2) as i:
                for par in range(2):
                    gates(i * 2 + par, par, False)
            for b in range(NB // 2 * 2, NB):
                gates(b, b % 2, False)

            L0 = U_PEER - L_SHIFT

            def units8(m0, half, mov, p_done=None):
                with pe.Fori(0, 4) as j:
                    for b in range(2):
                        m = m0 + b
                        par = (L0 + b) % 2
                        if p_done is not None and b == 0:
                            pe.wait_ge(s_p, p_done)
                        pe.wait_ge(s_w, U_PEER + m + j * 2 + 1)
                        pe.wait_ge(s_accf[par], (L0 + b) // 2 + half + j)
                        unit(None, None, mov[0], mov[1], slot=(U_PEER + b) % 2, par=par)

            def experts_s(m0, half):
                units8(m0, half, (g_hi, g_lo))

            def experts_v(m0, half, par, p_done):
                units8(m0, half, (p_hi[par], p_lo[par]), p_done)

            pe.wait_ge(s_gt, NB)
            experts_s(0, 0)
            with pe.Fori(0, NG // 2 - 1) as i:
                experts_s(i * 32 + 8, i * 16 + 4)
                experts_v(i * 32 + 16, i * 16 + 8, 0, i * 16 + 8)
                experts_s(i * 32 + 24, i * 16 + 12)
                experts_v(i * 32 + 32, i * 16 + 16, 1, i * 16 + 16)
            e0 = 32 * (NG // 2 - 1)
            experts_s(e0 + 8, e0 // 2 + 4)
            experts_v(e0 + 16, e0 // 2 + 8, 0, e0 // 2 + 8)
            experts_v(e0 + 24, e0 // 2 + 12, 1, e0 // 2 + 16)

            for k in range(KT):
                pe.wait_ge(s_sq, 2 * KT + XT + k + 1)
                for h in range(2):
                    last = mm(ssp[:, h, :], ones[:], sq[k % 2][:, h * HF:(h + 1) * HF],
                              start=k == 0, stop=k == KT - 1)
                last.then_inc(s_ss, 1)

        @block.scalar
        def _(act):
            chain = [0]

            def link(ins):
                chain[0] += 1
                ins.then_inc(s_ac, 1)
                act.wait_ge(s_ac, chain[0])

            def squares(q0):
                for k in range(KT):
                    if k >= 2:
                        act.wait_ge(s_ss, q0 + k - 1)
                    act.activation(sq[k % 2][:], x[:, k, :], ACT.Square).then_inc(s_sq, 1)

            def hi_parts(r, out):
                for k in range(KT):
                    act.wait_ge(s_hf, r * KT + k + 1)
                    act.activation(out[:, k, :], hf[k % 2][:], ACT.Copy).then_inc(s_hhi, 1)

            act.wait_ge(s_x, 16)
            squares(0)
            act.wait_ge(s_var, 1)
            act.activation(inv[:], var[:], ACT.Sqrt).then_inc(s_std, 1)
            hi_parts(0, h_hi)
            act.wait_ge(s_in, 64)

            act.wait_ge(s_unit, 1)
            act.activation(halves(sp[0][:]), acc[0][0:HEADS], ACT.Identity, bias=hd[:, 0:1])
            act.activation(halves(sp[1][:]), acc[0][0:HEADS], ACT.Abs, bias=hd[:, 0:1]).then_inc(s_accf[0], 1)
            act.wait_ge(s_accf[0], 1)
            act.activation(sp[2][:], sp[1][:], ACT.Exp, scale=-1.0).then_inc(s_spe, 1)
            act.activation(hd[:, 2:3], hd[:, 1:2], ACT.Exp).then_inc(s_spe, 1)
            act.wait_ge(s_sp, 1)
            act.activation(dq[64:96, :], dq[0:32, :], ACT.Exp).then_inc(s_de, 1)
            act.activation(sp[3][:], sp[2][:], ACT.Exp).then_inc(s_de, 1)

            for j in range(CT + 1):
                if j < CT:
                    n = U_XBC + j
                    line = line_s[j % 2]
                    if j >= 2:
                        act.wait_ge(s_cv, j - 1)
                    else:
                        act.wait_ge(s_sp, 2)
                    act.activation(sample_view(line[:, HS + TP:])[:, :, 0:HS], hists[:, j], ACT.Copy)
                    act.wait_ge(s_unit, n + 1)
                    ps_ = pieces(acc[n % 2], line, HS)
                    act.activation(ps_[0][1], ps_[0][0], ACT.Copy)
                    act.activation(ps_[1][1], ps_[1][0], ACT.Copy)
                    act.activation(ps_[2][1], ps_[2][0], ACT.Copy).then_inc(s_accf[n % 2], 1)
                if j:
                    i = j - 1
                    act.wait_ge(s_cv, i + 1)
                    cv = cv_s[i % 2]
                    dst = xs[:, i, :] if i < XT else bc[:, i - XT, :]
                    act.activation(dst[:, 0:TP], cv[:, 0:TP], ACT.Silu, bias=c_("cb", i))
                    act.activation(sample_view(dst[:, TP:]), line_out(cv, HS), ACT.Silu, bias=c_("cb", i))\
                        .then_inc(s_xbc, 1)

            for c, (t0, n) in enumerate(CHUNKS):
                act.wait_ge(s_dT, c + 1)
                act.activation(dqT[0:n, c, :], S0[0:n, 0:P], ACT.Copy).then_inc(s_dTs, 1)
            act.wait_ge(s_dT, NC + 1)
            act.activation(dend[:].rearrange("p h e -> p (h e)"), S0[:, 0:HEADS * NE], ACT.Copy)\
                .then_inc(s_dTs, 1)

            for c, (t0, n) in enumerate(CHUNKS):
                sample = c == NC - 1
                for g in range(GROUPS):
                    s = c * GROUPS + g
                    if sample:
                        if g:
                            act.wait_ge(s_snew, DEC_B * g)
                            act.dma_start(ssm_s[:, g - 1], prev[:]).then_inc(s_po, 16)
                            act.wait_ge(s_po, 16 * g)
                        act.dma_start(prev[:], ssm_in[:, g]).then_inc(s_pl, 16)
                    act.wait_ge(s_seg, s + 1)
                    link(act.activation(seg[0:n, :, 0:n], seg[0:n, :, 0:n], ACT.Relu, scale=-1.0))
                    act.activation(seg[0:n, :, 0:n], seg[0:n, :, 0:n], ACT.Exp, scale=-1.0).then_inc(s_exp, 1)
                if c == NC - 2:
                    act.wait_ge(s_state, (NC - 1) * GROUPS)
                    act.dma_start(ssm_p, state[:]).then_inc(s_out, 16)
            act.wait_ge(s_snew, DEC_B * GROUPS)
            act.dma_start(ssm_s[:, GROUPS - 1], prev[:]).then_inc(s_po, 16)
            act.dma_start(new_s, news[:]).then_inc(s_out, 16)

            for i in range(KT):
                n = U_A + 3 * i
                act.wait_ge(s_unit, n + 1)
                if i == 0:
                    act.wait_ge(s_y2, NC * GROUPS)
                    act.wait_ge(s_po, 16 * GROUPS)
                    act.wait_ge(s_out, 32)
                else:
                    act.wait_ge(s_v, i)
                act.activation(halves(c_sb[:]), acc[n % 2], ACT.Copy).then_inc(s_accf[n % 2], 1)
                act.wait_ge(s_vf, i + 1)
                act.activation(v_hi[:, i, :], v_f[:], ACT.Copy).then_inc(s_vhi, 1)
            act.wait_ge(s_v, KT)
            act.dma_start(new_a, newa[:]).then_inc(s_out, 16)
            for i in range(KT):
                n = U_AO + 2 * i
                if i >= 2:
                    act.wait_ge(s_ma, i - 1)
                act.wait_ge(s_unit, n + 1)
                act.activation(halves(bra[i % 2][:]), acc[n % 2], ACT.Copy).then_inc(s_accf[n % 2], 1)
                act.wait_ge(s_unit, n + 2)
                act.activation(halves(sga[i % 2][:]), acc[(n + 1) % 2], ACT.Sigmoid)\
                    .then_inc(s_accf[(n + 1) % 2], 1)
            for i in range(KT):
                n = U_GB + i
                act.wait_ge(s_unit, n + 1)
                act.activation(halves(sgb[:, i, :]), acc[n % 2], ACT.Sigmoid).then_inc(s_accf[n % 2], 1)
            act.wait_ge(s_ma, KT)

            def z_silu(j):
                n = U_Z + j
                if j % 4 == 0 and j:
                    act.wait_ge(s_n, j)
                act.wait_ge(s_unit, n + 1)
                act.activation(halves(sz(j)[:]), acc[n % 2], ACT.Silu).then_inc(s_accf[n % 2], 1)

            def z_square(j):
                act.wait_ge(s_gz, j + 1)
                if j >= 2:
                    act.wait_ge(s_ss, KT + j - 1)
                act.activation(sq[j % 2][:], xs[:, j, :], ACT.Square).then_inc(s_sq, 1)

            for g in range(GROUPS):
                for j in range(4 * g, 4 * g + 4):
                    z_silu(j)
                    z_square(j)
                act.wait_ge(s_var, 2 + g)
                act.activation(inv[:], var[:], ACT.Sqrt).then_inc(s_std, 1)
                for j in range(4 * g, 4 * g + 4):
                    act.wait_ge(s_nf, j + 1)
                    act.activation(n_hi[:, j, :], hf[j % 2][:], ACT.Copy).then_inc(s_nhi, 1)
            for j in range(KT):
                act.wait_ge(s_mf, j + 1)
                act.activation(m_hi[:, j, :], ma[:, j, :], ACT.Copy).then_inc(s_mhi, 1)
            act.dma_start(x[:], xT).then_inc(s_xr, 16)
            act.wait_ge(s_x1, KT)
            squares(KT + XT)
            act.wait_ge(s_var, 2 + GROUPS)
            act.activation(inv[:], var[:], ACT.Sqrt).then_inc(s_std, 1)
            hi_parts(1, g_hi)
            act.wait_ge(s_h, 2 * KT)
            act.dma_start(key_sb[:], keys).then_inc(s_key, 16)
            for j in range(N_WQ):
                n, L = U_WQ + j, U_WQ - L_SHIFT + j
                act.wait_ge(s_unit, n + 1)
                link(act.activation(halves(q[:, j, :]), acc[L % 2], ACT.Copy))
                act.sem_inc(s_accf[L % 2], 1)
                act.sem_inc(s_q, 1)
            for tt, (t0, n) in enumerate(TT):
                act.wait_ge(s_sc, tt + 1)
                act.activation(sc[0:n].rearrange("p (a b) k -> p a (b k)", a=4), ps[0:n, 4:8, :], ACT.Copy)\
                    .then_inc(s_scs, 1)
                act.wait_ge(s_be, tt + 1)
                act.activation(best[0:n], best[0:n], ACT.Exp).then_inc(s_bx, 1)
                act.wait_ge(s_pkT, tt + 1)
                act.activation(pickT[:, :, t0:t0 + n],
                               S0[:, 0:3 * P].rearrange("p (a t) -> p a t", a=3)[:, :, 0:n], ACT.Copy)\
                    .then_inc(s_pks, 1)

            def gates_out(b, par, stored):
                act.wait_ge(s_gm, b + 1)
                if stored is not None:
                    act.wait_ge(s_gs[par], stored)
                act.activation(gt[:, par].rearrange("p i t -> p t i"),
                               ps[:, 4 * par:4 * par + 4, :].rearrange("p a (t i) -> p (a t) i", i=P),
                               ACT.Copy).then_inc(s_gt, 1)
                act.wait_ge(s_gt, b + 1)
                act.dma_start(gate_dram[:, :, bass.ds(b, 1)].rearrange("g p a i t -> p g (a i t)"),
                              gt[:, par].rearrange("p (g i) t -> p g (i t)", g=NG))\
                    .then_inc(s_gs[par], 16)

            for b in range(2):
                gates_out(b, b, None)
            with act.Fori(1, NB // 2) as i:
                for par in range(2):
                    gates_out(i * 2 + par, par, i * 16)
            for b in range(NB // 2 * 2, NB):
                gates_out(b, b % 2, 16 * (b // 2))
            act.wait_ge(s_gs[0], 16 * ((NB + 1) // 2))
            act.wait_ge(s_gs[1], 16 * (NB // 2))

            L0 = U_PEER - L_SHIFT

            def gate_load(g, hb):
                src = gate_dram[bass.ds(g, 1), :, :, hb * 4:hb * 4 + 4, :]
                act.dma_start(gbuf[:, hb].rearrange("p b i t -> p b (i t)"),
                              src.rearrange("a p b i t -> (a p) b (i t)")).then_inc(s_gl[hb], 16)

            def act_group(g, par, m0, first=False, load=True):
                for u in range(0, GI, 2):
                    for b in range(2):
                        if not (first and u == 0):
                            act.wait_ge(s_p, g * GI + u + b - 1)
                        act.wait_ge(s_unit, U_PEER + m0 + u + b + 1)
                        act.activation(halves(ge[b][:]), acc[(L0 + b) % 2], ACT.Gelu)\
                            .then_inc(s_accf[(L0 + b) % 2], 1)
                    for b in range(2):
                        act.wait_ge(s_pm, g * GI + u + b + 1)
                        act.activation(p_hi[par][:, u + b, :], ge[b][:], ACT.Copy).then_inc(s_phi, 1)
                    if load and u % 4 == 2:
                        gate_load(g + 1, u // 4)

            for hb in range(2):
                gate_load(0, hb)
            act_group(0, 0, 0, first=True)
            with act.Fori(0, NG // 2 - 1) as i:
                act_group(i * 2 + 1, 1, i * 32 + 8)
                act_group(i * 2 + 2, 0, i * 32 + 24)
            act_group(NG - 1, 1, 32 * (NG // 2 - 1) + 8, load=False)

            act.wait_ge(s_x2, GI * NG)
            squares(2 * KT + XT)
            act.wait_ge(s_var, 3 + GROUPS)
            act.activation(inv[:], var[:], ACT.Sqrt).then_inc(s_std, 1)
            for k in range(KT):
                act.wait_ge(s_yo, k + 1)
                act.dma_start(yT[:, k], yo[k % 2][:]).then_inc(s_yd[k % 2], 16)
            act.wait_ge(s_out, 48)
            for i in range(2):
                act.wait_ge(s_yd[i], 16 * KT // 2)

        @block.vector
        def _(dve):
            chain = [0]

            def link(ins):
                chain[0] += 1
                ins.then_inc(s_dc, 1)
                dve.wait_ge(s_dc, chain[0])

            tt_, ts_, stt = dve.tensor_tensor, dve.tensor_scalar, dve.scalar_tensor_tensor

            def rsqrt(scale, ss_done, std_done):
                dve.wait_ge(s_ss, ss_done)
                ts_(halves(var[:]), ssp, scale, EPS, ALU.mult, ALU.add).then_inc(s_var, 1)
                dve.wait_ge(s_std, std_done)
                link(dve.reciprocal(inv[:], inv[:]))
                link(tt_(nw[:], inv[:], inv[:], ALU.mult))
                link(tt_(nw[:], nw[:], var[:], ALU.mult))
                link(ts_(nw[:], nw[:], -0.5, 1.5, ALU.mult, ALU.add))
                link(tt_(inv[:], inv[:], nw[:], ALU.mult))

            def normed(r, w, out_lo, out_hi):
                for k in range(KT + 1):
                    if k < KT:
                        if k >= 2:
                            dve.wait_ge(s_h, r * KT + k - 1)
                        stt(hf[k % 2][:], x[:, k, :], c_(w, k), inv[:], ALU.mult, ALU.mult).then_inc(s_hf, 1)
                    if k:
                        i = k - 1
                        dve.wait_ge(s_hhi, r * KT + i + 1)
                        dve.wait_ge(s_hf, r * KT + i + 1)
                        tt_(out_lo[:, i, :], hf[i % 2][:], out_hi[:, i, :].bitcast(F32), ALU.subtract)\
                            .then_inc(s_h, 1)

            dve.wait_ge(s_in, 64)
            rsqrt(1.0 / D, KT, 1)
            normed(0, "mix", h_lo, h_hi)

            dve.memset(reset[:], 1.0)
            dve.wait_ge(s_spe, 2)
            link(ts_(sp[1][:], sp[2][:], 2.0, None, ALU.add))
            link(dve.reciprocal(sp[1][:], sp[1][:]))
            link(tt_(sp[1][:], sp[1][:], sp[2][:], ALU.mult))
            link(tt_(sp[2][:], sp[1][:], sp[1][:], ALU.mult))
            link(ts_(sp[3][:], sp[2][:], 2.0 / 17, 2.0 / 15, ALU.mult, ALU.add))
            for k in (13, 11, 9, 7, 5, 3, 1):
                link(tt_(sp[3][:], sp[3][:], sp[2][:], ALU.mult))
                link(ts_(sp[3][:], sp[3][:], 2.0 / k, None, ALU.add))
            link(tt_(sp[3][:], sp[3][:], sp[1][:], ALU.mult))
            dve.memset(reset[:, 0:1], 0.0)
            dve.memset(reset[:, N_META:TP:P], 0.0)
            dve.memset(reset[:, TP:T:DEC_L], 0.0)
            link(stt(dq[32:64, :], sp[0][:], 0.0, sp[3][:], ALU.max, ALU.add))
            link(ts_(sp[1][:], dq[32:64, :], hd[:, 2:3], -1.0, ALU.mult, ALU.mult))
            link(dve.tensor_tensor_scan(dq[0:32, :], reset[:], sp[1][:], 0.0, ALU.mult, ALU.add))
            for c, (t0, n) in enumerate(CHUNKS[:-1]):
                last_c = dq[0:32, t0 + n - 1:t0 + n]
                ts_(sp[2][:, t0:t0 + n], dq[0:32, t0:t0 + n], last_c, -1.0, ALU.subtract, ALU.mult)
            cs = sample_view(dq[0:32, TP:T])
            tt_(sample_view(sp[2][:, TP:T]), cs[:, :, DEC_L - 1:DEC_L].to_broadcast([HEADS, DEC_B, DEC_L]), cs,
                ALU.subtract).then_inc(s_sp, 1)
            dve.wait_ge(s_de, 2)
            link(dve.tensor_copy(sp[1][:], dq[32:64, :]))
            tt_(dq[96:128, :], sp[3][:], sp[1][:], ALU.mult)
            ends = [(N_META - 1, 1, 1), (N_META + P - 1, NC - 2, P), (TP + DEC_L - 1, DEC_B, DEC_L)]
            link(dve.tensor_copy(sp[0][:, 0:1], dq[64:96, N_META - 1:N_META]))
            dve.tensor_copy(sp[0][:, 1:NC - 1], dq[64:96, N_META + P - 1:TP:P])
            link(dve.tensor_copy(sp[0][:, NC - 1:NE], dq[64:96, TP + DEC_L - 1:T:DEC_L]))
            link(tt_(bde[:], ident[0:HEADS, 0:HEADS].unsqueeze(2).to_broadcast([HEADS, HEADS, NE]),
                     sp[0][:, 0:NE].unsqueeze(1).to_broadcast([HEADS, HEADS, NE]), ALU.mult))
            dve.memset(line_s[0][:, 0:HS], 0.0)
            dve.memset(line_s[1][:, 0:HS], 0.0)
            link(dve.memset(cm[:], 0.0))
            dve.sem_inc(s_ds, 1)
            dve.sem_inc(s_sp, 1)

            for j in range(CT):
                line, cv = line_s[j % 2], cv_s[j % 2]
                W = LS - HS
                dve.wait_ge(s_accf[(U_XBC + j) % 2], (U_XBC + j) // 2 + 1)
                if j >= 2:
                    dve.wait_ge(s_xbc, j - 1)
                link(ts_(cv[:, 0:W], line[:, 0:W], c_("cs", 4 * j), None, ALU.mult))
                link(stt(cv[:, 0:W], line[:, 1:W + 1], c_("cs", 4 * j + 1), cv[:, 0:W], ALU.mult, ALU.add))
                link(stt(cv[:, 0:W], line[:, 2:W + 2], c_("cs", 4 * j + 2), cv[:, 0:W], ALU.mult, ALU.add))
                dve.tensor_copy(news[:, j, 0, :], line[:, TP:HS + TP])
                dve.tensor_copy(news[:, j, 1:, :], sample_view(line[:, HS + TP:])[:, :, DEC_L:])
                stt(cv[:, 0:W], line[:, 3:W + 3], c_("cs", 4 * j + 3), cv[:, 0:W], ALU.mult, ALU.add).then_inc(s_cv, 1)

            dve.wait_ge(s_dTs, NC + 1)
            dve.wait_ge(s_xbc, CT)
            for c, (t0, n) in enumerate(CHUNKS):
                sample = c == NC - 1
                mask = smask[:].rearrange("p b r -> p (b r)") if sample else causal[0:n, 0:n]
                for g in range(GROUPS):
                    s = c * GROUPS + g
                    hs = slice(g * HPG, (g + 1) * HPG)

                    def per_head(i, w):
                        return dqT[0:n, c, i * 32 + g * HPG:i * 32 + (g + 1) * HPG].unsqueeze(2)\
                            .to_broadcast([n, HPG, w])

                    tt_(bd[:, :, 0:n], ident[0:HEADS, hs].unsqueeze(2).to_broadcast([HEADS, HPG, n]),
                        dq[0:HEADS, t0:t0 + n].unsqueeze(1).to_broadcast([HEADS, HPG, n]), ALU.mult)\
                        .then_inc(s_bd, 1)
                    if sample:
                        dve.tensor_copy(cm[:, :, 0:DEC_L], sample_view(bc[:, GROUPS + g, TP:T]))
                    dve.wait_ge(s_pre, s + 1)
                    cq = ps[0:n, 5:7, 0:4 * n].rearrange("p a (h q) -> p a h q", h=4)
                    ck = dqT[0:n, c, g * HPG:(g + 1) * HPG].rearrange("p (a h) -> p a h", a=2)\
                        .unsqueeze(3).to_broadcast([n, 2, 4, n])
                    tt_(seg[0:n, :, 0:n].rearrange("p (a h) q -> p a h q", a=2), cq, ck, ALU.subtract)\
                        .then_inc(s_seg, 1)
                    tt_(cbm[0:n, 0:n], S0[0:n, 0:n], mask, ALU.mult)
                    xg = S3[0:n, :].rearrange("p (h w) -> p h w", h=HPG)
                    tt_(xdt[0:n, :].rearrange("p (h w) -> p h w", h=HPG), xg, per_head(1, HEADDIM), ALU.mult)
                    if sample:
                        tt_(bTm[:], S0[0:n, P:2 * P].unsqueeze(1).to_broadcast([n, DEC_B, P]),
                            rowmask[:].unsqueeze(2).to_broadcast([n, DEC_B, P]), ALU.mult)
                    else:
                        dve.tensor_copy(bT[0:n, :], S0[0:n, P:2 * P])
                    link(tt_(xde[0:n, :].rearrange("p (h w) -> p h w", h=HPG), xg, per_head(3, HEADDIM), ALU.mult))
                    dve.wait_ge(s_exp, s + 1)
                    tt_(wT[0:n, :, 0:n], seg[0:n, :, 0:n],
                        cbm[0:n, 0:n].unsqueeze(1).to_broadcast([n, HPG, n]), ALU.mult).then_inc(s_wT, 1)
                    dve.wait_ge(s_y, s + 1)
                    if c:
                        link(tt_(ysb[0:n, :].rearrange("p (h w) -> p h w", h=HPG),
                                 S2[0:n, :].rearrange("p (h w) -> p h w", h=HPG), per_head(2, HEADDIM), ALU.mult))
                        tt_(ysb[0:n, :], ysb[0:n, :], S1[0:n, :], ALU.add).then_inc(s_ysb, 1)
                    else:
                        dve.tensor_copy(ysb[0:n, :], S1[0:n, :]).then_inc(s_ysb, 1)

                    def decay(e):
                        return dend[:, hs, e:e + 1].to_broadcast([P, HPG, HEADDIM])

                    if sample:
                        for b in range(DEC_B):
                            pb = prev[:, b, :]
                            pv = pb.rearrange("p (h w) -> p h w", h=HPG)
                            link(tt_(pv, pv, decay(NC - 1 + b), ALU.mult))
                            dve.wait_ge(s_sst, g * DEC_B + b + 1)
                            tt_(pb, pb, (S3, S1)[b % 2], ALU.add).then_inc(s_snew, 1)
                        dve.wait_ge(s_snew, DEC_B * (g + 1))
                        dve.sem_inc(s_state, 1)
                    else:
                        st = state[:, g, :]
                        if c:
                            sv = st.rearrange("p (h w) -> p h w", h=HPG)
                            link(tt_(sv, sv, decay(c), ALU.mult))
                            dve.wait_ge(s_st, s + 1)
                            tt_(st, st, S3, ALU.add).then_inc(s_state, 1)
                        else:
                            dve.wait_ge(s_st, s + 1)
                            dve.tensor_copy(st, S3).then_inc(s_state, 1)
                    dve.wait_ge(s_yT, s + 1)
                    for j in range(4):
                        xj = xs[:, 4 * g + j, t0:t0 + n]
                        last = stt(xj, xj, c_("dd", 4 * g + j), S0[:, j * n:(j + 1) * n], ALU.mult, ALU.add)
                    last.then_inc(s_y2, 1)

            dve.wait_ge(s_y2, NC * GROUPS)
            dve.memset(line_a[:, 0:HA], 0.0)
            for i in range(KT):
                n = U_A + 3 * i
                W = LA - HA
                dve.tensor_copy(sample_view(line_a[:, HA + TP:])[:, :, 0:HA], hista[:, i])
                dve.wait_ge(s_accf[n % 2], n // 2 + 1)
                dve.wait_ge(s_unit, n + 2)
                px = pieces(acc[(n + 1) % 2], line_a, HA)
                cpc = [c_sb[:, 0:HF], c_sb[:, HF:TP], sample_view(c_sb[:, TP:T])]
                tt_(px[0][1], px[0][0], cpc[0], ALU.mult)
                tt_(px[1][1], px[1][0], cpc[1], ALU.mult)
                tt_(px[2][1], px[2][0], cpc[2], ALU.mult).then_inc(s_accf[(n + 1) % 2], 1)
                dve.wait_ge(s_accf[(n + 1) % 2], (n + 1) // 2 + 1)
                link(ts_(cv_a[:, 0:W], line_a[:, 0:W], c_("ca", 3 * i), None, ALU.mult))
                link(stt(cv_a[:, 0:W], line_a[:, 1:W + 1], c_("ca", 3 * i + 1), cv_a[:, 0:W], ALU.mult, ALU.add))
                link(stt(cv_a[:, 0:W], line_a[:, 2:W + 2], c_("ca", 3 * i + 2), cv_a[:, 0:W], ALU.mult, ALU.add))
                dve.tensor_copy(newa[:, i, 0, :], line_a[:, TP:HA + TP])
                dve.tensor_copy(newa[:, i, 1:, :], sample_view(line_a[:, HA + TP:])[:, :, DEC_L:])
                dve.wait_ge(s_unit, n + 3)
                a = acc[(n + 2) % 2]
                vs = [v_f[:, 0:HF], v_f[:, HF:TP], sample_view(v_f[:, TP:T])]
                co = [cv_a[:, 0:HF], cv_a[:, HF:TP], line_out(cv_a, HA)]
                ao = [a[:, 0, :], a[:, 1, 0:HP], sample_view(a[:, 1, HP:HF])]
                tt_(vs[0], ao[0], co[0], ALU.mult)
                tt_(vs[1], ao[1], co[1], ALU.mult)
                link(tt_(vs[2], ao[2], co[2], ALU.mult))
                dve.sem_inc(s_accf[(n + 2) % 2], 1)
                dve.sem_inc(s_vf, 1)
                dve.wait_ge(s_vhi, i + 1)
                tt_(v_lo[:, i, :], v_f[:], v_hi[:, i, :].bitcast(F32), ALU.subtract).then_inc(s_v, 1)
            for i in range(KT):
                n = U_AO + 2 * i
                dve.wait_ge(s_accf[(n + 1) % 2], (n + 1) // 2 + 1)
                dve.wait_ge(s_accf[n % 2], n // 2 + 1)
                tt_(ma[:, i, :], bra[i % 2][:], sga[i % 2][:], ALU.mult).then_inc(s_ma, 1)

            for g in range(GROUPS):
                for j in range(4 * g, 4 * g + 4):
                    n = U_Z + j
                    dve.wait_ge(s_accf[n % 2], n // 2 + 1)
                    tt_(xs[:, j, :], xs[:, j, :], sz(j)[:], ALU.mult).then_inc(s_gz, 1)
                rsqrt(1.0 / GW, KT + 4 * g + 4, 2 + g)
                for j in range(4 * g, 4 * g + 4):
                    if j > 4 * g + 1:
                        dve.wait_ge(s_n, j - 1)
                    stt(hf[j % 2][:], xs[:, j, :], c_("sn", j), inv[:], ALU.mult, ALU.mult).then_inc(s_nf, 1)
                    dve.wait_ge(s_nhi, j + 1)
                    tt_(n_lo[:, j, :], hf[j % 2][:], n_hi[:, j, :].bitcast(F32), ALU.subtract).then_inc(s_n, 1)

            for j in range(KT):
                L = U_SO + j
                dve.wait_ge(s_unit, U_SO + 2 * j + 2)
                link(tt_(halves(mt[j % 2][:]), acc[L % 2], halves(sgb[:, j, :]), ALU.mult))
                dve.sem_inc(s_accf[L % 2], 1)
                tt_(ma[:, j, :], ma[:, j, :], mt[j % 2][:], ALU.add).then_inc(s_mf, 1)
                dve.wait_ge(s_mhi, j + 1)
                tt_(m_lo[:, j, :], ma[:, j, :], m_hi[:, j, :].bitcast(F32), ALU.subtract).then_inc(s_m, 1)
            dve.wait_ge(s_xr, 16)
            for j in range(KT):
                L = L_WO + j
                dve.wait_ge(s_unit, U_WO + j + 1)
                link(tt_(halves(x[:, j, :]), halves(x[:, j, :]), acc[L % 2], ALU.add))
                dve.sem_inc(s_accf[L % 2], 1)
                dve.sem_inc(s_x1, 1)
            rsqrt(1.0 / D, 2 * KT + XT, 2 + GROUPS)
            normed(1, "ffn", g_lo, g_hi)

            def top16(vals, idx, src, src2, rows):
                for i in range(rows):
                    last = dve.max(vals[:, i, 0:8], src[:, i, :])
                link(last)
                for i in range(rows):
                    dve.max_index(idx[:, i, 0:8], vals[:, i, 0:8], src[:, i, :])
                    last = dve.match_replace(src2[:, i, :], vals[:, i, 0:8], src[:, i, :], LOWEST)
                link(last)
                for i in range(rows):
                    last = dve.max(vals[:, i, 8:16], src2[:, i, :])
                link(last)
                for i in range(rows):
                    last = dve.max_index(idx[:, i, 8:16], vals[:, i, 8:16], src2[:, i, :])
                link(last)

            for tt, (t0, n) in enumerate(TT):
                dve.wait_ge(s_scs, tt + 1)
                top16(top[0:n], topi[0:n], sc[0:n], sc2[0:n], 2 * PH)
                pair = top[0:n].rearrange("p (h i) k -> p h i k", i=2)
                shape = [n, PH, TOPK, TOPK]
                link(tt_(cand[0:n].rearrange("p h (j k) -> p h j k", j=TOPK),
                         pair[:, :, 0, :].unsqueeze(3).to_broadcast(shape),
                         pair[:, :, 1, :].unsqueeze(2).to_broadcast(shape), ALU.add))
                top16(best[0:n], besti[0:n].rearrange("p (h k) -> p h k", h=PH), cand[0:n], cand2[0:n], PH)
                link(dve.tensor_copy(sm[0:n, 0, :], best[0:n, :, 0]))
                tt_(best[0:n], best[0:n], sm[0:n, 0, :].unsqueeze(2).to_broadcast([n, PH, TOPK]),
                    ALU.subtract).then_inc(s_be, 1)
                ts_(bsel[0:n, 0, :], besti[0:n], 4, None, ALU.logical_shift_right)
                ts_(bsel[0:n, 1, :], besti[0:n], 15, None, ALU.bitwise_and)
                link(dve.tensor_copy(topf[0:n], topi[0:n]))
                link(dve.tensor_copy(bself[0:n], bsel[0:n]))
                keyf = topf[0:n].rearrange("p (h i) k -> p h i k", i=2)
                for i, eq in enumerate((cand, cand2)):
                    e3 = eq[0:n].rearrange("p h (k j) -> p (h k) j", j=TOPK)
                    tt_(e3, bself[0:n, i, :].unsqueeze(2).to_broadcast([n, PH * TOPK, TOPK]),
                        iota[0:n, 0:TOPK].unsqueeze(1).to_broadcast([n, PH * TOPK, TOPK]), ALU.is_equal)\
                        .then_inc(s_dc, 1)
                    chain[0] += 1
                dve.wait_ge(s_dc, chain[0])
                for i, eq in enumerate((cand, cand2)):
                    e4 = eq[0:n].rearrange("p h (k j) -> p h k j", j=TOPK)
                    tt_(e4, e4, keyf[:, :, i, :].unsqueeze(2).to_broadcast(shape), ALU.mult).then_inc(s_dc, 1)
                    chain[0] += 1
                dve.wait_ge(s_dc, chain[0])
                if tt:
                    dve.wait_ge(s_pkT, tt)
                for i, eq in enumerate((cand, cand2)):
                    dve.tensor_reduce(pick[0:n, i, :], eq[0:n].rearrange("p h (k j) -> p (h k) j", j=TOPK),
                                      AX.X, ALU.add)
                dve.wait_ge(s_bx, tt + 1)
                link(dve.tensor_reduce(sm[0:n, 0, :], best[0:n], AX.X, ALU.add))
                link(dve.reciprocal(sm[0:n, 1, :], sm[0:n, 0, :]))
                tt_(pick[0:n, 2, :].rearrange("p (h k) -> p h k", h=PH), best[0:n],
                    sm[0:n, 1, :].unsqueeze(2).to_broadcast([n, PH, TOPK]), ALU.mult).then_inc(s_pk, 1)

            def one_hots(b, par, first, t):
                if not first:
                    dve.wait_ge(s_gm, b - 1)
                tt_(oh_2[:, par], iota[:].unsqueeze(1).to_broadcast([P, TB, P]),
                    pickT[:, 1, t(0, TB)].unsqueeze(2).to_broadcast([P, TB, P]), ALU.is_equal)
                for j in range(TB):
                    last = ts_(oh_g[:, par, j, :], iota[:], pickT[:, 0, t(j, 1)], pickT[:, 2, t(j, 1)],
                               ALU.is_equal, ALU.mult)
                last.then_inc(s_oh, 1)

            dve.wait_ge(s_pks, len(TT))
            for b in range(2):
                one_hots(b, b, True, lambda j, w: slice(b * TB + j, b * TB + j + w))
            with dve.Fori(1, NB // 2) as i:
                for par in range(2):
                    one_hots(i * 2 + par, par, False, lambda j, w: bass.ds(i * 2 * TB + (par * TB + j), w))
            for b in range(NB // 2 * 2, NB):
                one_hots(b, b % 2, False, lambda j, w: slice(b * TB + j, b * TB + j + w))

            L0 = U_PEER - L_SHIFT

            def gate_group(g, par, half):
                for u in range(0, GI, 2):
                    if u % 4 == 0:
                        dve.wait_ge(s_gl[u // 4], g * 16 + 16)
                    for b in range(2):
                        dve.wait_ge(s_accf[(L0 + b) % 2], (L0 + b) // 2 + u // 2 + half + 1)
                        v = ge[b][:].rearrange("p (n t) -> p n t", t=TB)
                        tt_(v, v, gbuf[:, u // 4, :, (u + b) % 4, :], ALU.mult).then_inc(s_pm, 1)
                    for b in range(2):
                        dve.wait_ge(s_phi, g * GI + u + b + 1)
                        tt_(p_lo[par][:, u + b, :], ge[b][:], p_hi[par][:, u + b, :].bitcast(F32),
                            ALU.subtract).then_inc(s_p, 1)

            def add_group(m0, g):
                for u in range(KT):
                    p_ = (L0 + u) % 2
                    dve.wait_ge(s_unit, U_PEER + m0 + u + 1)
                    tt_(halves(x[:, u, :]), halves(x[:, u, :]), acc[p_], ALU.add).then_inc(s_x2, 1)
                    dve.wait_ge(s_x2, g * KT + u + 1)
                    dve.sem_inc(s_accf[p_], 1)

            gate_group(0, 0, 0)
            with dve.Fori(0, NG // 2 - 1) as i:
                gate_group(i * 2 + 1, 1, i * 16 + 4)
                add_group(i * 32 + 16, i * 2)
                gate_group(i * 2 + 2, 0, i * 16 + 12)
                add_group(i * 32 + 32, i * 2 + 1)
            e0 = 32 * (NG // 2 - 1)
            gate_group(NG - 1, 1, e0 // 2 + 4)
            add_group(e0 + 16, NG - 2)
            add_group(e0 + 24, NG - 1)

            rsqrt(1.0 / D, 3 * KT + XT, 3 + GROUPS)
            for k in range(KT):
                if k >= 2:
                    dve.wait_ge(s_yd[k % 2], 16 * (k // 2))
                stt(yo[k % 2][:], x[:, k, :], c_("fin", k), inv[:], ALU.mult, ALU.mult).then_inc(s_yo, 1)


def inputs_of(x_prompt, x_sample, state_conv_a, state_conv_ssd, state_ssm, meta_tokens, norm_mix_w, w_in,
              conv_a_w, w_a_out, ssd_conv_w, ssd_conv_b, ssd_dt_bias, ssd_a_log, ssd_d, ssd_norm_w,
              w_ssd_out, w_o, norm_ffn_w, peer_w_q, peer_sub_keys, peer_u, peer_v, norm_final_w):
    import numpy as np
    A = lambda a: np.asarray(a)
    tokens = np.concatenate([A(meta_tokens), A(x_prompt)[0], A(x_sample).reshape(TS, D)], 0)
    xT = np.ascontiguousarray(tokens.reshape(T, KT, P).transpose(2, 1, 0))

    def tiles(w):
        return w.reshape(KT, P, -1, P).transpose(2, 1, 0, 3).reshape(-1, P, D)

    wi = A(w_in)[0]
    o = np.cumsum([0, D, D, D, 2 * D, CT * P, HEADS, D, D])
    aB, aC, aX, z, xbc, dt, ga, gb = (wi[:, o[i]:o[i + 1]] for i in range(8))
    dt_p = np.zeros((D, P), wi.dtype)
    dt_p[:, :HEADS] = dt
    units = np.empty((UNITS, P, D), wi.dtype)
    units[U_DT:U_XBC] = tiles(dt_p)
    units[U_XBC:U_A] = tiles(xbc)
    for i, w in enumerate((aC, aX, aB)):
        units[U_A + i:U_AO:3] = tiles(w)
    units[U_AO:U_GB:2] = tiles(A(w_a_out)[0])
    units[U_AO + 1:U_GB:2] = tiles(ga)
    units[U_GB:U_Z] = tiles(gb)
    units[U_Z:U_SO] = tiles(z)
    so = A(w_ssd_out)[0].reshape(2, KT, P, KT, P).transpose(3, 0, 2, 1, 4).reshape(2 * KT, P, D)
    units[U_SO:U_WO] = so
    units[U_WO:U_WQ] = tiles(A(w_o)[0])
    units[U_WQ:U_PEER] = tiles(A(peer_w_q)[0])
    uu = A(peer_u)[0].reshape(NKEYS, NKEYS, KT, P).transpose(1, 3, 2, 0).reshape(NG, GI, P, D)
    vv = A(peer_v)[0].reshape(NKEYS, NG, GI, KT, P).transpose(1, 3, 0, 2, 4).reshape(NG, KT, P, D)
    e = units[U_PEER:].reshape(2 * NG, GI, P, D)
    e[0] = uu[0]
    e[1:2 * NG - 1:2] = uu[1:]
    e[2:2 * NG - 1:2] = vv[:NG - 1]
    e[2 * NG - 1] = vv[NG - 1]
    keys = np.ascontiguousarray(A(peer_sub_keys)[0].transpose(3, 0, 1, 2).reshape(P, 2 * PH, NKEYS))
    colp = lambda a: A(a).reshape(-1, P).T
    cols = np.ascontiguousarray(np.concatenate([
        colp(norm_mix_w), colp(norm_ffn_w), colp(norm_final_w),
        A(conv_a_w)[0].reshape(3, KT, P).transpose(2, 1, 0).reshape(P, 3 * KT),
        A(ssd_conv_w)[0].reshape(4, CT, P).transpose(2, 1, 0).reshape(P, 4 * CT),
        colp(ssd_conv_b), colp(ssd_norm_w), colp(np.repeat(A(ssd_d)[0], HEADDIM))], 1))
    heads = np.ascontiguousarray(np.stack([A(ssd_dt_bias)[0], A(ssd_a_log)[0]], 1))
    hist = lambda a, n: np.ascontiguousarray(A(a)[0].reshape(DEC_B, -1, n, P).transpose(3, 2, 0, 1))
    ssm = np.ascontiguousarray(A(state_ssm)[0].reshape(DEC_B, GROUPS, GW, STATE).transpose(3, 1, 0, 2))
    return dict(xT=xT, units=units, keys=keys, cols=cols, heads=heads, hist_a=hist(state_conv_a, KT),
                hist_s=hist(state_conv_ssd, CT), ssm_in=ssm)


OUTS = dict(yT=(P, KT, T), new_a=(P, KT, 1 + DEC_B, HA), new_s=(P, CT, 1 + DEC_B, HS),
            ssm_p=(P, GROUPS, GW), ssm_s=(P, GROUPS, DEC_B, GW))


def outputs_of(yT, new_a, new_s, ssm_p, ssm_s):
    import numpy as np
    y = yT.transpose(2, 1, 0).reshape(T, D)
    conv = lambda a: np.ascontiguousarray(a.transpose(2, 3, 1, 0)).reshape(1, 1 + DEC_B, a.shape[3], -1)
    na, ns = conv(new_a), conv(new_s)
    sp = ssm_p.transpose(1, 2, 0).reshape(1, 1, HEADS, HEADDIM, STATE)
    ss = ssm_s.transpose(2, 1, 3, 0).reshape(1, DEC_B, HEADS, HEADDIM, STATE)
    c = np.ascontiguousarray
    return (c(y[N_META:TP])[None], c(y[TP:]).reshape(DEC_B, DEC_L, D), c(na[:, :1]), c(ns[:, :1]), c(sp),
            c(na[:, 1:]), c(ns[:, 1:]), c(ss))


def kernel(**inputs):
    import numpy as np
    import concourse.bacc as bacc
    from concourse.bass_utils import run_bass_kernel_spmd

    nc = bacc.Bacc("TRN2", target_bir_lowering=False, num_devices=1)
    arrays = inputs_of(**inputs)
    args = [nc.dram_tensor(k, a.shape, mybir.dt.from_np(a.dtype), kind="ExternalInput").ap()
            for k, a in arrays.items()]
    args += [nc.dram_tensor(k, s, F32, kind="ExternalOutput").ap() for k, s in OUTS.items()]
    trunk(nc, *args)
    r = run_bass_kernel_spmd(nc, [arrays], core_ids=[0])
    return outputs_of(**{k: r.results[0][k] for k in OUTS})
```

```python
from contextlib import ExitStack

import concourse.bass as bass
from concourse import mybir

ALU = mybir.AluOpType
ACT = mybir.ActivationFunctionType
AX = mybir.AxisListType
F32 = mybir.dt.float32
F32R = mybir.dt.float32r
U32 = mybir.dt.uint32

P = 128
D = 1024
KT = D // P
N_META, SEQ = 16, 512
DEC_B, DEC_L = 8, 8
TP = N_META + SEQ
TS = DEC_B * DEC_L
T = TP + TS
HF = T // 2
HP = TP - HF
EPS = 1e-6
HEADS, HEADDIM, STATE = 32, 64, 128
GROUPS, HPG = 4, 8
GW = HPG * HEADDIM
XT = 2 * D // P
CT = XT + 2 * GROUPS
HA, HS = 2, 3
LA = HA + TP + DEC_B * (HA + DEC_L)
LS = HS + TP + DEC_B * (HS + DEC_L)
CHUNKS = [(0, N_META)] + [(N_META + P * c, P) for c in range(SEQ // P)] + [(TP, TS)]
NC = len(CHUNKS)
PH, NKEYS, TOPK = 8, 128, 16
TT = [(t, min(P, T - t)) for t in range(0, T, P)]
TB = 16
NB = T // TB
GI = 8
NG = NKEYS // GI
LOWEST = -3.0e38
M_TOP = 8 * len(TT)
M_GATE = M_TOP + 2 * NB

N_DT, N_XBC, N_A, N_Z, N_GB, N_GA, N_AO, N_SO, N_WO, N_WQ = 1, CT, 3 * KT, XT, KT, KT, KT, 2 * KT, KT, 2 * KT
U_DT = 0
U_XBC = U_DT + N_DT
U_A = U_XBC + N_XBC
U_Z = U_A + N_A
U_GB = U_Z + N_Z
U_GA = U_GB + N_GB
U_AO = U_GA + N_GA
U_SO = U_AO + N_AO
U_WO = U_SO + N_SO
U_WQ = U_WO + N_WO
U_PEER = U_WQ + N_WQ
UNITS = U_PEER + 2 * NKEYS
SPILL = U_GA - U_A
L_WO = U_SO + KT
L_SHIFT = U_WO - L_WO
TURN0 = 4
RAW = 4
COLS = dict(mix=0, ffn=8, fin=16, ca=24, cs=48, cb=144, sn=168, dd=184)
NCOLS = 200


def trunk(nc, xT, units, keys, cols, heads, hist_a, hist_s, ssm_in,
          yT, new_a, new_s, ssm_p, ssm_s):
    gate_dram = nc.dram_tensor("gate_scratch", [NG, P, NB, GI, TB], F32).ap()
    spill = nc.dram_tensor("parked_tiles", [SPILL, P, T], F32).ap()
    act_dram = nc.dram_tensor("activation_scratch", [NKEYS, P, T], F32).ap()
    base = ((nc.sbuf_base + 63) // 64) * 64
    end = nc.sbuf_usable_end
    with ExitStack() as ctx:
        def at(name, off, shape, dt=F32):
            n = 4
            for s in shape[1:]:
                n *= s
            assert base + off + n <= end, (name, off + n, end - base)
            return nc.alloc_sbuf_tensor_at(name, shape, dt, offset=base + off)

        def sem(name):
            return ctx.enter_context(nc.semaphore(name))

        TW = 4 * T
        LSB, LAB = ((4 * w + 31) // 32 * 32 for w in (LS, LA))
        pos = [0]

        def const(name, shape, dt=F32):
            n = 4
            for s in shape[1:]:
                n *= s
            r = at(name, pos[0], shape, dt)
            pos[0] += (n + 31) // 32 * 32
            return r

        ident = const("ident", [P, P])
        causal = const("causal", [P, P])
        smask = const("smask", [TS, DEC_B, DEC_L])
        rowmask = const("rowmask", [TS, DEC_B])
        iota_i = const("iota_i", [P, P], mybir.dt.int32)
        iota = const("iota", [P, P])
        ones = const("ones", [P, P])
        col = const("col", [P, NCOLS])
        hd = const("hd", [HEADS, 4])
        hista = const("hista", [P, KT, DEC_B, HA])
        hists = const("hists", [P, CT, DEC_B, HS])
        newa = const("newa", [P, KT, 1 + DEC_B, HA])
        news = const("news", [P, CT, 1 + DEC_B, HS])
        R_HT = pos[0]
        R_RING = R_HT + 2 * KT * TW
        R_XS = R_RING + (RAW + 4) * 4 * D
        R1 = R_XS + XT * TW
        R_TMP = R1 + 2 * KT * TW
        R_X = R_TMP + 18400
        R_MA = R_X + KT * TW
        h_hi = at("h_hi", R_HT, [P, KT, T], F32R)
        h_lo = at("h_lo", R_HT + KT * TW, [P, KT, T], F32R)
        m_hi = at("m_hi", R1, [P, KT, T], F32R)
        m_lo = at("m_lo", R1 + KT * TW, [P, KT, T], F32R)
        g_hi = at("g_hi", R_HT, [P, KT, T], F32R)
        g_lo = at("g_lo", R_HT + KT * TW, [P, KT, T], F32R)
        raw = at("raw", R_RING, [P, RAW, D])
        w_hi = at("w_hi", R_RING + RAW * 4 * D, [P, 2, D], F32R)
        w_lo = at("w_lo", R_RING + (RAW + 2) * 4 * D, [P, 2, D], F32R)
        x = at("x", R_X, [P, KT, T])
        xs = at("xs", R_XS, [P, XT, T])
        bc = at("bc", R1, [P, 2 * GROUPS, T])
        tmp = [at(f"tmp{i}", R_TMP + i * TW, [P, T]) for i in range(7)]
        sq, hf, var, inv, nw = tmp[0:2], tmp[2:4], tmp[4], tmp[5], tmp[6]
        R_C = R1 + 2 * GROUPS * TW
        line_s = [at(f"line_s{i}", R_C + i * LSB, [P, LS]) for i in range(2)]
        cv_s = [at(f"cv_s{i}", R_C + (2 + i) * LSB, [P, LS]) for i in range(2)]
        spos = [R_C + 4 * LSB]

        def scr(name, shape):
            n = 4
            for s in shape[1:]:
                n *= s
            r = at(name, spos[0], shape)
            spos[0] += (n + 31) // 32 * 32
            return r

        dq = scr("dq", [P, T])
        sp = [at(f"sp{i}", R_C + i * TW, [HEADS, T]) for i in range(4)]
        reset = scr("reset", [HEADS, T])
        dqT = scr("dqT", [P, NC, P])
        NE = NC - 1 + DEC_B
        bde = scr("bde", [HEADS, HEADS, NE])
        dend = scr("dend", [P, HEADS, NE])
        bd = scr("bd", [HEADS, HPG, P])
        wT = scr("wT", [P, HPG, P])
        xdt = scr("xdt", [P, GW])
        xde = scr("xde", [P, GW])
        ysb = scr("ysb", [P, GW])
        state = scr("state", [P, GROUPS, GW])
        bT = scr("bT", [P, P])
        cbm = scr("cbm", [P, P])
        bTm = scr("bTm", [TS, DEC_B, P])
        cm = scr("cm", [P, DEC_B, TS + DEC_L])
        seg = at("seg", R_C, [P, HPG, P])
        prev = scr("prev", [P, DEC_B, GW])
        stage = [scr(f"stage{i}", [P, T]) for i in range(2)]
        v_hi = at("v_hi", R1, [P, KT, T], F32R)
        v_lo = at("v_lo", R1 + KT * TW, [P, KT, T], F32R)
        line_a = at("line_a", R_TMP, [P, LA])
        cv_a = at("cv_a", R_TMP + LAB, [P, LA])
        v_f = at("v_f", R_TMP + 2 * LAB, [P, T])
        cxb = [at("cxb0", R_X + 4 * TW, [P, 3, T]), at("cxb1", R_TMP + 4 * TW, [P, 3, T])]
        ma = at("ma", R_MA, [P, KT, T])
        sgb = at("sgb", R_X, [P, KT, T])
        n_hi = at("n_hi", R_XS, [P, XT, T], F32R)
        zb = [at(f"zb{i}", R_X + 4 * i * TW, [P, 4, T]) for i in range(2)]
        n_lo = at("n_lo", R_HT, [P, XT, T], F32R)
        mt = [at(f"mt{i}", R_TMP + i * TW, [P, T]) for i in range(2)]
        q = at("q", R_XS, [P, 2 * PH, T])
        tpos = [R1]

        def tk(name, shape, dt=F32):
            n = 4
            for s in shape[1:]:
                n *= s
            r = at(name, tpos[0], shape, dt)
            tpos[0] += (n + 31) // 32 * 32
            assert tpos[0] <= R_X
            return r

        sc = tk("sc", [P, 2 * PH, NKEYS])
        sc2 = tk("sc2", [P, 2 * PH, NKEYS])
        cand = tk("cand", [P, PH, TOPK * TOPK])
        cand2 = tk("cand2", [P, PH, TOPK * TOPK])
        key_sb = tk("key_sb", [P, 2 * PH, NKEYS])
        top = tk("top", [P, 2 * PH, TOPK])
        topi = tk("topi", [P, 2 * PH, TOPK], U32)
        topf = tk("topf", [P, 2 * PH, TOPK])
        best = tk("best", [P, PH, TOPK])
        besti = tk("besti", [P, PH * TOPK], U32)
        bsel = tk("bsel", [P, 2, PH * TOPK], U32)
        bself = tk("bself", [P, 2, PH * TOPK])
        sm = tk("sm", [P, 2, PH])
        pick = tk("pick", [P, 3, PH * TOPK])
        pickT = at("pickT", R_MA, [P, 3, T])
        oh_g = at("oh_g", R_XS, [P, 2, TB, P])
        oh_2 = at("oh_2", R_XS + 4 * 2 * TB * P, [P, 2, TB, P])
        gt = at("gt", R_TMP, [P, 2, NKEYS, TB])
        ge = [at(f"ge{i}", R_MA + 3 * TW + i * TW, [P, T]) for i in range(2)]
        p_hi = [at("p_hi0", R1, [P, GI, T], F32R), at("p_hi1", R_HT, [P, GI, T], F32R)]
        p_lo = [at("p_lo0", R1 + GI * TW, [P, GI, T], F32R), at("p_lo1", R_HT + GI * TW, [P, GI, T], F32R)]
        abuf = at("abuf", R_XS, [P, 2, GI // 2, T])
        gbuf = at("gbuf", R_XS + GI * TW, [P, 2, NB, GI // 2, TB])
        yo = [at(f"yo{i}", R_XS + i * TW, [P, T]) for i in range(2)]

        ps = ctx.enter_context(nc.psum_tensor("ps", [P, 8, 512], F32))
        acc = [ps[:, 0:2, 0:HF], ps[:, 2:4, 0:HF]]
        ssp = ps[:, 4:6, 0:HF]
        S0, S1, S2, S3 = (ps[:, 4 + i, :] for i in range(4))

        ld = [sem(f"unit_loaded{i}") for i in range(RAW)]
        s_wbeg = sem("split_begun")
        s_whi = sem("weights_hi")
        s_w = sem("weights_split")
        s_unit = sem("unit_used")
        s_accf = [sem("acc0_read"), sem("acc1_read")]
        s_x = sem("x_loaded")
        s_in = sem("small_inputs_loaded")
        s_c = sem("constants_made")
        s_pc = sem("pool_chain")
        s_dc = sem("vector_chain")
        s_ac = sem("scalar_chain")
        s_sq = sem("squares_ready")
        s_ss = sem("squares_summed")
        s_var = sem("variance_ready")
        s_std = sem("deviation_ready")
        s_hf = sem("normed_ready")
        s_hhi = sem("normed_hi")
        s_h = sem("normed_split")
        s_line = sem("conv_line_ready")
        s_cv = sem("conv_done")
        s_xbc = sem("xbc_ready")
        s_sp = sem("dt_for_exp")
        s_spe = sem("dt_exp_done")
        s_ds = sem("decays_ready")
        s_de = sem("decay_exp_done")
        s_dT = sem("decays_transposed")
        s_dTs = sem("decays_copied")
        s_bd = sem("head_rows_ready")
        s_pre = sem("chunk_products")
        s_seg = sem("segments_ready")
        s_exp = sem("segments_exp")
        s_wT = sem("mix_weights_ready")
        s_y = sem("chunk_outputs")
        s_ysb = sem("chunk_output_ready")
        s_st = sem("chunk_states")
        s_state = sem("state_updated")
        s_yT = sem("output_turned")
        s_y2 = sem("output_merged")
        s_pl = sem("sample_state_loaded")
        s_sst = sem("sample_state_product")
        s_snew = sem("sample_state_updated")
        s_po = sem("sample_state_stored")
        s_parked = [sem("parked0"), sem("parked1")]
        s_cxb = [sem("cxb_loaded0"), sem("cxb_loaded1")]
        s_zl = [sem("silu_z_loaded0"), sem("silu_z_loaded1")]
        s_gbl = [sem("gate_b_loaded0"), sem("gate_b_loaded1")]
        s_vf = sem("v_ready")
        s_vhi = sem("v_hi_ready")
        s_v = sem("v_split")
        s_gz = sem("gated_ready")
        s_nf = sem("group_normed_ready")
        s_nhi = sem("group_normed_hi")
        s_n = sem("group_normed_split")
        s_mf = sem("merge_ready")
        s_mhi = sem("merge_hi")
        s_m = sem("merge_split")
        s_xr = sem("x_reloaded")
        s_x1 = sem("x_after_mixer")
        s_q = sem("queries_ready")
        s_key = sem("keys_loaded")
        s_sc = sem("scores_ready")
        s_scs = sem("scores_copied")
        s_be = sem("softmax_shifted")
        s_bx = sem("softmax_exp")
        s_pk = sem("picks_ready")
        s_pkT = sem("picks_turned")
        s_pks = sem("picks_copied")
        s_oh = sem("one_hots_ready")
        s_gm = sem("gates_built")
        s_gt = sem("gates_copied")
        s_gs = [sem("gates_stored0"), sem("gates_stored1")]
        s_gl = [sem("gates_loaded0"), sem("gates_loaded1")]
        s_al = [sem("activations_loaded0"), sem("activations_loaded1")]
        s_as = [sem("activations_stored0"), sem("activations_stored1")]
        s_scf = sem("scores_read")
        s_pm = sem("expert_gated")
        s_phi = sem("expert_hi")
        s_p = sem("expert_split")
        s_x2 = sem("x_after_experts")
        s_yo = sem("y_ready")
        s_yd = [sem("y_stored0"), sem("y_stored1")]
        s_out = sem("states_stored")

        block = ctx.enter_context(nc.Block())

        def halves(a):
            return a.rearrange("p (a t) -> p a t", a=2)

        def pieces(a, line, h):
            tail = line[:, h + TP:].rearrange("p (b r) -> p b r", b=DEC_B)
            return [(a[:, 0, :], line[:, h:h + HF]), (a[:, 1, 0:HP], line[:, h + HF:h + TP]),
                    (a[:, 1, HP:HF].rearrange("p (b r) -> p b r", b=DEC_B), tail[:, :, h:])]

        def sample_view(a):
            return a.rearrange("p (b r) -> p b r", b=DEC_B)

        def line_out(cv, h):
            return sample_view(cv[:, h + TP:])[:, :, 0:DEC_L]

        def c_(name, i):
            return col[:, COLS[name] + i:COLS[name] + i + 1]

        @block.sync
        def _(sp_):
            sp_.dma_start(x[:], xT).then_inc(s_x, 16)
            sp_.dma_start(col[:], cols).then_inc(s_in, 16)
            sp_.dma_start(hd[:, 0:2], heads).then_inc(s_in, 16)
            sp_.dma_start(hista[:], hist_a).then_inc(s_in, 16)
            sp_.dma_start(hists[:], hist_s).then_inc(s_in, 16)
            for n in range(RAW):
                sp_.dma_start(raw[:, n, :], units[n]).then_inc(ld[n], 16)

            def stream(n, r):
                sp_.wait_ge(s_w, n - RAW + 1)
                sp_.dma_start(raw[:, r, :], units[bass.ds(n, 1)].rearrange("a p k -> (a p) k")).then_inc(ld[r], 16)

            with sp_.Fori(1, UNITS // RAW) as i:
                for r in range(RAW):
                    stream(i * RAW + r, r)
            for n in range(UNITS // RAW * RAW, UNITS):
                sp_.wait_ge(s_w, n - RAW + 1)
                sp_.dma_start(raw[:, n % RAW, :], units[n]).then_inc(ld[n % RAW], 16)

        @block.gpsimd
        def _(pool):
            chain = [0]

            def link(ins):
                chain[0] += 1
                ins.then_inc(s_pc, 1)
                pool.wait_ge(s_pc, chain[0])

            pool.memset(ones[:], 1.0)
            pool.memset(ident[:], 0.0)
            pool.memset(causal[:], 1.0)
            pool.memset(smask[:], 1.0)
            pool.iota(iota_i[:], [[1, P]], base=0, channel_multiplier=0)
            link(pool.memset(rowmask[:], 1.0))
            pool.affine_select(out=ident[:], in_=ident[:], compare_op=ALU.not_equal, fill=1.0, base=0,
                               pattern=[[-1, P]], channel_multiplier=1)
            pool.affine_select(out=causal[:], in_=causal[:], compare_op=ALU.is_ge, fill=0.0, base=0,
                               pattern=[[1, P]], channel_multiplier=-1)
            pool.affine_select(out=smask[:], in_=smask[:], compare_op=ALU.is_ge, fill=0.0, base=0,
                               pattern=[[DEC_L, DEC_B], [1, DEC_L]], channel_multiplier=-1)
            link(pool.affine_select(out=rowmask[:], in_=rowmask[:], compare_op=ALU.is_ge, fill=0.0, base=0,
                                    pattern=[[-DEC_L, DEC_B]], channel_multiplier=1))
            pool.affine_select(out=smask[:], in_=smask[:], compare_op=ALU.is_ge, fill=0.0, base=0,
                               pattern=[[-DEC_L, DEC_B], [0, DEC_L]], channel_multiplier=1)
            pool.tensor_copy(iota[:], iota_i[:])
            pool.affine_select(out=rowmask[:], in_=rowmask[:], compare_op=ALU.is_ge, fill=0.0,
                               base=DEC_L - 1, pattern=[[DEC_L, DEC_B]], channel_multiplier=-1)\
                .then_inc(s_c, 1)

            def split_unit(r, s, landed, used, hi_done):
                pool.wait_ge(ld[r], landed)
                if used is not None:
                    pool.wait_ge(s_unit, used)
                pool.sem_inc(s_wbeg, 1)
                pool.tensor_scalar(w_hi[:, s, :], raw[:, r, :], 1.0, 1.0, ALU.mult, ALU.mult).then_inc(s_whi, 1)
                pool.wait_ge(s_whi, hi_done)
                pool.tensor_tensor(w_lo[:, s, :], raw[:, r, :], w_hi[:, s, :].bitcast(F32), ALU.subtract)\
                    .then_inc(s_w, 1)

            for n in range(RAW):
                split_unit(n, n % 2, 16, n - 1 if n >= 2 else None, n + 1)
            with pool.Fori(1, UNITS // RAW) as i:
                for r in range(RAW):
                    split_unit(r, r % 2, i * 16 + 16, i * RAW + r - 1, i * RAW + r + 1)
            for n in range(UNITS // RAW * RAW, UNITS):
                split_unit(n % RAW, n % 2, 16 * (n // RAW + 1), n - 1, n + 1)

        @block.tensor
        def _(pe):
            mm = pe.matmul

            def unit(n, L, mov_hi, mov_lo, k0=0, start=True, stop=True, slot=None, par=None,
                     ks=(0, KT)):
                s = n % 2 if slot is None else slot
                a = acc[L % 2 if par is None else par]
                for k in range(*ks):
                    wh, wl = (w[:, s, k * P:(k + 1) * P] for w in (w_hi, w_lo))
                    for i, (w, m) in enumerate(((wh, mov_hi), (wh, mov_lo), (wl, mov_hi))):
                        for h in range(2):
                            last = mm(a[:, h, :], w, m[:, k0 + k, h * HF:(h + 1) * HF],
                                      start=start and k == 0 and i == 0, stop=stop and k == KT - 1 and i == 2)
                if ks[1] == KT:
                    last.then_inc(s_unit, 1)

            def part(n, k0, k1):
                if k0 == 0:
                    pe.wait_ge(s_accf[n % 2], n // 2)
                    pe.wait_ge(s_w, n + 1)
                unit(n, n, h_hi, h_lo, ks=(k0, k1))

            def tile(n, L, mov_hi, mov_lo, units_=1):
                if L >= 2:
                    pe.wait_ge(s_accf[L % 2], L // 2)
                for u in range(units_):
                    pe.wait_ge(s_w, n + u + 1)
                    unit(n + u, L, mov_hi, mov_lo, u * KT, u == 0, u == units_ - 1)

            def square_sums(r):
                for k in range(KT):
                    pe.wait_ge(s_sq, KT * r + k + 1)
                    for h in range(2):
                        last = mm(ssp[:, h, :], ones[:], sq[k % 2][:, h * HF:(h + 1) * HF],
                                  start=k == 0, stop=k == KT - 1)
                    last.then_inc(s_ss, 1)

            pe.wait_ge(s_c, 1)
            square_sums(0)
            pe.wait_ge(s_h, KT)
            for n in range(U_DT, U_A + 1):
                tile(n, n, h_hi, h_lo)
                c = n - U_XBC - TURN0
                if c == 0:
                    pe.wait_ge(s_ds, 1)
                elif 0 < c <= NC:
                    pe.wait_ge(s_dTs, c)
                if 0 <= c < NC:
                    t0, w = CHUNKS[c]
                    pe.transpose(S0[0:w, 0:P], dq[:, t0:t0 + w], ident[:]).then_inc(s_dT, 1)
                elif c == NC:
                    mm(S0[:, 0:HEADS * NE], ones[0:HEADS, :], bde[:].rearrange("p h e -> p (h e)"),
                       start=True, stop=True).then_inc(s_dT, 1)

            pe.wait_ge(s_xbc, CT)
            for c, (t0, n) in enumerate(CHUNKS):
                sample = c == NC - 1
                for g in range(GROUPS):
                    s = c * GROUPS + g
                    ch = slice(t0, t0 + n)
                    Bg, Cg = bc[:, g, ch], bc[:, GROUPS + g, ch]
                    pe.wait_ge(s_bd, s + 1)
                    if s:
                        pe.wait_ge(s_y2, s)
                        pe.wait_ge(s_state, s)
                    else:
                        pe.wait_ge(s_dTs, NC + 1)
                    for hh in range(2):
                        mm((S1, S2)[hh][0:n, 0:4 * n].rearrange("p (h q) -> p h q", h=4), ones[0:HEADS, 0:n],
                           bd[:, 4 * hh:4 * hh + 4, 0:n], start=True, stop=True)
                    mm(S0[0:n, 0:n], Bg, Cg, start=True, stop=True)
                    pe.transpose(S0[0:n, P:2 * P], Bg, ident[:])
                    for j in range(4):
                        last = pe.transpose(S3[0:n, j * P:(j + 1) * P], xs[:, 4 * g + j, ch], ident[:])
                    last.then_inc(s_pre, 1)
                    beside = U_A + 1 + 2 * s
                    part(beside, 0, KT)
                    pe.wait_ge(s_wT, s + 1)
                    for h in range(HPG):
                        last = mm(S1[0:n, h * HEADDIM:(h + 1) * HEADDIM], wT[0:n, h, 0:n],
                                  xdt[0:n, h * HEADDIM:(h + 1) * HEADDIM], start=True, stop=True)
                    if sample:
                        pe.wait_ge(s_pl, 16 * (g + 1))
                        cmf = cm[:].rearrange("p b r -> p (b r)")
                        for b in range(DEC_B):
                            last = mm(S2[0:n, :], cmf[:, b * TS:(b + 1) * TS], prev[:, b, :],
                                      start=b == 0, stop=b == DEC_B - 1)
                    elif c:
                        last = mm(S2[0:n, :], Cg, state[:, g, :], start=True, stop=True)
                    last.then_inc(s_y, 1)
                    if sample:
                        pe.wait_ge(s_ysb, s + 1)
                        for b in range(DEC_B):
                            k = g * DEC_B + b
                            if b >= 2:
                                pe.wait_ge(s_snew, k - 1)
                            mm((S3, S1)[b % 2], bTm[:, b, :], xde[0:n, :], start=True, stop=True)\
                                .then_inc(s_sst, 1)
                    else:
                        mm(S3, bT[0:n, :], xde[0:n, :], start=True, stop=True).then_inc(s_st, 1)
                    if beside + 1 < U_GA:
                        part(beside + 1, 0, KT // 2)
                    pe.wait_ge(s_ysb, s + 1)
                    for j in range(4):
                        last = pe.transpose(S0[:, j * n:(j + 1) * n], ysb[0:n, j * P:(j + 1) * P],
                                            ident[0:n, 0:n])
                    last.then_inc(s_yT, 1)
                    if beside + 1 < U_GA:
                        part(beside + 1, KT // 2, KT)

            for n in range(U_GA, U_AO):
                tile(n, n, h_hi, h_lo)
            pe.wait_ge(s_v, KT)
            for g in range(GROUPS):
                n = U_AO + 2 * g
                tile(n, n, v_hi, v_lo)
                for j in range(4 * g, 4 * g + 4):
                    pe.wait_ge(s_sq, KT + j + 1)
                    if j % 4 == 0 and g:
                        pe.wait_ge(s_var, 1 + g)
                    for h in range(2):
                        last = mm(ssp[:, h, :], ones[:], sq[j % 2][:, h * HF:(h + 1) * HF],
                                  start=j % 4 == 0, stop=j % 4 == 3)
                    last.then_inc(s_ss, 1)
                tile(n + 1, n + 1, v_hi, v_lo)
            pe.wait_ge(s_n, XT)
            for j in range(KT):
                tile(U_SO + 2 * j, U_SO + j, n_hi, n_lo, 2)
            pe.wait_ge(s_m, KT)
            for j in range(KT):
                tile(U_WO + j, L_WO + j, m_hi, m_lo)
            for k in range(KT):
                pe.wait_ge(s_sq, KT + XT + k + 1)
                for h in range(2):
                    last = mm(ssp[:, h, :], ones[:], sq[k % 2][:, h * HF:(h + 1) * HF],
                              start=k == 0, stop=k == KT - 1)
                last.then_inc(s_ss, 1)
            pe.wait_ge(s_h, 2 * KT)
            for j in range(N_WQ):
                tile(U_WQ + j, U_WQ - L_SHIFT + j, g_hi, g_lo)
            pe.wait_ge(s_q, N_WQ)
            pe.wait_ge(s_key, 16)
            L0 = U_PEER - L_SHIFT

            def unit_pair(m, half, mov):
                for b in range(2):
                    par = (L0 + b) % 2
                    pe.wait_ge(s_w, U_PEER + b + 1 + m)
                    pe.wait_ge(s_accf[par], (L0 + b) // 2 + half)
                    unit(None, None, mov[0], mov[1], slot=(U_PEER + b) % 2, par=par)

            def scores(tt):
                t0, n = TT[tt]
                for i in range(2 * PH):
                    last = mm(ps[0:n, 4 + i // 4, i % 4 * P:(i % 4 + 1) * P], q[:, i, t0:t0 + n],
                              key_sb[:, i, :], start=True, stop=True)
                last.then_inc(s_sc, 1)

            h_all = (g_hi, g_lo)
            scores(0)
            for tt, (t0, n) in enumerate(TT):
                unit_pair(8 * tt, 4 * tt, h_all)
                if tt + 1 < len(TT):
                    pe.wait_ge(s_scs, tt + 1)
                    if tt:
                        pe.wait_ge(s_pks, tt)
                    scores(tt + 1)
                with pe.Fori(0, 3) as j:
                    unit_pair(j * 2 + (8 * tt + 2), j + (4 * tt + 1), h_all)
                if tt + 1 < len(TT):
                    pe.wait_ge(s_scs, tt + 2)
                pe.wait_ge(s_pk, tt + 1)
                for i in range(3):
                    last = pe.transpose(S0[:, i * P:i * P + n], pick[0:n, i, :], ident[0:n, 0:n])
                last.then_inc(s_pkT, 1)

            def gates(b, par, first):
                pe.wait_ge(s_oh, b + 1)
                if not first:
                    pe.wait_ge(s_gt, b)
                for j in range(TB):
                    last = mm(ps[:, 4 + j // 4, j % 4 * P:(j % 4 + 1) * P], oh_g[:, par, j, :],
                              oh_2[:, par, j, :], start=True, stop=True)
                last.then_inc(s_gm, 1)

            pe.wait_ge(s_pks, len(TT))
            for b in range(2):
                gates(b, b, b == 0)
                unit_pair(M_TOP + 2 * b, M_TOP // 2 + b, h_all)
            with pe.Fori(1, NB // 2) as i:
                for par in range(2):
                    gates(i * 2 + par, par, False)
                    unit_pair(i * 4 + (M_TOP + 2 * par), i * 2 + (M_TOP // 2 + par), h_all)
            for b in range(NB // 2 * 2, NB):
                gates(b, b % 2, False)
                unit_pair(M_TOP + 2 * b, M_TOP // 2 + b, h_all)
            with pe.Fori(0, (NKEYS - M_GATE) // 2) as j:
                unit_pair(j * 2 + M_GATE, j + M_GATE // 2, h_all)

            def outputs(g, par):
                with pe.Fori(0, KT // 2) as j:
                    pe.wait_ge(s_p, g * GI + GI)
                    unit_pair(g * KT + j * 2 + NKEYS, g * (KT // 2) + j + NKEYS // 2, (p_hi[par], p_lo[par]))

            with pe.Fori(0, NG // 2) as i:
                for par in range(2):
                    outputs(i * 2 + par, par)

            for k in range(KT):
                pe.wait_ge(s_sq, 2 * KT + XT + k + 1)
                for h in range(2):
                    last = mm(ssp[:, h, :], ones[:], sq[k % 2][:, h * HF:(h + 1) * HF],
                              start=k == 0, stop=k == KT - 1)
                last.then_inc(s_ss, 1)

        @block.scalar
        def _(act):
            chain = [0]

            def link(ins):
                chain[0] += 1
                ins.then_inc(s_ac, 1)
                act.wait_ge(s_ac, chain[0])

            def squares(q0):
                for k in range(KT):
                    if k >= 2:
                        act.wait_ge(s_ss, q0 + k - 1)
                    act.activation(sq[k % 2][:], x[:, k, :], ACT.Square).then_inc(s_sq, 1)

            def hi_parts(r, out):
                for k in range(KT):
                    act.wait_ge(s_hf, r * KT + k + 1)
                    act.activation(out[:, k, :], hf[k % 2][:], ACT.Copy).then_inc(s_hhi, 1)

            act.wait_ge(s_x, 16)
            squares(0)
            act.wait_ge(s_var, 1)
            act.activation(inv[:], var[:], ACT.Sqrt).then_inc(s_std, 1)
            hi_parts(0, h_hi)
            act.wait_ge(s_in, 64)

            act.wait_ge(s_unit, 1)
            act.activation(halves(sp[0][:]), acc[0][0:HEADS], ACT.Identity, bias=hd[:, 0:1])
            act.activation(halves(sp[1][:]), acc[0][0:HEADS], ACT.Abs, bias=hd[:, 0:1]).then_inc(s_accf[0], 1)
            act.wait_ge(s_accf[0], 1)
            act.activation(sp[2][:], sp[1][:], ACT.Exp, scale=-1.0).then_inc(s_spe, 1)
            act.activation(hd[:, 2:3], hd[:, 1:2], ACT.Exp).then_inc(s_spe, 1)
            act.wait_ge(s_sp, 1)
            act.activation(dq[64:96, :], dq[0:32, :], ACT.Exp).then_inc(s_de, 1)
            act.activation(sp[3][:], sp[2][:], ACT.Exp).then_inc(s_de, 1)

            for j in range(CT + 1):
                if j < CT:
                    n = U_XBC + j
                    line = line_s[j % 2]
                    if j >= 2:
                        act.wait_ge(s_cv, j - 1)
                    else:
                        act.wait_ge(s_sp, 2)
                    act.activation(sample_view(line[:, HS + TP:])[:, :, 0:HS], hists[:, j], ACT.Copy)
                    act.wait_ge(s_unit, n + 1)
                    ps_ = pieces(acc[n % 2], line, HS)
                    act.activation(ps_[0][1], ps_[0][0], ACT.Copy)
                    act.activation(ps_[1][1], ps_[1][0], ACT.Copy)
                    act.activation(ps_[2][1], ps_[2][0], ACT.Copy).then_inc(s_accf[n % 2], 1)
                if j:
                    i = j - 1
                    act.wait_ge(s_cv, i + 1)
                    cv = cv_s[i % 2]
                    dst = xs[:, i, :] if i < XT else bc[:, i - XT, :]
                    act.activation(dst[:, 0:TP], cv[:, 0:TP], ACT.Silu, bias=c_("cb", i))
                    act.activation(sample_view(dst[:, TP:]), line_out(cv, HS), ACT.Silu, bias=c_("cb", i))\
                        .then_inc(s_xbc, 1)
                c = j - TURN0
                if 0 <= c < NC:
                    w = CHUNKS[c][1]
                    act.wait_ge(s_dT, c + 1)
                    act.activation(dqT[0:w, c, :], S0[0:w, 0:P], ACT.Copy).then_inc(s_dTs, 1)
                elif c == NC:
                    act.wait_ge(s_dT, NC + 1)
                    act.activation(dend[:].rearrange("p h e -> p (h e)"), S0[:, 0:HEADS * NE], ACT.Copy)\
                        .then_inc(s_dTs, 1)

            def park(n):
                b = n - U_A
                if b >= 2:
                    act.wait_ge(s_parked[b % 2], 16 * (b // 2))
                act.wait_ge(s_unit, n + 1)
                f = ACT.Copy if n < U_Z else ACT.Silu if n < U_GB else ACT.Sigmoid
                act.activation(halves(stage[b % 2][:]), acc[n % 2], f).then_inc(s_accf[n % 2], 1)
                act.wait_ge(s_accf[n % 2], n // 2 + 1)
                act.dma_start(spill[b], stage[b % 2][:]).then_inc(s_parked[b % 2], 16)

            park(U_A)

            for c, (t0, n) in enumerate(CHUNKS):
                sample = c == NC - 1
                for g in range(GROUPS):
                    s = c * GROUPS + g
                    if sample:
                        if g:
                            act.wait_ge(s_snew, DEC_B * g)
                            act.dma_start(ssm_s[:, g - 1], prev[:]).then_inc(s_po, 16)
                            act.wait_ge(s_po, 16 * g)
                        act.dma_start(prev[:], ssm_in[:, g]).then_inc(s_pl, 16)
                    act.wait_ge(s_seg, s + 1)
                    link(act.activation(seg[0:n, :, 0:n], seg[0:n, :, 0:n], ACT.Relu, scale=-1.0))
                    act.activation(seg[0:n, :, 0:n], seg[0:n, :, 0:n], ACT.Exp, scale=-1.0).then_inc(s_exp, 1)
                    for m in range(U_A + 1 + 2 * s, min(U_A + 3 + 2 * s, U_GA)):
                        park(m)
                if c == NC - 2:
                    act.wait_ge(s_state, (NC - 1) * GROUPS)
                    act.dma_start(ssm_p, state[:]).then_inc(s_out, 16)
            act.wait_ge(s_snew, DEC_B * GROUPS)
            act.dma_start(ssm_s[:, GROUPS - 1], prev[:]).then_inc(s_po, 16)
            act.dma_start(new_s, news[:]).then_inc(s_out, 16)

            for b in range(2):
                act.wait_ge(s_parked[b], 16 * SPILL // 2)
            act.wait_ge(s_y2, NC * GROUPS)
            act.wait_ge(s_po, 16 * GROUPS)
            act.wait_ge(s_out, 32)

            def load_cxb(i):
                act.dma_start(cxb[i % 2][:], spill[3 * i:3 * i + 3].rearrange("a p t -> p a t"))\
                    .then_inc(s_cxb[i % 2], 16)

            def load_z(g):
                z0 = U_Z - U_A + 4 * g
                act.dma_start(zb[g % 2][:], spill[z0:z0 + 4].rearrange("a p t -> p a t")).then_inc(s_zl[g % 2], 16)

            load_cxb(0)
            load_cxb(1)
            load_z(0)
            for i in range(KT):
                act.wait_ge(s_vf, i + 1)
                act.activation(v_hi[:, i, :], v_f[:], ACT.Copy).then_inc(s_vhi, 1)
                if i + 2 < KT:
                    load_cxb(i + 2)
                elif i == KT - 2:
                    load_z(1)
                n = U_GA + i
                act.wait_ge(s_unit, n + 1)
                act.activation(halves(ma[:, i, :]), acc[n % 2], ACT.Sigmoid).then_inc(s_accf[n % 2], 1)
            act.wait_ge(s_v, KT)
            act.dma_start(new_a, newa[:]).then_inc(s_out, 16)

            for g in range(GROUPS):
                for j in range(4 * g, 4 * g + 4):
                    act.wait_ge(s_gz, j + 1)
                    if j >= 2:
                        act.wait_ge(s_ss, KT + j - 1)
                    act.activation(sq[j % 2][:], xs[:, j, :], ACT.Square).then_inc(s_sq, 1)
                if g + 2 < GROUPS:
                    load_z(g + 2)
                else:
                    i0 = 4 * (g - 2)
                    b0 = U_GB - U_A + i0
                    act.dma_start(sgb[:, i0:i0 + 4, :], spill[b0:b0 + 4].rearrange("a p t -> p a t"))\
                        .then_inc(s_gbl[g - 2], 16)
                act.wait_ge(s_var, 2 + g)
                act.activation(inv[:], var[:], ACT.Sqrt).then_inc(s_std, 1)
                for j in range(4 * g, 4 * g + 4):
                    act.wait_ge(s_nf, j + 1)
                    act.activation(n_hi[:, j, :], hf[j % 2][:], ACT.Copy).then_inc(s_nhi, 1)
            for j in range(KT):
                act.wait_ge(s_mf, j + 1)
                act.activation(m_hi[:, j, :], ma[:, j, :], ACT.Copy).then_inc(s_mhi, 1)
            act.dma_start(x[:], xT).then_inc(s_xr, 16)
            act.wait_ge(s_x1, KT)
            squares(KT + XT)
            act.wait_ge(s_var, 2 + GROUPS)
            act.activation(inv[:], var[:], ACT.Sqrt).then_inc(s_std, 1)
            hi_parts(1, g_hi)
            act.wait_ge(s_h, 2 * KT)
            act.dma_start(key_sb[:], keys).then_inc(s_key, 16)
            for j in range(N_WQ):
                n, L = U_WQ + j, U_WQ - L_SHIFT + j
                act.wait_ge(s_unit, n + 1)
                link(act.activation(halves(q[:, j, :]), acc[L % 2], ACT.Copy))
                act.sem_inc(s_accf[L % 2], 1)
                act.sem_inc(s_q, 1)
            L0 = U_PEER - L_SHIFT

            def gelu(m, half, b, first=False):
                par = (L0 + b) % 2
                if not first:
                    act.wait_ge(s_as[b], half * 16)
                act.wait_ge(s_unit, U_PEER + 1 + m)
                act.activation(halves(ge[b][:]), acc[par], ACT.Gelu).then_inc(s_accf[par], 1)
                act.wait_ge(s_accf[par], (L0 + b) // 2 + 1 + half)
                act.dma_start(act_dram[bass.ds(m, 1)].rearrange("a p t -> (a p) t"), ge[b][:])\
                    .then_inc(s_as[b], 16)

            def scores_out(tt):
                n = TT[tt][1]
                act.wait_ge(s_sc, tt + 1)
                if tt:
                    act.wait_ge(s_scf, tt)
                act.activation(sc[0:n].rearrange("p (a b) k -> p a (b k)", a=4), ps[0:n, 4:8, :], ACT.Copy)\
                    .then_inc(s_scs, 1)

            scores_out(0)
            for tt, (t0, n) in enumerate(TT):
                for m in range(8 * tt, 8 * tt + 8):
                    if m % 8 == 3 and tt + 1 < len(TT):
                        scores_out(tt + 1)
                    if m % 8 == 5:
                        act.wait_ge(s_be, tt + 1)
                        act.activation(best[0:n], best[0:n], ACT.Exp).then_inc(s_bx, 1)
                    gelu(m, m // 2, m % 2, m < 2)
                act.wait_ge(s_pkT, tt + 1)
                act.activation(pickT[:, :, t0:t0 + n],
                               S0[:, 0:3 * P].rearrange("p (a t) -> p a t", a=3)[:, :, 0:n], ACT.Copy)\
                    .then_inc(s_pks, 1)

            def gates_out(b, par, stored):
                act.wait_ge(s_gm, b + 1)
                if stored is not None:
                    act.wait_ge(s_gs[par], stored)
                act.activation(gt[:, par].rearrange("p i t -> p t i"),
                               ps[:, 4:8, :].rearrange("p a (t i) -> p (a t) i", i=P),
                               ACT.Copy).then_inc(s_gt, 1)
                act.wait_ge(s_gt, b + 1)
                act.dma_start(gate_dram[:, :, bass.ds(b, 1)].rearrange("g p a i t -> p g (a i t)"),
                              gt[:, par].rearrange("p (g i) t -> p g (i t)", g=NG))\
                    .then_inc(s_gs[par], 16)

            for b in range(2):
                gates_out(b, b, None)
                for c in range(2):
                    gelu(M_TOP + 2 * b + c, M_TOP // 2 + b, c)
            with act.Fori(1, NB // 2) as i:
                for par in range(2):
                    gates_out(i * 2 + par, par, i * 16)
                    for c in range(2):
                        gelu(i * 4 + (M_TOP + 2 * par + c), i * 2 + (M_TOP // 2 + par), c)
            for b in range(NB // 2 * 2, NB):
                gates_out(b, b % 2, 16 * (b // 2))
                for c in range(2):
                    gelu(M_TOP + 2 * b + c, M_TOP // 2 + b, c)
            act.wait_ge(s_gs[0], 16 * ((NB + 1) // 2))
            act.wait_ge(s_gs[1], 16 * (NB // 2))

            def load_half(g, hb):
                act.dma_start(abuf[:, hb], act_dram[bass.ds(g * GI + hb * (GI // 2), GI // 2)]
                              .rearrange("m p t -> p m t")).then_inc(s_al[hb], 16)
                src = gate_dram[bass.ds(g, 1), :, :, hb * 4:hb * 4 + 4, :]
                act.dma_start(gbuf[:, hb].rearrange("p b i t -> p b (i t)"),
                              src.rearrange("a p b i t -> (a p) b (i t)")).then_inc(s_gl[hb], 16)

            def hi_part(g, u, par):
                act.wait_ge(s_pm, g * GI + u + 1)
                act.activation(p_hi[par][:, u, :], abuf[:, u // 4, u % 4, :], ACT.Copy).then_inc(s_phi, 1)

            for hb in range(2):
                load_half(0, hb)
            for m in range(M_GATE, NKEYS):
                gelu(m, m // 2, m % 2)
                if m - M_GATE < GI:
                    hi_part(0, m - M_GATE, 0)
            for b in range(2):
                act.wait_ge(s_as[b], 16 * NKEYS // 2)
            for hb in range(2):
                act.wait_ge(s_p, 4 * hb + 4)
                load_half(1, hb)

            def group(g, par, load):
                for u in range(GI):
                    hi_part(g, u, par)
                    if load and u % 4 == 3:
                        act.wait_ge(s_p, g * GI + u + 1)
                        load_half(g + 1, u // 4)

            group(1, 1, True)
            with act.Fori(1, NG // 2 - 1) as i:
                group(i * 2, 0, True)
                group(i * 2 + 1, 1, True)
            group(NG - 2, 0, True)
            group(NG - 1, 1, False)

            act.wait_ge(s_x2, GI * NG)
            squares(2 * KT + XT)
            act.wait_ge(s_var, 3 + GROUPS)
            act.activation(inv[:], var[:], ACT.Sqrt).then_inc(s_std, 1)
            for k in range(KT):
                act.wait_ge(s_yo, k + 1)
                act.dma_start(yT[:, k], yo[k % 2][:]).then_inc(s_yd[k % 2], 16)
            act.wait_ge(s_out, 48)
            for i in range(2):
                act.wait_ge(s_yd[i], 16 * KT // 2)

        @block.vector
        def _(dve):
            chain = [0]

            def link(ins):
                chain[0] += 1
                ins.then_inc(s_dc, 1)
                dve.wait_ge(s_dc, chain[0])

            tt_, ts_, stt = dve.tensor_tensor, dve.tensor_scalar, dve.scalar_tensor_tensor

            def rsqrt(scale, ss_done, std_done, between=None):
                dve.wait_ge(s_ss, ss_done)
                ts_(halves(var[:]), ssp, scale, EPS, ALU.mult, ALU.add).then_inc(s_var, 1)
                if between:
                    between()
                dve.wait_ge(s_std, std_done)
                link(dve.reciprocal(inv[:], inv[:]))
                link(tt_(nw[:], inv[:], inv[:], ALU.mult))
                link(tt_(nw[:], nw[:], var[:], ALU.mult))
                link(ts_(nw[:], nw[:], -0.5, 1.5, ALU.mult, ALU.add))
                link(tt_(inv[:], inv[:], nw[:], ALU.mult))

            def normed(r, w, out_lo, out_hi):
                for k in range(KT + 1):
                    if k < KT:
                        if k >= 2:
                            dve.wait_ge(s_h, r * KT + k - 1)
                        stt(hf[k % 2][:], x[:, k, :], c_(w, k), inv[:], ALU.mult, ALU.mult).then_inc(s_hf, 1)
                    if k:
                        i = k - 1
                        dve.wait_ge(s_hhi, r * KT + i + 1)
                        dve.wait_ge(s_hf, r * KT + i + 1)
                        tt_(out_lo[:, i, :], hf[i % 2][:], out_hi[:, i, :].bitcast(F32), ALU.subtract)\
                            .then_inc(s_h, 1)

            dve.wait_ge(s_in, 64)
            rsqrt(1.0 / D, KT, 1)
            normed(0, "mix", h_lo, h_hi)

            dve.memset(reset[:], 1.0)
            dve.wait_ge(s_spe, 2)
            link(ts_(sp[1][:], sp[2][:], 2.0, None, ALU.add))
            link(dve.reciprocal(sp[1][:], sp[1][:]))
            link(tt_(sp[1][:], sp[1][:], sp[2][:], ALU.mult))
            link(tt_(sp[2][:], sp[1][:], sp[1][:], ALU.mult))
            link(ts_(sp[3][:], sp[2][:], 2.0 / 17, 2.0 / 15, ALU.mult, ALU.add))
            for k in (13, 11, 9, 7, 5, 3, 1):
                link(tt_(sp[3][:], sp[3][:], sp[2][:], ALU.mult))
                link(ts_(sp[3][:], sp[3][:], 2.0 / k, None, ALU.add))
            link(tt_(sp[3][:], sp[3][:], sp[1][:], ALU.mult))
            dve.memset(reset[:, 0:1], 0.0)
            dve.memset(reset[:, N_META:TP:P], 0.0)
            dve.memset(reset[:, TP:T:DEC_L], 0.0)
            link(stt(dq[32:64, :], sp[0][:], 0.0, sp[3][:], ALU.max, ALU.add))
            link(ts_(sp[1][:], dq[32:64, :], hd[:, 2:3], -1.0, ALU.mult, ALU.mult))
            link(dve.tensor_tensor_scan(dq[0:32, :], reset[:], sp[1][:], 0.0, ALU.mult, ALU.add))
            for c, (t0, n) in enumerate(CHUNKS[:-1]):
                last_c = dq[0:32, t0 + n - 1:t0 + n]
                ts_(sp[2][:, t0:t0 + n], dq[0:32, t0:t0 + n], last_c, -1.0, ALU.subtract, ALU.mult)
            cs = sample_view(dq[0:32, TP:T])
            tt_(sample_view(sp[2][:, TP:T]), cs[:, :, DEC_L - 1:DEC_L].to_broadcast([HEADS, DEC_B, DEC_L]), cs,
                ALU.subtract).then_inc(s_sp, 1)
            dve.wait_ge(s_de, 2)
            link(dve.tensor_copy(sp[1][:], dq[32:64, :]))
            tt_(dq[96:128, :], sp[3][:], sp[1][:], ALU.mult)
            ends = [(N_META - 1, 1, 1), (N_META + P - 1, NC - 2, P), (TP + DEC_L - 1, DEC_B, DEC_L)]
            link(dve.tensor_copy(sp[0][:, 0:1], dq[64:96, N_META - 1:N_META]))
            dve.tensor_copy(sp[0][:, 1:NC - 1], dq[64:96, N_META + P - 1:TP:P])
            link(dve.tensor_copy(sp[0][:, NC - 1:NE], dq[64:96, TP + DEC_L - 1:T:DEC_L]))
            link(tt_(bde[:], ident[0:HEADS, 0:HEADS].unsqueeze(2).to_broadcast([HEADS, HEADS, NE]),
                     sp[0][:, 0:NE].unsqueeze(1).to_broadcast([HEADS, HEADS, NE]), ALU.mult))
            dve.memset(line_s[0][:, 0:HS], 0.0)
            dve.memset(line_s[1][:, 0:HS], 0.0)
            link(dve.memset(cm[:], 0.0))
            dve.sem_inc(s_ds, 1)
            dve.sem_inc(s_sp, 1)

            for j in range(CT):
                line, cv = line_s[j % 2], cv_s[j % 2]
                W = LS - HS
                dve.wait_ge(s_accf[(U_XBC + j) % 2], (U_XBC + j) // 2 + 1)
                if j >= 2:
                    dve.wait_ge(s_xbc, j - 1)
                link(ts_(cv[:, 0:W], line[:, 0:W], c_("cs", 4 * j), None, ALU.mult))
                link(stt(cv[:, 0:W], line[:, 1:W + 1], c_("cs", 4 * j + 1), cv[:, 0:W], ALU.mult, ALU.add))
                link(stt(cv[:, 0:W], line[:, 2:W + 2], c_("cs", 4 * j + 2), cv[:, 0:W], ALU.mult, ALU.add))
                dve.tensor_copy(news[:, j, 0, :], line[:, TP:HS + TP])
                dve.tensor_copy(news[:, j, 1:, :], sample_view(line[:, HS + TP:])[:, :, DEC_L:])
                stt(cv[:, 0:W], line[:, 3:W + 3], c_("cs", 4 * j + 3), cv[:, 0:W], ALU.mult, ALU.add).then_inc(s_cv, 1)

            def head_rows(s):
                t0, n = CHUNKS[s // GROUPS]
                h0 = s % GROUPS * HPG
                tt_(bd[:, :, 0:n], ident[0:HEADS, h0:h0 + HPG].unsqueeze(2).to_broadcast([HEADS, HPG, n]),
                    dq[0:HEADS, t0:t0 + n].unsqueeze(1).to_broadcast([HEADS, HPG, n]), ALU.mult)\
                    .then_inc(s_bd, 1)

            head_rows(0)
            dve.wait_ge(s_dTs, NC + 1)
            dve.wait_ge(s_xbc, CT)
            for c, (t0, n) in enumerate(CHUNKS):
                sample = c == NC - 1
                mask = smask[:].rearrange("p b r -> p (b r)") if sample else causal[0:n, 0:n]
                for g in range(GROUPS):
                    s = c * GROUPS + g
                    hs = slice(g * HPG, (g + 1) * HPG)

                    def per_head(i, w):
                        return dqT[0:n, c, i * 32 + g * HPG:i * 32 + (g + 1) * HPG].unsqueeze(2)\
                            .to_broadcast([n, HPG, w])

                    if sample:
                        dve.tensor_copy(cm[:, :, 0:DEC_L], sample_view(bc[:, GROUPS + g, TP:T]))
                    dve.wait_ge(s_pre, s + 1)
                    cq = ps[0:n, 5:7, 0:4 * n].rearrange("p a (h q) -> p a h q", h=4)
                    ck = dqT[0:n, c, g * HPG:(g + 1) * HPG].rearrange("p (a h) -> p a h", a=2)\
                        .unsqueeze(3).to_broadcast([n, 2, 4, n])
                    tt_(seg[0:n, :, 0:n].rearrange("p (a h) q -> p a h q", a=2), cq, ck, ALU.subtract)\
                        .then_inc(s_seg, 1)
                    tt_(cbm[0:n, 0:n], S0[0:n, 0:n], mask, ALU.mult)
                    xg = S3[0:n, :].rearrange("p (h w) -> p h w", h=HPG)
                    tt_(xdt[0:n, :].rearrange("p (h w) -> p h w", h=HPG), xg, per_head(1, HEADDIM), ALU.mult)
                    if sample:
                        tt_(bTm[:], S0[0:n, P:2 * P].unsqueeze(1).to_broadcast([n, DEC_B, P]),
                            rowmask[:].unsqueeze(2).to_broadcast([n, DEC_B, P]), ALU.mult)
                    else:
                        dve.tensor_copy(bT[0:n, :], S0[0:n, P:2 * P])
                    link(tt_(xde[0:n, :].rearrange("p (h w) -> p h w", h=HPG), xg, per_head(3, HEADDIM), ALU.mult))
                    dve.wait_ge(s_exp, s + 1)
                    tt_(wT[0:n, :, 0:n], seg[0:n, :, 0:n],
                        cbm[0:n, 0:n].unsqueeze(1).to_broadcast([n, HPG, n]), ALU.mult).then_inc(s_wT, 1)
                    if s + 1 < NC * GROUPS:
                        head_rows(s + 1)
                    dve.wait_ge(s_y, s + 1)
                    if c:
                        link(tt_(ysb[0:n, :].rearrange("p (h w) -> p h w", h=HPG),
                                 S2[0:n, :].rearrange("p (h w) -> p h w", h=HPG), per_head(2, HEADDIM), ALU.mult))
                        tt_(ysb[0:n, :], ysb[0:n, :], S1[0:n, :], ALU.add).then_inc(s_ysb, 1)
                    else:
                        dve.tensor_copy(ysb[0:n, :], S1[0:n, :]).then_inc(s_ysb, 1)

                    def decay(e):
                        return dend[:, hs, e:e + 1].to_broadcast([P, HPG, HEADDIM])

                    if sample:
                        for b in range(DEC_B):
                            pb = prev[:, b, :]
                            pv = pb.rearrange("p (h w) -> p h w", h=HPG)
                            link(tt_(pv, pv, decay(NC - 1 + b), ALU.mult))
                            dve.wait_ge(s_sst, g * DEC_B + b + 1)
                            tt_(pb, pb, (S3, S1)[b % 2], ALU.add).then_inc(s_snew, 1)
                        dve.wait_ge(s_snew, DEC_B * (g + 1))
                        dve.sem_inc(s_state, 1)
                    else:
                        st = state[:, g, :]
                        if c:
                            sv = st.rearrange("p (h w) -> p h w", h=HPG)
                            link(tt_(sv, sv, decay(c), ALU.mult))
                            dve.wait_ge(s_st, s + 1)
                            tt_(st, st, S3, ALU.add).then_inc(s_state, 1)
                        else:
                            dve.wait_ge(s_st, s + 1)
                            dve.tensor_copy(st, S3).then_inc(s_state, 1)
                    dve.wait_ge(s_yT, s + 1)
                    for j in range(4):
                        xj = xs[:, 4 * g + j, t0:t0 + n]
                        last = stt(xj, xj, c_("dd", 4 * g + j), S0[:, j * n:(j + 1) * n], ALU.mult, ALU.add)
                    last.then_inc(s_y2, 1)

            dve.wait_ge(s_y2, NC * GROUPS)
            dve.memset(line_a[:, 0:HA], 0.0)
            for i in range(KT):
                W = LA - HA
                dve.tensor_copy(sample_view(line_a[:, HA + TP:])[:, :, 0:HA], hista[:, i])
                C, X, B = (cxb[i % 2][:, a, :] for a in range(3))
                dve.wait_ge(s_cxb[i % 2], 16 * (i // 2 + 1))
                tt_(line_a[:, HA:HA + TP], C[:, 0:TP], X[:, 0:TP], ALU.mult)
                link(tt_(sample_view(line_a[:, HA + TP:])[:, :, HA:], sample_view(C[:, TP:]),
                         sample_view(X[:, TP:]), ALU.mult))
                link(ts_(cv_a[:, 0:W], line_a[:, 0:W], c_("ca", 3 * i), None, ALU.mult))
                link(stt(cv_a[:, 0:W], line_a[:, 1:W + 1], c_("ca", 3 * i + 1), cv_a[:, 0:W], ALU.mult, ALU.add))
                link(stt(cv_a[:, 0:W], line_a[:, 2:W + 2], c_("ca", 3 * i + 2), cv_a[:, 0:W], ALU.mult, ALU.add))
                dve.tensor_copy(newa[:, i, 0, :], line_a[:, TP:HA + TP])
                dve.tensor_copy(newa[:, i, 1:, :], sample_view(line_a[:, HA + TP:])[:, :, DEC_L:])
                tt_(v_f[:, 0:TP], B[:, 0:TP], cv_a[:, 0:TP], ALU.mult)
                tt_(sample_view(v_f[:, TP:]), sample_view(B[:, TP:]), line_out(cv_a, HA), ALU.mult)\
                    .then_inc(s_vf, 1)
                dve.wait_ge(s_vhi, i + 1)
                tt_(v_lo[:, i, :], v_f[:], v_hi[:, i, :].bitcast(F32), ALU.subtract).then_inc(s_v, 1)

            def gate_group(g):
                dve.wait_ge(s_zl[g % 2], 16 * (g // 2 + 1))
                for j in range(4):
                    tt_(xs[:, 4 * g + j, :], xs[:, 4 * g + j, :], zb[g % 2][:, j, :], ALU.mult).then_inc(s_gz, 1)

            def branch_a_out(i):
                dve.wait_ge(s_unit, U_AO + i + 1)
                tt_(halves(ma[:, i, :]), halves(ma[:, i, :]), acc[(U_AO + i) % 2], ALU.mult)\
                    .then_inc(s_accf[(U_AO + i) % 2], 1)

            gate_group(0)
            for g in range(GROUPS):
                branch_a_out(2 * g)
                rsqrt(1.0 / GW, KT + 4 * g + 4, 2 + g, (lambda: gate_group(g + 1)) if g + 1 < GROUPS else None)
                for j in range(4 * g, 4 * g + 4):
                    if j > 4 * g + 1:
                        dve.wait_ge(s_n, j - 1)
                    stt(hf[j % 2][:], xs[:, j, :], c_("sn", j), inv[:], ALU.mult, ALU.mult).then_inc(s_nf, 1)
                    dve.wait_ge(s_nhi, j + 1)
                    tt_(n_lo[:, j, :], hf[j % 2][:], n_hi[:, j, :].bitcast(F32), ALU.subtract).then_inc(s_n, 1)
                    if j == 4 * g + 1:
                        branch_a_out(2 * g + 1)

            for j in range(KT):
                L = U_SO + j
                if j % 4 == 0:
                    dve.wait_ge(s_gbl[j // 4], 16)
                dve.wait_ge(s_unit, U_SO + 2 * j + 2)
                link(tt_(halves(mt[j % 2][:]), acc[L % 2], halves(sgb[:, j, :]), ALU.mult))
                dve.sem_inc(s_accf[L % 2], 1)
                tt_(ma[:, j, :], ma[:, j, :], mt[j % 2][:], ALU.add).then_inc(s_mf, 1)
                dve.wait_ge(s_mhi, j + 1)
                tt_(m_lo[:, j, :], ma[:, j, :], m_hi[:, j, :].bitcast(F32), ALU.subtract).then_inc(s_m, 1)
            dve.wait_ge(s_xr, 16)
            for j in range(KT):
                L = L_WO + j
                dve.wait_ge(s_unit, U_WO + j + 1)
                link(tt_(halves(x[:, j, :]), halves(x[:, j, :]), acc[L % 2], ALU.add))
                dve.sem_inc(s_accf[L % 2], 1)
                dve.sem_inc(s_x1, 1)
            rsqrt(1.0 / D, 2 * KT + XT, 2 + GROUPS)
            normed(1, "ffn", g_lo, g_hi)

            def top16(vals, idx, src, src2, rows):
                for i in range(rows):
                    last = dve.max(vals[:, i, 0:8], src[:, i, :])
                link(last)
                for i in range(rows):
                    dve.max_index(idx[:, i, 0:8], vals[:, i, 0:8], src[:, i, :])
                    last = dve.match_replace(src2[:, i, :], vals[:, i, 0:8], src[:, i, :], LOWEST)
                link(last)
                for i in range(rows):
                    last = dve.max(vals[:, i, 8:16], src2[:, i, :])
                link(last)
                for i in range(rows):
                    last = dve.max_index(idx[:, i, 8:16], vals[:, i, 8:16], src2[:, i, :])
                link(last)

            for tt, (t0, n) in enumerate(TT):
                dve.wait_ge(s_scs, tt + 1)
                top16(top[0:n], topi[0:n], sc[0:n], sc2[0:n], 2 * PH)
                dve.sem_inc(s_scf, 1)
                pair = top[0:n].rearrange("p (h i) k -> p h i k", i=2)
                shape = [n, PH, TOPK, TOPK]
                link(tt_(cand[0:n].rearrange("p h (j k) -> p h j k", j=TOPK),
                         pair[:, :, 0, :].unsqueeze(3).to_broadcast(shape),
                         pair[:, :, 1, :].unsqueeze(2).to_broadcast(shape), ALU.add))
                top16(best[0:n], besti[0:n].rearrange("p (h k) -> p h k", h=PH), cand[0:n], cand2[0:n], PH)
                link(dve.tensor_copy(sm[0:n, 0, :], best[0:n, :, 0]))
                tt_(best[0:n], best[0:n], sm[0:n, 0, :].unsqueeze(2).to_broadcast([n, PH, TOPK]),
                    ALU.subtract).then_inc(s_be, 1)
                ts_(bsel[0:n, 0, :], besti[0:n], 4, None, ALU.logical_shift_right)
                ts_(bsel[0:n, 1, :], besti[0:n], 15, None, ALU.bitwise_and)
                link(dve.tensor_copy(topf[0:n], topi[0:n]))
                link(dve.tensor_copy(bself[0:n], bsel[0:n]))
                keyf = topf[0:n].rearrange("p (h i) k -> p h i k", i=2)
                for i, eq in enumerate((cand, cand2)):
                    e3 = eq[0:n].rearrange("p h (k j) -> p (h k) j", j=TOPK)
                    tt_(e3, bself[0:n, i, :].unsqueeze(2).to_broadcast([n, PH * TOPK, TOPK]),
                        iota[0:n, 0:TOPK].unsqueeze(1).to_broadcast([n, PH * TOPK, TOPK]), ALU.is_equal)\
                        .then_inc(s_dc, 1)
                    chain[0] += 1
                dve.wait_ge(s_dc, chain[0])
                for i, eq in enumerate((cand, cand2)):
                    e4 = eq[0:n].rearrange("p h (k j) -> p h k j", j=TOPK)
                    tt_(e4, e4, keyf[:, :, i, :].unsqueeze(2).to_broadcast(shape), ALU.mult).then_inc(s_dc, 1)
                    chain[0] += 1
                dve.wait_ge(s_dc, chain[0])
                if tt:
                    dve.wait_ge(s_pkT, tt)
                for i, eq in enumerate((cand, cand2)):
                    dve.tensor_reduce(pick[0:n, i, :], eq[0:n].rearrange("p h (k j) -> p (h k) j", j=TOPK),
                                      AX.X, ALU.add)
                dve.wait_ge(s_bx, tt + 1)
                link(dve.tensor_reduce(sm[0:n, 0, :], best[0:n], AX.X, ALU.add))
                link(dve.reciprocal(sm[0:n, 1, :], sm[0:n, 0, :]))
                tt_(pick[0:n, 2, :].rearrange("p (h k) -> p h k", h=PH), best[0:n],
                    sm[0:n, 1, :].unsqueeze(2).to_broadcast([n, PH, TOPK]), ALU.mult).then_inc(s_pk, 1)

            def one_hots(b, par, first, t):
                if not first:
                    dve.wait_ge(s_gm, b - 1)
                tt_(oh_2[:, par], iota[:].unsqueeze(1).to_broadcast([P, TB, P]),
                    pickT[:, 1, t(0, TB)].unsqueeze(2).to_broadcast([P, TB, P]), ALU.is_equal)
                for j in range(TB):
                    last = ts_(oh_g[:, par, j, :], iota[:], pickT[:, 0, t(j, 1)], pickT[:, 2, t(j, 1)],
                               ALU.is_equal, ALU.mult)
                last.then_inc(s_oh, 1)

            dve.wait_ge(s_pks, len(TT))
            for b in range(2):
                one_hots(b, b, True, lambda j, w: slice(b * TB + j, b * TB + j + w))
            with dve.Fori(1, NB // 2) as i:
                for par in range(2):
                    one_hots(i * 2 + par, par, False, lambda j, w: bass.ds(i * 2 * TB + (par * TB + j), w))
            for b in range(NB // 2 * 2, NB):
                one_hots(b, b % 2, False, lambda j, w: slice(b * TB + j, b * TB + j + w))

            L0 = U_PEER - L_SHIFT + NKEYS

            def group(g, par, add):
                for u in range(GI):
                    a = abuf[:, u // 4, u % 4, :]
                    if u % 4 == 0:
                        dve.wait_ge(s_al[u // 4], g * 16 + 16)
                        dve.wait_ge(s_gl[u // 4], g * 16 + 16)
                    v = a.rearrange("p (n t) -> p n t", t=TB)
                    tt_(v, v, gbuf[:, u // 4, :, u % 4, :], ALU.mult).then_inc(s_pm, 1)
                    if add:
                        add_tile(g - 1, u)
                    dve.wait_ge(s_phi, g * GI + u + 1)
                    tt_(p_lo[par][:, u, :], a, p_hi[par][:, u, :].bitcast(F32), ALU.subtract).then_inc(s_p, 1)

            def add_tile(g, u):
                p_ = (L0 + u) % 2
                dve.wait_ge(s_unit, g * KT + (U_PEER + NKEYS + u + 1))
                tt_(halves(x[:, u, :]), halves(x[:, u, :]), acc[p_], ALU.add).then_inc(s_x2, 1)
                dve.wait_ge(s_x2, g * KT + u + 1)
                dve.sem_inc(s_accf[p_], 1)

            group(0, 0, False)
            group(1, 1, True)
            with dve.Fori(1, NG // 2) as i:
                group(i * 2, 0, True)
                group(i * 2 + 1, 1, True)
            for u in range(KT):
                add_tile(NG - 1, u)

            rsqrt(1.0 / D, 3 * KT + XT, 3 + GROUPS)
            for k in range(KT):
                if k >= 2:
                    dve.wait_ge(s_yd[k % 2], 16 * (k // 2))
                stt(yo[k % 2][:], x[:, k, :], c_("fin", k), inv[:], ALU.mult, ALU.mult).then_inc(s_yo, 1)


def inputs_of(x_prompt, x_sample, state_conv_a, state_conv_ssd, state_ssm, meta_tokens, norm_mix_w, w_in,
              conv_a_w, w_a_out, ssd_conv_w, ssd_conv_b, ssd_dt_bias, ssd_a_log, ssd_d, ssd_norm_w,
              w_ssd_out, w_o, norm_ffn_w, peer_w_q, peer_sub_keys, peer_u, peer_v, norm_final_w):
    import numpy as np
    A = lambda a: np.asarray(a)
    tokens = np.concatenate([A(meta_tokens), A(x_prompt)[0], A(x_sample).reshape(TS, D)], 0)
    xT = np.ascontiguousarray(tokens.reshape(T, KT, P).transpose(2, 1, 0))

    def tiles(w):
        return w.reshape(KT, P, -1, P).transpose(2, 1, 0, 3).reshape(-1, P, D)

    wi = A(w_in)[0]
    o = np.cumsum([0, D, D, D, 2 * D, CT * P, HEADS, D, D])
    aB, aC, aX, z, xbc, dt, ga, gb = (wi[:, o[i]:o[i + 1]] for i in range(8))
    dt_p = np.zeros((D, P), wi.dtype)
    dt_p[:, :HEADS] = dt
    units = np.empty((UNITS, P, D), wi.dtype)
    units[U_DT:U_XBC] = tiles(dt_p)
    units[U_XBC:U_A] = tiles(xbc)
    for i, w in enumerate((aC, aX, aB)):
        units[U_A + i:U_Z:3] = tiles(w)
    units[U_AO:U_SO] = tiles(A(w_a_out)[0])
    units[U_GA:U_AO] = tiles(ga)
    units[U_GB:U_GA] = tiles(gb)
    units[U_Z:U_GB] = tiles(z)
    so = A(w_ssd_out)[0].reshape(2, KT, P, KT, P).transpose(3, 0, 2, 1, 4).reshape(2 * KT, P, D)
    units[U_SO:U_WO] = so
    units[U_WO:U_WQ] = tiles(A(w_o)[0])
    units[U_WQ:U_PEER] = tiles(A(peer_w_q)[0])
    uu = A(peer_u)[0].reshape(NKEYS, NKEYS, KT, P).transpose(1, 3, 2, 0).reshape(NG, GI, P, D)
    vv = A(peer_v)[0].reshape(NKEYS, NG, GI, KT, P).transpose(1, 3, 0, 2, 4).reshape(NG, KT, P, D)
    e = units[U_PEER:].reshape(2 * NG, GI, P, D)
    e[:NG], e[NG:] = uu, vv
    keys = np.ascontiguousarray(A(peer_sub_keys)[0].transpose(3, 0, 1, 2).reshape(P, 2 * PH, NKEYS))
    colp = lambda a: A(a).reshape(-1, P).T
    cols = np.ascontiguousarray(np.concatenate([
        colp(norm_mix_w), colp(norm_ffn_w), colp(norm_final_w),
        A(conv_a_w)[0].reshape(3, KT, P).transpose(2, 1, 0).reshape(P, 3 * KT),
        A(ssd_conv_w)[0].reshape(4, CT, P).transpose(2, 1, 0).reshape(P, 4 * CT),
        colp(ssd_conv_b), colp(ssd_norm_w), colp(np.repeat(A(ssd_d)[0], HEADDIM))], 1))
    heads = np.ascontiguousarray(np.stack([A(ssd_dt_bias)[0], A(ssd_a_log)[0]], 1))
    hist = lambda a, n: np.ascontiguousarray(A(a)[0].reshape(DEC_B, -1, n, P).transpose(3, 2, 0, 1))
    ssm = np.ascontiguousarray(A(state_ssm)[0].reshape(DEC_B, GROUPS, GW, STATE).transpose(3, 1, 0, 2))
    return dict(xT=xT, units=units, keys=keys, cols=cols, heads=heads, hist_a=hist(state_conv_a, KT),
                hist_s=hist(state_conv_ssd, CT), ssm_in=ssm)


OUTS = dict(yT=(P, KT, T), new_a=(P, KT, 1 + DEC_B, HA), new_s=(P, CT, 1 + DEC_B, HS),
            ssm_p=(P, GROUPS, GW), ssm_s=(P, GROUPS, DEC_B, GW))


def outputs_of(yT, new_a, new_s, ssm_p, ssm_s):
    import numpy as np
    y = yT.transpose(2, 1, 0).reshape(T, D)
    conv = lambda a: np.ascontiguousarray(a.transpose(2, 3, 1, 0)).reshape(1, 1 + DEC_B, a.shape[3], -1)
    na, ns = conv(new_a), conv(new_s)
    sp = ssm_p.transpose(1, 2, 0).reshape(1, 1, HEADS, HEADDIM, STATE)
    ss = ssm_s.transpose(2, 1, 3, 0).reshape(1, DEC_B, HEADS, HEADDIM, STATE)
    c = np.ascontiguousarray
    return (c(y[N_META:TP])[None], c(y[TP:]).reshape(DEC_B, DEC_L, D), c(na[:, :1]), c(ns[:, :1]), c(sp),
            c(na[:, 1:]), c(ns[:, 1:]), c(ss))


def kernel(**inputs):
    import numpy as np
    import concourse.bacc as bacc
    from concourse.bass_utils import run_bass_kernel_spmd

    nc = bacc.Bacc("TRN2", target_bir_lowering=False, num_devices=1)
    arrays = inputs_of(**inputs)
    args = [nc.dram_tensor(k, a.shape, mybir.dt.from_np(a.dtype), kind="ExternalInput").ap()
            for k, a in arrays.items()]
    args += [nc.dram_tensor(k, s, F32, kind="ExternalOutput").ap() for k, s in OUTS.items()]
    trunk(nc, *args)
    r = run_bass_kernel_spmd(nc, [arrays], core_ids=[0])
    return outputs_of(**{k: r.results[0][k] for k in OUTS})
```

```python
from contextlib import ExitStack

import concourse.bass as bass
from concourse import mybir

ALU = mybir.AluOpType
ACT = mybir.ActivationFunctionType
AX = mybir.AxisListType
F32 = mybir.dt.float32
F32R = mybir.dt.float32r
BF16 = mybir.dt.bfloat16
U32 = mybir.dt.uint32

P = 128
D = 1024
KT = D // P
N_META, SEQ = 16, 512
DEC_B, DEC_L = 8, 8
TP = N_META + SEQ
TS = DEC_B * DEC_L
T = TP + TS
HF = T // 2
HP = TP - HF
TK = T - N_META
HK = TK // 2
EPS = 1e-6
HEADS, HEADDIM, STATE = 32, 64, 128
GROUPS, HPG = 4, 8
GW = HPG * HEADDIM
XT = 2 * D // P
CT = XT + 2 * GROUPS
HA, HS = 2, 3
LA = HA + TP + DEC_B * (HA + DEC_L)
LS = HS + TP + DEC_B * (HS + DEC_L)
CHUNKS = [(0, N_META)] + [(N_META + P * c, P) for c in range(SEQ // P)] + [(TP, TS)]
NC = len(CHUNKS)
PH, NKEYS, TOPK = 8, 128, 16
TT = [(t, min(P, TK - t)) for t in range(0, TK, P)]
TB = 16
NB = TK // TB
GI = 8
NG = NKEYS // GI
LOWEST = -3.0e38
NT = 8
NQ = T // NT
M_TOP = 8 * len(TT) + 4
M_GATE = M_TOP + 2 * NB

N_DT, N_XBC, N_A, N_Z, N_GB, N_GA, N_AO, N_SO, N_WO, N_WQ = 1, CT, 3 * KT, XT, KT, KT, KT, 2 * KT, KT, 2 * KT
N_PARK = N_A + N_Z + N_GB
N_PRE = 4
U_DT = 0
U_PRE = U_DT + N_DT
U_XBC = U_PRE + N_PRE
U_PARK = U_XBC + N_XBC
U_GA = U_PARK + N_PARK - N_PRE
U_AO = U_GA + N_GA
U_SO = U_AO + N_AO
U_WO = U_SO + N_SO
U_WQ = U_WO + N_WO
U_PEER = U_WQ + N_WQ
UNITS = U_PEER + 2 * NKEYS
PARKED = [*range(U_PRE, U_XBC), *range(U_PARK, U_GA)]
L_WO = U_SO + KT
L_SHIFT = U_WO - L_WO
TURN0 = 4
RAW = 4
COLS = dict(mix=0, ffn=8, fin=16, ca=24, cs=48, cb=144, sn=168, dd=184)
NCOLS = 200


def trunk(nc, xT, units, keys, cols, heads, hist_a, hist_s, ssm_in,
          yT, new_a, new_s, ssm_p, ssm_s):
    gate_dram = nc.dram_tensor("gate_scratch", [2 * NG, P, NB, GI // 2 * TB], F32).ap()
    spill = nc.dram_tensor("parked_tiles", [N_PARK, P, T], F32).ap()
    act_dram = nc.dram_tensor("activation_scratch", [NKEYS, P, TK], F32).ap()
    base = ((nc.sbuf_base + 63) // 64) * 64
    end = nc.sbuf_usable_end
    with ExitStack() as ctx:
        def at(name, off, shape, dt=F32):
            n = 4
            for s in shape[1:]:
                n *= s
            assert base + off + n <= end, (name, off + n, end - base)
            return nc.alloc_sbuf_tensor_at(name, shape, dt, offset=base + off)

        def sem(name):
            return ctx.enter_context(nc.semaphore(name))

        TW = 4 * T
        LSB, LAB = ((4 * w + 31) // 32 * 32 for w in (LS, LA))

        def stack(start):
            pos = [start]

            def put(name, shape, dt=F32):
                n = 4
                for s in shape[1:]:
                    n *= s
                r = at(name, pos[0], shape, dt)
                pos[0] += (n + 31) // 32 * 32
                return r
            return put, pos

        const, pos = stack(0)
        ident = const("ident", [P, P])
        causal = const("causal", [P, P])
        smask = const("smask", [TS, DEC_B, DEC_L])
        rowmask = const("rowmask", [TS, DEC_B])
        iota_i = const("iota_i", [P, P], mybir.dt.int32)
        iota = const("iota", [P, P])
        ones_r = const("ones", [P, P], F32R)
        ones = ones_r[:].bitcast(F32)
        fold = const("fold", [2 * HEADS, HEADS])
        col = const("col", [P, NCOLS])
        hd = const("hd", [HEADS, 4])
        hista = const("hista", [P, KT, DEC_B, HA])
        hists = const("hists", [P, CT, DEC_B, HS])
        newa = const("newa", [P, KT, 1 + DEC_B, HA])
        news = const("news", [P, CT, 1 + DEC_B, HS])
        R_HT = pos[0]
        R_RING = R_HT + 2 * KT * TW
        R_XS = R_RING + (RAW + 4) * 4 * D
        R1 = R_XS + XT * TW
        R_TMP = R1 + 2 * KT * TW
        R_X = R_TMP + 18400
        R_MA = R_X + KT * TW
        h_hi = at("h_hi", R_HT, [P, KT, T], F32R)
        h_lo = at("h_lo", R_HT + KT * TW, [P, KT, T], F32R)
        m_hi = at("m_hi", R1, [P, KT, TK], F32R)
        m_lo = at("m_lo", R1 + KT * TW, [P, KT, TK], F32R)
        g_hi = at("g_hi", R_HT, [P, KT, TK], F32R)
        g_lo = at("g_lo", R_HT + KT * TW, [P, KT, TK], F32R)
        raw = at("raw", R_RING, [P, RAW, D])
        w_hi = at("w_hi", R_RING + RAW * 4 * D, [P, 2, D], F32R)
        w_lo = at("w_lo", R_RING + (RAW + 2) * 4 * D, [P, 2, D], F32R)
        x = at("x", R_X, [P, KT, T])
        xs = at("xs", R_XS, [P, XT, T])
        bc = at("bc", R1, [P, 2 * GROUPS, T])
        tmp = [at(f"tmp{i}", R_TMP + i * TW, [P, T]) for i in range(7)]
        sq, hf = tmp[0:2], tmp[2:4]
        sqa = tmp[2]
        sums_row = tmp[4]
        root = at("root", R_TMP + 5 * TW, [NQ, 3, NT])
        spread = at("spread", R_TMP + 6 * TW, [NQ, T])
        R_C = R1 + 2 * GROUPS * TW
        line_s = [at(f"line_s{i}", R_C + i * LSB, [P, LS]) for i in range(2)]
        cv_s = [at(f"cv_s{i}", R_C + (2 + i) * LSB, [P, LS]) for i in range(2)]
        scr, spos = stack(R_C + 4 * LSB)
        dq = scr("dq", [P, T])
        sp = [at(f"sp{i}", R_C + i * TW, [HEADS, T]) for i in range(4)]
        reset = scr("reset", [HEADS, T])
        cum2 = at("cum2", spos[0] - TW, [2 * HEADS, T], F32R)
        dqT = scr("dqT", [P, NC, P])
        NE = NC - 1 + DEC_B
        bde = scr("bde", [HEADS, HEADS, NE])
        dend = scr("dend", [P, HEADS, NE])
        prev = scr("prev", [P, 3, DEC_B // 2, GW])
        wT = scr("wT", [P, HPG, P])
        xdt = scr("xdt", [P, GW])
        xde = scr("xde", [P, GW])
        ysb = scr("ysb", [P, GW])
        state = scr("state", [P, GROUPS, GW])
        bTm = scr("bTm", [TS, DEC_B, P])
        cm = scr("cm", [P, DEC_B, TS + DEC_L])
        seg = at("seg", R_C, [P, HPG, P])
        bd = at("bd", R_C + 4 * HPG * P, [2 * HEADS, HPG, P], F32R)
        bT = at("bT", R_C + 8 * HPG * P, [P, P])
        cbm = at("cbm", R_C + 8 * HPG * P + 4 * P, [P, P])
        stage = [scr(f"stage{i}", [P, T]) for i in range(2)]
        v_hi = at("v_hi", R1, [P, KT, T], F32R)
        v_lo = at("v_lo", R1 + KT * TW, [P, KT, T], F32R)
        line_a = at("line_a", R_TMP, [P, LA])
        cv_a = at("cv_a", R_TMP + LAB, [P, LA])
        v_f = [at(f"v_f{i}", R_TMP + 2 * LAB + i * TW, [P, T]) for i in range(2)]
        cxb = [at("cxb0", R_X + 4 * TW, [P, 3, T]), at("cxb1", R_X - 3 * TW, [P, 3, T])]
        ma = at("ma", R_MA, [P, KT, TK])
        sgb = at("sgb", R_X, [P, KT, TK])
        n_hi = at("n_hi", R_XS, [P, XT, T], F32R)
        zb = [at(f"zb{i}", R_X + 4 * i * TW, [P, 4, TK]) for i in range(2)]
        n_lo = at("n_lo", R_HT, [P, XT, T], F32R)
        sqg = [at(f"sqg{i}", R_HT + (XT - 4 + i) * TW, [P, TK]) for i in range(4)]
        mt = [at(f"mt{i}", R_TMP + i * TW, [P, TK]) for i in range(2)]
        q = at("q", R_XS, [P, 2 * PH, TK])
        tk, tpos = stack(R1)
        sc = tk("sc", [P, 2 * PH, NKEYS])
        sc2 = tk("sc2", [P, 2 * PH, NKEYS])
        cand = tk("cand", [P, PH, TOPK * TOPK])
        cand2 = tk("cand2", [P, PH, TOPK * TOPK])
        key_sb = tk("key_sb", [P, 2 * PH, NKEYS])
        top = tk("top", [P, 2 * PH, TOPK])
        topi = tk("topi", [P, 2 * PH, TOPK], U32)
        topf = tk("topf", [P, 2 * PH, TOPK])
        best = tk("best", [P, PH, TOPK])
        besti = tk("besti", [P, PH * TOPK], U32)
        bsel = tk("bsel", [P, 2, PH * TOPK], U32)
        bself = tk("bself", [P, 2, PH * TOPK])
        sm = tk("sm", [P, 2, PH])
        pick = tk("pick", [P, 3, PH * TOPK])
        pickT = at("pickT", R_MA, [P, 3, TK])
        oh_g = at("oh_g", R_XS, [P, 2, 3, TB, P], BF16)
        oh_2 = at("oh_2", R_XS + 12 * TB * P, [P, 2, TB, P], BF16)
        wpart = at("wpart", R_MA + 5 * TW, [P, 3, TK])
        wb = tk("wb", [P, 3, P], BF16)
        assert tpos[0] <= R_X
        iota_b = at("iota_b", R_XS + 16 * TB * P, [P, P], BF16)
        gt = at("gt", R_TMP, [P, 2, NKEYS, TB])
        ge = [at(f"ge{i}", R_MA + 3 * TW + i * TW, [P, TK]) for i in range(2)]
        p_hi = [at("p_hi0", R1, [P, GI, TK], F32R), at("p_hi1", R_HT, [P, GI, TK], F32R)]
        p_lo = [at("p_lo0", R1 + GI * TW, [P, GI, TK], F32R), at("p_lo1", R_HT + GI * TW, [P, GI, TK], F32R)]
        abuf = at("abuf", R_XS, [P, 2, GI // 2, TK])
        gbuf = at("gbuf", R_XS + GI * TW, [P, 2, NB, GI // 2, TB])
        yo = [at(f"yo{i}", R_XS + i * TW, [P, TK]) for i in range(2)]

        ps = ctx.enter_context(nc.psum_tensor("ps", [P, 8, 512], F32))
        acc = [ps[:, 0:2, 0:HF], ps[:, 2:4, 0:HF]]
        acck = [ps[:, 0:2, 0:HK], ps[:, 2:4, 0:HK]]
        ssp = ps[:, 4:6, 0:HF]
        inv = ps[:, 6:8, 0:HF]
        turned = ps[0:NQ, 7, 400:400 + NT]
        S3, S0, S1, S2 = (ps[:, 4 + i, :] for i in range(4))

        pair_banks = [ps[:, 6:8, :], ps[:, 4:6, :]]

        ld = [sem(f"unit_loaded{i}") for i in range(RAW)]
        s_wbeg = sem("split_begun")
        s_whi = sem("weights_hi")
        s_w = sem("weights_split")
        s_unit = sem("unit_used")
        s_accf = [sem("acc0_read"), sem("acc1_read")]
        s_x = [sem(f"x_loaded{i}") for i in range(4)]
        s_in = sem("small_inputs_loaded")
        s_c = sem("constants_made")
        s_pc = sem("pool_chain")
        s_dc = sem("vector_chain")
        s_ac = sem("scalar_chain")
        s_sq = sem("squares_ready")
        s_sqa = sem("squares_added")
        s_ss = sem("squares_summed")
        s_var = sem("mean_squares_ready")
        s_turn = sem("mean_squares_turned")
        s_vt = sem("mean_squares_copied")
        s_std = sem("deviation_ready")
        s_diag = sem("diagonals_ready")
        s_inv = sem("inverse_spread")
        s_hf = sem("normed_ready")
        s_hhi = sem("normed_hi")
        s_h = sem("normed_split")
        s_cv = sem("conv_done")
        s_xbc = sem("xbc_ready")
        s_sp = sem("dt_for_exp")
        s_spe = sem("dt_exp_done")
        s_ds = sem("decays_ready")
        s_de = sem("decay_exp_done")
        s_dT = sem("decays_transposed")
        s_dTs = sem("decays_copied")
        s_bd = sem("head_rows_ready")
        s_pre = sem("chunk_products")
        s_seg = sem("segments_ready")
        s_exp = sem("segments_exp")
        s_wT = sem("mix_weights_ready")
        s_y = sem("chunk_outputs")
        s_ysb = sem("chunk_output_ready")
        s_st = sem("chunk_states")
        s_state = sem("state_updated")
        s_yT = sem("output_turned")
        s_y2 = sem("output_merged")
        s_pl = [sem(f"sample_states_loaded{i}") for i in range(3)]
        s_sst = sem("sample_state_product")
        s_snew = sem("sample_state_updated")
        s_po = [sem(f"sample_states_stored{i}") for i in range(3)]
        s_parked = [sem("parked0"), sem("parked1")]
        s_cxb = [sem("cxb_loaded0"), sem("cxb_loaded1")]
        s_zl = [sem("silu_z_loaded0"), sem("silu_z_loaded1")]
        s_gbl = [sem("gate_b_loaded0"), sem("gate_b_loaded1")]
        s_vf = sem("v_ready")
        s_vhi = sem("v_hi_ready")
        s_v = sem("v_split")
        s_gz = sem("gated_ready")
        s_nf = sem("group_normed_ready")
        s_nhi = sem("group_normed_hi")
        s_n = sem("group_normed_split")
        s_mf = sem("merge_ready")
        s_mhi = sem("merge_hi")
        s_m = sem("merge_split")
        s_xr = sem("x_reloaded")
        s_x1 = sem("x_after_mixer")
        s_q = sem("queries_ready")
        s_key = sem("keys_loaded")
        s_sc = sem("scores_ready")
        s_scs = sem("scores_copied")
        s_be = sem("softmax_shifted")
        s_bx = sem("softmax_exp")
        s_pk = sem("picks_ready")
        s_pkT = sem("picks_turned")
        s_pks = sem("picks_copied")
        s_oh = sem("one_hots_ready")
        s_gm = sem("gates_built")
        s_gt = sem("gates_copied")
        s_gs = [sem("gates_stored0"), sem("gates_stored1")]
        s_gl = [sem("gates_loaded0"), sem("gates_loaded1")]
        s_al = [sem("activations_loaded0"), sem("activations_loaded1")]
        s_as = [sem("activations_stored0"), sem("activations_stored1")]
        s_scf = sem("scores_read")
        s_pm = sem("expert_gated")
        s_phi = sem("expert_hi")
        s_p = sem("expert_split")
        s_x2 = sem("x_after_experts")
        s_yo = sem("y_ready")
        s_yd = [sem("y_stored0"), sem("y_stored1")]
        s_out = sem("states_stored")

        block = ctx.enter_context(nc.Block())

        def halves(a):
            return a.rearrange("p (a t) -> p a t", a=2)

        def squares_of(i):
            if KT <= i < KT + XT:
                return sqg[i % 4][:]
            return sq[i % 2][:, 0:T if i < KT else TK]

        def kept(a):
            return a[:, N_META:]

        def pieces(a, line, h):
            tail = line[:, h + TP:].rearrange("p (b r) -> p b r", b=DEC_B)
            return [(a[:, 0, :], line[:, h:h + HF]), (a[:, 1, 0:HP], line[:, h + HF:h + TP]),
                    (a[:, 1, HP:HF].rearrange("p (b r) -> p b r", b=DEC_B), tail[:, :, h:])]

        def sample_view(a):
            return a.rearrange("p (b r) -> p b r", b=DEC_B)

        def line_out(cv, h):
            return sample_view(cv[:, h + TP:])[:, :, 0:DEC_L]

        def c_(name, i):
            return col[:, COLS[name] + i:COLS[name] + i + 1]

        @block.sync
        def _(sp_):
            for i in range(4):
                sp_.dma_start(x[:, 2 * i:2 * i + 2], xT[:, 2 * i:2 * i + 2]).then_inc(s_x[i], 16)
            sp_.dma_start(col[:], cols).then_inc(s_in, 16)
            sp_.dma_start(hd[:, 0:2], heads).then_inc(s_in, 16)
            sp_.dma_start(hista[:], hist_a).then_inc(s_in, 16)
            sp_.dma_start(hists[:], hist_s).then_inc(s_in, 16)
            for n in range(RAW):
                sp_.dma_start(raw[:, n, :], units[n]).then_inc(ld[n], 16)

            def stream(n, r):
                sp_.wait_ge(s_w, n - RAW + 1)
                sp_.dma_start(raw[:, r, :], units[bass.ds(n, 1)].rearrange("a p k -> (a p) k")).then_inc(ld[r], 16)

            with sp_.Fori(1, UNITS // RAW) as i:
                for r in range(RAW):
                    stream(i * RAW + r, r)
            for n in range(UNITS // RAW * RAW, UNITS):
                sp_.wait_ge(s_w, n - RAW + 1)
                sp_.dma_start(raw[:, n % RAW, :], units[n]).then_inc(ld[n % RAW], 16)

        @block.gpsimd
        def _(pool):
            chain = [0]

            def link(ins):
                chain[0] += 1
                ins.then_inc(s_pc, 1)
                pool.wait_ge(s_pc, chain[0])

            pool.memset(ones, 1.0)
            pool.memset(ident[:], 0.0)
            pool.memset(causal[:], 1.0)
            pool.memset(smask[:], 1.0)
            pool.iota(iota_i[:], [[1, P]], base=0, channel_multiplier=0)
            link(pool.memset(rowmask[:], 1.0))
            pool.affine_select(out=ident[:], in_=ident[:], compare_op=ALU.not_equal, fill=1.0, base=0,
                               pattern=[[-1, P]], channel_multiplier=1)
            pool.affine_select(out=causal[:], in_=causal[:], compare_op=ALU.is_ge, fill=0.0, base=0,
                               pattern=[[1, P]], channel_multiplier=-1)
            pool.affine_select(out=smask[:], in_=smask[:], compare_op=ALU.is_ge, fill=0.0, base=0,
                               pattern=[[DEC_L, DEC_B], [1, DEC_L]], channel_multiplier=-1)
            link(pool.affine_select(out=rowmask[:], in_=rowmask[:], compare_op=ALU.is_ge, fill=0.0, base=0,
                                    pattern=[[-DEC_L, DEC_B]], channel_multiplier=1))
            pool.affine_select(out=smask[:], in_=smask[:], compare_op=ALU.is_ge, fill=0.0, base=0,
                               pattern=[[-DEC_L, DEC_B], [0, DEC_L]], channel_multiplier=1)
            pool.tensor_copy(iota[:], iota_i[:])
            pool.affine_select(out=rowmask[:], in_=rowmask[:], compare_op=ALU.is_ge, fill=0.0,
                               base=DEC_L - 1, pattern=[[DEC_L, DEC_B]], channel_multiplier=-1)\
                .then_inc(s_c, 1)

            def split_unit(r, s, landed, used, hi_done):
                pool.wait_ge(ld[r], landed)
                if used is not None:
                    pool.wait_ge(s_unit, used)
                pool.sem_inc(s_wbeg, 1)
                pool.tensor_scalar(w_hi[:, s, :], raw[:, r, :], 1.0, 1.0, ALU.mult, ALU.mult).then_inc(s_whi, 1)
                pool.wait_ge(s_whi, hi_done)
                pool.tensor_tensor(w_lo[:, s, :], raw[:, r, :], w_hi[:, s, :].bitcast(F32), ALU.subtract)\
                    .then_inc(s_w, 1)

            for n in range(RAW):
                split_unit(n, n % 2, 16, n - 1 if n >= 2 else None, n + 1)
            with pool.Fori(1, UNITS // RAW) as i:
                for r in range(RAW):
                    split_unit(r, r % 2, i * 16 + 16, i * RAW + r - 1, i * RAW + r + 1)
            for n in range(UNITS // RAW * RAW, UNITS):
                split_unit(n % RAW, n % 2, 16 * (n // RAW + 1), n - 1, n + 1)

        @block.tensor
        def _(pe):
            mm = pe.matmul

            def unit(n, L, mov_hi, mov_lo, k0=0, start=True, stop=True, slot=None, par=None,
                     ks=(0, KT)):
                s = n % 2 if slot is None else slot
                par = L % 2 if par is None else par
                all_tokens = n is not None and n < U_GA and n not in PARKED[N_A:]
                a, w_ = (acc[par], HF) if all_tokens else (acck[par], HK)
                t0 = 0 if all_tokens or mov_hi.shape[2] == TK else N_META
                for k in range(*ks):
                    wh, wl = (w[:, s, k * P:(k + 1) * P] for w in (w_hi, w_lo))
                    for i, (w, m) in enumerate(((wh, mov_hi), (wh, mov_lo), (wl, mov_hi))):
                        for h in range(2):
                            last = mm(a[:, h, :], w, m[:, k0 + k, t0 + h * w_:t0 + (h + 1) * w_],
                                      start=start and k == 0 and i == 0, stop=stop and k == KT - 1 and i == 2)
                if ks[1] == KT:
                    last.then_inc(s_unit, 1)

            def part(n, k0, k1, mov=(h_hi, h_lo), L=None):
                L = n if L is None else L
                if k0 == 0:
                    if L >= 2:
                        pe.wait_ge(s_accf[L % 2], L // 2)
                    pe.wait_ge(s_w, n + 1)
                unit(n, L, *mov, ks=(k0, k1))

            def tile(n, L, mov_hi, mov_lo, units_=1):
                if L >= 2:
                    pe.wait_ge(s_accf[L % 2], L // 2)
                for u in range(units_):
                    pe.wait_ge(s_w, n + u + 1)
                    unit(n + u, L, mov_hi, mov_lo, u * KT, u == 0, u == units_ - 1)

            def square_sum(i, first, last_one):
                pe.wait_ge(s_sq, i + 1)
                w = HF if i < KT else HK
                for h in range(2):
                    last = mm(ssp[:, h, 0:w], ones, squares_of(i)[:, h * w:(h + 1) * w],
                              start=first, stop=last_one)
                last.then_inc(s_ss, 1)

            def square_sums(i0):
                for k in range(KT):
                    square_sum(i0 + k, k == 0, k == KT - 1)

            def added_squares(r):
                pe.wait_ge(s_sqa, KT * (r - GROUPS))
                for h in range(2):
                    last = mm(ssp[:, h, 0:HK], ones, sqa[:, h * HK:(h + 1) * HK], start=True, stop=True)
                last.then_inc(s_ss, 1)

            def turn(r):
                pe.wait_ge(s_var, r + 1)
                nq = (TK if r else T) // NT
                for i in range(NT):
                    last = mm(turned[0:nq, i:i + 1], sums_row[0:1, i * nq:(i + 1) * nq], ones[0:1, 0:1],
                              start=True, stop=True)
                last.then_inc(s_turn, 1)

            def spread_out(r):
                pe.wait_ge(s_diag, r + 1)
                nq, w = (TK // NT, HK) if r else (NQ, HF)
                for h in range(2):
                    last = mm(inv[:, h, 0:w], ones[0:nq, :], spread[0:nq, h * w:(h + 1) * w], start=True, stop=True)
                last.then_inc(s_inv, 1)

            def first_tile(n, L, mov, ready):
                units_ = mov[0].shape[1] // KT
                for k in range(KT * units_):
                    u, k1 = divmod(k, KT)
                    pe.wait_ge(ready, k + 1)
                    if k == 0:
                        pe.wait_ge(s_accf[L % 2], L // 2)
                    if k1 == 0:
                        pe.wait_ge(s_w, n + u + 1)
                    unit(n + u, L, *mov, u * KT, u == 0, u == units_ - 1, ks=(k1, k1 + 1))

            def two_tiles(n, L, mov, h0):
                for k in range(KT):
                    pe.wait_ge(s_h, h0 + k + 1)
                    part(n, k, k + 1, mov, L)
                    part(n + 1, k, k + 1, mov, L + 1)

            pe.wait_ge(s_c, 1)
            square_sums(0)
            turn(0)
            spread_out(0)
            two_tiles(U_DT, U_DT, (h_hi, h_lo), 0)
            for n in range(U_DT + 2, U_PARK + 1):
                tile(n, n, h_hi, h_lo)
                c = n - U_XBC - TURN0
                if c == 0:
                    pe.wait_ge(s_ds, 1)
                elif 0 < c <= NC:
                    pe.wait_ge(s_dTs, c)
                if 0 <= c < NC:
                    t0, w = CHUNKS[c]
                    pe.transpose(S0[0:w, 0:P], dq[:, t0:t0 + w], ident[:]).then_inc(s_dT, 1)
                elif c == NC:
                    mm(S0[:, 0:HEADS * NE], ones[0:HEADS, :], bde[:].rearrange("p h e -> p (h e)"),
                       start=True, stop=True).then_inc(s_dT, 1)

            pe.wait_ge(s_xbc, CT)

            for c, (t0, n) in enumerate(CHUNKS):
                sample = c == NC - 1
                for g in range(GROUPS):
                    s = c * GROUPS + g
                    ch = slice(t0, t0 + n)
                    Bg, Cg = bc[:, g, ch], bc[:, GROUPS + g, ch]
                    ys = s - GROUPS
                    n1 = U_PARK + 1 + s if ys < 0 else U_PARK + 1 + GROUPS + 2 * ys
                    if s:
                        pe.wait_ge(s_state, s)
                    else:
                        pe.wait_ge(s_dTs, NC + 1)
                    if ys < 0:
                        pe.transpose(S0[0:n, P:2 * P], Bg, ident[:])
                        for j in range(4):
                            last = pe.transpose(S3[0:n, j * P:(j + 1) * P], xs[:, 4 * g + j, ch], ident[:])
                        last.then_inc(s_pre, 1)
                        part(n1, 0, 4)
                        pe.wait_ge(s_wT, s + 1)
                        mm(S3, bT[0:n, :], xde[0:n, :], start=True, stop=True).then_inc(s_st, 1)
                        part(n1, 4, KT)
                        continue
                    pe.wait_ge(s_bd, ys + 1)
                    if ys:
                        pe.wait_ge(s_y2, ys)
                    for hh in range(2):
                        mm((S1, S2)[hh][0:n, 0:4 * n].rearrange("p (h q) -> p h q", h=4), ones_r[0:2 * HEADS, 0:n],
                           bd[:, 4 * hh:4 * hh + 4, 0:n], start=True, stop=True)
                    mm(S0[0:n, 0:n], Bg, Cg, start=True, stop=True)
                    pe.transpose(S0[0:n, P:2 * P], Bg, ident[:])
                    for j in range(4):
                        last = pe.transpose(S3[0:n, j * P:(j + 1) * P], xs[:, 4 * g + j, ch], ident[:])
                    last.then_inc(s_pre, 1)
                    beside = ((n1, 0, KT), (n1 + 1, 0, 4), (n1 + 1, 4, 6), (n1 + 1, 6, KT))
                    part(*beside[0])
                    pe.wait_ge(s_wT, s + 1)
                    for h in range(HPG):
                        last = mm(S1[0:n, h * HEADDIM:(h + 1) * HEADDIM], wT[0:n, h, 0:n],
                                  xdt[0:n, h * HEADDIM:(h + 1) * HEADDIM], start=True, stop=True)
                    if sample:
                        for hb in range(2):
                            k = 2 * g + hb
                            pe.wait_ge(s_pl[k % 3], 16 * (k // 3 + 1))
                        cmf = cm[:].rearrange("p b r -> p (b r)")
                        for b in range(DEC_B):
                            last = mm(S2[0:n, :], cmf[:, b * TS:(b + 1) * TS],
                                      prev[:, (2 * g + b // 4) % 3, b % 4, :],
                                      start=b == 0, stop=b == DEC_B - 1)
                    else:
                        last = mm(S2[0:n, :], Cg, state[:, g, :], start=True, stop=True)
                    last.then_inc(s_y, 1)
                    if not sample:
                        mm(S3, bT[0:n, :], xde[0:n, :], start=True, stop=True).then_inc(s_st, 1)
                    part(*beside[1])
                    pe.wait_ge(s_ysb, ys + 1)
                    for j in range(4):
                        last = pe.transpose(S0[:, j * n:(j + 1) * n], ysb[0:n, j * P:(j + 1) * P],
                                            ident[0:n, 0:n])
                    last.then_inc(s_yT, 1)
                    if sample:
                        for q_ in range(4):
                            if q_ == 1:
                                pe.wait_ge(s_y2, ys + 1)
                            if q_ >= 2:
                                pe.wait_ge(s_snew, 4 * g + q_ - 1)
                            for b in range(2):
                                last = mm(pair_banks[q_ % 2][:, b, :], bTm[:, 2 * q_ + b, :], xde[0:n, :],
                                          start=True, stop=True)
                            last.then_inc(s_sst, 1)
                            if q_ in (0, 2):
                                part(*beside[2 + q_ // 2])
                    else:
                        part(*beside[2])
                        part(*beside[3])

            for n in range(U_GA + 1, U_AO):
                tile(n, n, h_hi, h_lo)
            v = (v_hi, v_lo)

            def group_sums(g):
                for j in range(4 * g, 4 * g + 4):
                    square_sum(KT + j, j % 4 == 0, j % 4 == 3)

            first_tile(U_AO, U_AO, v, s_v)
            group_sums(0)
            part(U_AO + 1, 0, 2, v)
            turn(1)
            part(U_AO + 1, 2, 6, v)
            spread_out(1)
            part(U_AO + 1, 6, KT, v)
            for g in range(1, GROUPS):
                n = U_AO + 2 * g
                group_sums(g)
                part(n, 0, 4, v)
                turn(1 + g)
                part(n, 4, KT, v)
                if g < GROUPS - 1:
                    part(n + 1, 0, KT, v)
                pe.wait_ge(s_nf, 4 * g)
                spread_out(1 + g)
            part(U_AO + KT - 1, 0, KT, v)
            first_tile(U_SO, U_SO, (n_hi, n_lo), s_n)
            for j in range(1, KT):
                tile(U_SO + 2 * j, U_SO + j, n_hi, n_lo, 2)
            first_tile(U_WO, L_WO, (m_hi, m_lo), s_m)
            for j in range(1, KT):
                tile(U_WO + j, L_WO + j, m_hi, m_lo)
            added_squares(1 + GROUPS)
            turn(1 + GROUPS)
            spread_out(1 + GROUPS)
            two_tiles(U_WQ, U_WQ - L_SHIFT, (g_hi, g_lo), KT)
            for j in range(2, N_WQ):
                tile(U_WQ + j, U_WQ - L_SHIFT + j, g_hi, g_lo)
            pe.wait_ge(s_q, N_WQ)
            pe.wait_ge(s_key, 16)
            L0 = U_PEER - L_SHIFT

            def unit_pair(m, half, mov):
                for b in range(2):
                    par = (L0 + b) % 2
                    pe.wait_ge(s_w, U_PEER + b + 1 + m)
                    pe.wait_ge(s_accf[par], (L0 + b) // 2 + half)
                    unit(None, None, mov[0], mov[1], slot=(U_PEER + b) % 2, par=par)

            def scores(tt):
                t0, n = TT[tt]
                for i in range(2 * PH):
                    last = mm(ps[0:n, 4 + i // 4, i % 4 * P:(i % 4 + 1) * P], q[:, i, t0:t0 + n],
                              key_sb[:, i, :], start=True, stop=True)
                last.then_inc(s_sc, 1)

            h_all = (g_hi, g_lo)
            scores(0)
            for tt, (t0, n) in enumerate(TT):
                unit_pair(8 * tt, 4 * tt, h_all)
                if tt + 1 < len(TT):
                    pe.wait_ge(s_scs, tt + 1)
                    if tt:
                        pe.wait_ge(s_pks, tt)
                    scores(tt + 1)
                with pe.Fori(0, 3) as j:
                    unit_pair(j * 2 + (8 * tt + 2), j + (4 * tt + 1), h_all)
                if tt + 1 < len(TT):
                    pe.wait_ge(s_scs, tt + 2)
                else:
                    unit_pair(M_TOP - 4, M_TOP // 2 - 2, h_all)
                pe.wait_ge(s_pk, tt + 1)
                for i in range(3):
                    last = pe.transpose(S0[:, i * P:i * P + n], pick[0:n, i, :], ident[0:n, 0:n])
                last.then_inc(s_pkT, 1)

            def gates(b, par, first):
                pe.wait_ge(s_oh, b + 1)
                if not first:
                    pe.wait_ge(s_gt, b)
                for j in range(TB):
                    for i in range(3):
                        last = mm(ps[:, 4 + j // 4, j % 4 * P:(j % 4 + 1) * P], oh_g[:, par, i, j, :],
                                  oh_2[:, par, j, :], start=i == 0, stop=i == 2)
                last.then_inc(s_gm, 1)

            unit_pair(M_TOP - 2, M_TOP // 2 - 1, h_all)
            pe.wait_ge(s_pks, len(TT))
            for b in range(2):
                gates(b, b, b == 0)
                unit_pair(M_TOP + 2 * b, M_TOP // 2 + b, h_all)
            with pe.Fori(1, NB // 2) as i:
                for par in range(2):
                    gates(i * 2 + par, par, False)
                    unit_pair(i * 4 + (M_TOP + 2 * par), i * 2 + (M_TOP // 2 + par), h_all)
            for b in range(NB // 2 * 2, NB):
                gates(b, b % 2, False)
                unit_pair(M_TOP + 2 * b, M_TOP // 2 + b, h_all)
            with pe.Fori(0, (NKEYS - M_GATE) // 2) as j:
                unit_pair(j * 2 + M_GATE, j + M_GATE // 2, h_all)

            def outputs(g, par):
                with pe.Fori(0, KT // 2) as j:
                    pe.wait_ge(s_p, g * GI + GI)
                    unit_pair(g * KT + j * 2 + NKEYS, g * (KT // 2) + j + NKEYS // 2, (p_hi[par], p_lo[par]))

            with pe.Fori(0, NG // 2) as i:
                for par in range(2):
                    outputs(i * 2 + par, par)

            added_squares(2 + GROUPS)
            turn(2 + GROUPS)
            spread_out(2 + GROUPS)

        @block.scalar
        def _(act):
            chain = [0]

            def link(ins):
                chain[0] += 1
                ins.then_inc(s_ac, 1)
                act.wait_ge(s_ac, chain[0])

            def square(i, src):
                a = i - KT - XT
                if a >= 2:
                    act.wait_ge(s_sqa, a - 1)
                elif a < 0:
                    n = 4 if i >= KT else 2
                    if i >= n:
                        act.wait_ge(s_ss, i - n + 1)
                act.activation(squares_of(i), src, ACT.Square).then_inc(s_sq, 1)

            def deviation(r):
                act.wait_ge(s_vt, r + 1)
                nq = (TK if r else T) // NT
                act.activation(root[0:nq, 1, :], root[0:nq, 0, :], ACT.Sqrt).then_inc(s_std, 1)

            def hi_parts(r, out):
                for k in range(KT):
                    act.wait_ge(s_hf, r * KT + k + 1)
                    act.activation(out[:, k, :], hf[k % 2][:, 0:out.shape[2]], ACT.Copy).then_inc(s_hhi, 1)

            for k in range(KT):
                if k % 2 == 0:
                    act.wait_ge(s_x[k // 2], 16)
                square(k, x[:, k, :])
            deviation(0)
            hi_parts(0, h_hi)
            act.wait_ge(s_in, 64)

            act.wait_ge(s_unit, 1)
            act.activation(halves(sp[0][:]), acc[0][0:HEADS], ACT.Identity, bias=hd[:, 0:1])
            act.activation(halves(sp[1][:]), acc[0][0:HEADS], ACT.Abs, bias=hd[:, 0:1]).then_inc(s_accf[0], 1)
            act.wait_ge(s_accf[0], 1)
            act.activation(sp[2][:], sp[1][:], ACT.Exp, scale=-1.0).then_inc(s_spe, 1)
            act.activation(hd[:, 2:3], hd[:, 1:2], ACT.Exp).then_inc(s_spe, 1)

            def park(b):
                n = PARKED[b]
                if b >= 2:
                    act.wait_ge(s_parked[b % 2], 16 * (b // 2))
                act.wait_ge(s_unit, n + 1)
                f = ACT.Copy if b < N_A else ACT.Silu if b < N_A + N_Z else ACT.Sigmoid
                a, w = (acc, T) if b < N_A else (acck, TK)
                act.activation(halves(stage[b % 2][:, 0:w]), a[n % 2], f).then_inc(s_accf[n % 2], 1)
                act.wait_ge(s_accf[n % 2], n // 2 + 1)
                act.dma_start(spill[b][:, 0:w], stage[b % 2][:, 0:w]).then_inc(s_parked[b % 2], 16)

            park(0)
            park(1)
            act.wait_ge(s_sp, 1)
            act.activation(dq[64:96, :], dq[0:32, :], ACT.Exp).then_inc(s_de, 1)
            act.activation(sp[3][:], sp[2][:], ACT.Exp).then_inc(s_de, 1)
            park(2)
            park(3)

            for j in range(CT + 1):
                if j < CT:
                    n = U_XBC + j
                    line = line_s[j % 2]
                    if j >= 2:
                        act.wait_ge(s_cv, j - 1)
                    else:
                        act.wait_ge(s_sp, 2)
                    act.activation(sample_view(line[:, HS + TP:])[:, :, 0:HS], hists[:, j], ACT.Copy)
                    act.wait_ge(s_unit, n + 1)
                    ps_ = pieces(acc[n % 2], line, HS)
                    act.activation(ps_[0][1], ps_[0][0], ACT.Copy)
                    act.activation(ps_[1][1], ps_[1][0], ACT.Copy)
                    act.activation(ps_[2][1], ps_[2][0], ACT.Copy).then_inc(s_accf[n % 2], 1)
                if j:
                    i = j - 1
                    act.wait_ge(s_cv, i + 1)
                    cv = cv_s[i % 2]
                    dst = xs[:, i, :] if i < XT else bc[:, i - XT, :]
                    act.activation(dst[:, 0:TP], cv[:, 0:TP], ACT.Silu, bias=c_("cb", i))
                    act.activation(sample_view(dst[:, TP:]), line_out(cv, HS), ACT.Silu, bias=c_("cb", i))\
                        .then_inc(s_xbc, 1)
                c = j - TURN0
                if 0 <= c < NC:
                    w = CHUNKS[c][1]
                    act.wait_ge(s_dT, c + 1)
                    act.activation(dqT[0:w, c, :], S0[0:w, 0:P], ACT.Copy).then_inc(s_dTs, 1)
                elif c == NC:
                    act.wait_ge(s_dT, NC + 1)
                    act.activation(dend[:].rearrange("p h e -> p (h e)"), S0[:, 0:HEADS * NE], ACT.Copy)\
                        .then_inc(s_dTs, 1)

            park(N_PRE)

            def load_states(k):
                act.dma_start(prev[:, k % 3], ssm_in[:, k // 2, k % 2 * 4:k % 2 * 4 + 4]).then_inc(s_pl[k % 3], 16)

            def store_states(k):
                act.wait_ge(s_snew, 2 * k + 2)
                act.dma_start(ssm_s[:, k // 2, k % 2 * 4:k % 2 * 4 + 4], prev[:, k % 3]).then_inc(s_po[k % 3], 16)

            def stored_states(k):
                act.wait_ge(s_po[k % 3], 16 * (k // 3 + 1))

            for k in range(3):
                load_states(k)
            for c, (t0, n) in enumerate(CHUNKS):
                sample = c == NC - 1
                for g in range(GROUPS):
                    s = c * GROUPS + g
                    if c == 0:
                        park(N_PRE + 1 + s)
                        continue
                    ys = s - GROUPS
                    act.wait_ge(s_seg, ys + 1)
                    link(act.activation(seg[0:n, :, 0:n], seg[0:n, :, 0:n], ACT.Relu, scale=-1.0))
                    act.activation(seg[0:n, :, 0:n], seg[0:n, :, 0:n], ACT.Exp, scale=-1.0).then_inc(s_exp, 1)
                    b1 = N_PRE + 1 + GROUPS + 2 * ys
                    if sample and g:
                        stored_states(2 * g - 1)
                        if 2 * g + 2 < 2 * GROUPS:
                            load_states(2 * g + 2)
                    park(b1)
                    if sample:
                        store_states(2 * g)
                    if b1 + 1 < N_PARK:
                        park(b1 + 1)
                    if sample:
                        stored_states(2 * g)
                        if 2 * g + 3 < 2 * GROUPS:
                            load_states(2 * g + 3)
                        store_states(2 * g + 1)
                if c == NC - 2:
                    act.wait_ge(s_state, (NC - 1) * GROUPS)
                    act.dma_start(ssm_p, state[:]).then_inc(s_out, 16)

            for b in range(2):
                act.wait_ge(s_parked[b], 16 * N_PARK // 2)
            act.wait_ge(s_y2, (NC - 1) * GROUPS)
            act.wait_ge(s_out, 16)

            def load_cxb(i):
                act.dma_start(cxb[i % 2][:], spill[3 * i:3 * i + 3].rearrange("a p t -> p a t"))\
                    .then_inc(s_cxb[i % 2], 16)

            def load_z(g):
                z0 = N_A + 4 * g
                act.dma_start(zb[g % 2][:], spill[z0:z0 + 4, :, 0:TK].rearrange("a p t -> p a t"))\
                    .then_inc(s_zl[g % 2], 16)


            def gate_a(i):
                n = U_GA + i
                act.wait_ge(s_unit, n + 1)
                act.activation(halves(ma[:, i, :]), acck[n % 2], ACT.Sigmoid).then_inc(s_accf[n % 2], 1)

            load_cxb(0)
            gate_a(0)
            stored_states(2 * GROUPS - 1)
            load_cxb(1)
            load_z(0)
            act.dma_start(new_s, news[:]).then_inc(s_out, 16)
            gate_a(1)
            for i in range(KT):
                act.wait_ge(s_vf, i + 1)
                act.activation(v_hi[:, i, :], v_f[i % 2][:], ACT.Copy).then_inc(s_vhi, 1)
                if i + 2 < KT:
                    load_cxb(i + 2)
                elif i == KT - 2:
                    load_z(1)
                if i + 2 < KT:
                    gate_a(i + 2)
            act.wait_ge(s_v, KT)
            act.dma_start(new_a, newa[:]).then_inc(s_out, 16)

            def group_squares(g):
                for j in range(4 * g, 4 * g + 4):
                    act.wait_ge(s_gz, j + 1)
                    square(KT + j, kept(xs[:, j, :]))
                if g + 2 < GROUPS:
                    load_z(g + 2)
                else:
                    i0 = 4 * (g - 2)
                    b0 = N_A + N_Z + i0
                    act.dma_start(sgb[:, i0:i0 + 4, :], spill[b0:b0 + 4, :, 0:TK].rearrange("a p t -> p a t"))\
                        .then_inc(s_gbl[g - 2], 16)

            act.wait_ge(s_unit, U_AO)
            group_squares(0)
            deviation(1)
            group_squares(1)
            for g in range(GROUPS):
                for j in range(4 * g, 4 * g + 4):
                    if j % 4 == 2 and g + 1 < GROUPS:
                        deviation(2 + g)
                        if g + 2 < GROUPS:
                            group_squares(g + 2)
                    act.wait_ge(s_nf, j + 1)
                    act.activation(kept(n_hi[:, j, :]), hf[j % 2][:, 0:TK], ACT.Copy).then_inc(s_nhi, 1)
            for j in range(KT):
                act.wait_ge(s_mf, j + 1)
                act.activation(m_hi[:, j, :], ma[:, j, :], ACT.Copy).then_inc(s_mhi, 1)
            act.dma_start(x[:], xT).then_inc(s_xr, 16)
            for k in range(KT):
                act.wait_ge(s_x1, k + 1)
                square(KT + XT + k, kept(x[:, k, :]))
            deviation(1 + GROUPS)
            hi_parts(1, g_hi)
            act.wait_ge(s_h, 2 * KT)
            act.dma_start(key_sb[:], keys).then_inc(s_key, 16)
            for j in range(N_WQ):
                n, L = U_WQ + j, U_WQ - L_SHIFT + j
                act.wait_ge(s_unit, n + 1)
                link(act.activation(halves(q[:, j, :]), acck[L % 2], ACT.Copy))
                act.sem_inc(s_accf[L % 2], 1)
                act.sem_inc(s_q, 1)
            L0 = U_PEER - L_SHIFT

            def gelu(m, half, b, first=False):
                par = (L0 + b) % 2
                if not first:
                    act.wait_ge(s_as[b], half * 16)
                act.wait_ge(s_unit, U_PEER + 1 + m)
                act.activation(halves(ge[b][:]), acck[par], ACT.Gelu).then_inc(s_accf[par], 1)
                act.wait_ge(s_accf[par], (L0 + b) // 2 + 1 + half)
                act.dma_start(act_dram[bass.ds(m, 1)].rearrange("a p t -> (a p) t"), ge[b][:])\
                    .then_inc(s_as[b], 16)

            def scores_out(tt):
                n = TT[tt][1]
                act.wait_ge(s_sc, tt + 1)
                if tt:
                    act.wait_ge(s_scf, tt)
                act.activation(sc[0:n].rearrange("p (a b) k -> p a (b k)", a=4), ps[0:n, 4:8, :], ACT.Copy)\
                    .then_inc(s_scs, 1)

            scores_out(0)
            for tt, (t0, n) in enumerate(TT):
                for m in range(8 * tt, 8 * tt + 8 if tt + 1 < len(TT) else M_TOP - 2):
                    if m == 8 * tt + 3 and tt + 1 < len(TT):
                        scores_out(tt + 1)
                    if m == 8 * tt + 5:
                        act.wait_ge(s_be, tt + 1)
                        act.activation(best[0:n], best[0:n], ACT.Exp).then_inc(s_bx, 1)
                    gelu(m, m // 2, m % 2, m < 2)
                act.wait_ge(s_pkT, tt + 1)
                act.activation(pickT[:, :, t0:t0 + n],
                               S0[:, 0:3 * P].rearrange("p (a t) -> p a t", a=3)[:, :, 0:n], ACT.Copy)\
                    .then_inc(s_pks, 1)

            for m in range(M_TOP - 2, M_TOP):
                gelu(m, m // 2, m % 2)

            def gates_out(b, par, stored):
                act.wait_ge(s_gm, b + 1)
                if stored is not None:
                    act.wait_ge(s_gs[par], stored)
                act.activation(gt[:, par].rearrange("p i t -> p t i"),
                               ps[:, 4:8, :].rearrange("p a (t i) -> p (a t) i", i=P),
                               ACT.Copy).then_inc(s_gt, 1)
                act.wait_ge(s_gt, b + 1)
                act.dma_start(gate_dram[:, :, bass.ds(b, 1)].rearrange("g p a i -> p g (a i)"),
                              gt[:, par].rearrange("p (g i) t -> p g (i t)", g=2 * NG))\
                    .then_inc(s_gs[par], 16)

            for b in range(2):
                gates_out(b, b, None)
                for c in range(2):
                    gelu(M_TOP + 2 * b + c, M_TOP // 2 + b, c)
            with act.Fori(1, NB // 2) as i:
                for par in range(2):
                    gates_out(i * 2 + par, par, i * 16)
                    for c in range(2):
                        gelu(i * 4 + (M_TOP + 2 * par + c), i * 2 + (M_TOP // 2 + par), c)
            for b in range(NB // 2 * 2, NB):
                gates_out(b, b % 2, 16 * (b // 2))
                for c in range(2):
                    gelu(M_TOP + 2 * b + c, M_TOP // 2 + b, c)
            act.wait_ge(s_gs[0], 16 * ((NB + 1) // 2))
            act.wait_ge(s_gs[1], 16 * (NB // 2))

            def load_half(g, hb):
                act.dma_start(abuf[:, hb], act_dram[bass.ds(g * GI + hb * (GI // 2), GI // 2)]
                              .rearrange("m p t -> p m t")).then_inc(s_al[hb], 16)
                act.dma_start(gbuf[:, hb].rearrange("p b i t -> p b (i t)"),
                              gate_dram[bass.ds(g * 2 + hb, 1)].rearrange("a p b i -> (a p) b i"))\
                    .then_inc(s_gl[hb], 16)

            def hi_part(g, u, par):
                act.wait_ge(s_pm, g * GI + u + 1)
                act.activation(p_hi[par][:, u, :], abuf[:, u // 4, u % 4, :], ACT.Copy).then_inc(s_phi, 1)

            for hb in range(2):
                load_half(0, hb)
            for m in range(M_GATE, NKEYS):
                gelu(m, m // 2, m % 2)
                i = m - M_GATE - 4
                if 0 <= i < GI // 2:
                    for u in (2 * i, 2 * i + 1):
                        hi_part(0, u, 0)
                if i in (2, 4):
                    act.wait_ge(s_p, 2 * i)
                    load_half(1, i // 2 - 1)
            for b in range(2):
                act.wait_ge(s_as[b], 16 * NKEYS // 2)

            def group(g, par, load):
                for u in range(GI):
                    hi_part(g, u, par)
                    if load and u % 4 == 3:
                        act.wait_ge(s_p, g * GI + u + 1)
                        load_half(g + 1, u // 4)

            group(1, 1, True)
            with act.Fori(1, NG // 2 - 1) as i:
                group(i * 2, 0, True)
                group(i * 2 + 1, 1, True)
            group(NG - 2, 0, True)
            group(NG - 1, 1, False)

            for k in range(KT):
                act.wait_ge(s_x2, GI * (NG - 1) + k + 1)
                square(2 * KT + XT + k, kept(x[:, k, :]))
            deviation(2 + GROUPS)
            for k in range(KT):
                act.wait_ge(s_yo, k + 1)
                act.dma_start(yT[:, k], yo[k % 2][:]).then_inc(s_yd[k % 2], 16)
            act.wait_ge(s_out, 48)
            for i in range(2):
                act.wait_ge(s_yd[i], 16 * KT // 2)

        @block.vector
        def _(dve):
            chain = [0]

            def link(ins):
                chain[0] += 1
                ins.then_inc(s_dc, 1)
                dve.wait_ge(s_dc, chain[0])

            tt_, ts_, stt = dve.tensor_tensor, dve.tensor_scalar, dve.scalar_tensor_tensor

            def rsqrt(r, scale, ss_done, between=None):
                w_ = TK if r else T
                nq = w_ // NT
                dve.wait_ge(s_ss, ss_done)
                ts_(halves(sums_row[0:1, 0:w_]), ssp[0:1, :, 0:w_ // 2], scale, EPS, ALU.mult, ALU.add)\
                    .then_inc(s_var, 1)
                if between:
                    between()
                v, i, w = (root[0:nq, k, :] for k in range(3))
                dve.wait_ge(s_turn, r + 1)
                dve.tensor_copy(v, turned[0:nq]).then_inc(s_vt, 1)
                dve.wait_ge(s_vt, r + 1)
                dve.wait_ge(s_std, r + 1)
                link(dve.reciprocal(i, i))
                link(tt_(w, i, i, ALU.mult))
                link(tt_(w, w, v, ALU.mult))
                link(ts_(w, w, -0.5, 1.5, ALU.mult, ALU.add))
                link(tt_(i, i, w, ALU.mult))
                tt_(spread[0:nq, 0:w_].rearrange("p (a b) -> p a b", a=NT),
                    ident[0:nq, 0:nq].unsqueeze(1).to_broadcast([nq, NT, nq]),
                    i.unsqueeze(2).to_broadcast([nq, NT, nq]), ALU.mult).then_inc(s_diag, 1)
            def normed(r, w, out_lo, out_hi):
                n = out_lo.shape[2]
                for k in range(KT + 1):
                    if k < KT:
                        if k >= 2:
                            dve.wait_ge(s_h, r * KT + k - 1)
                        stt(halves(hf[k % 2][:, 0:n]), halves(x[:, k, T - n:]), c_(w, k), inv[:, :, 0:n // 2],
                            ALU.mult, ALU.mult).then_inc(s_hf, 1)
                    if k:
                        i = k - 1
                        dve.wait_ge(s_hhi, r * KT + i + 1)
                        dve.wait_ge(s_hf, r * KT + i + 1)
                        tt_(out_lo[:, i, :], hf[i % 2][:, 0:n], out_hi[:, i, :].bitcast(F32), ALU.subtract)\
                            .then_inc(s_h, 1)

            dve.wait_ge(s_in, 64)
            rsqrt(0, 1.0 / D, KT)
            dve.wait_ge(s_inv, 1)
            normed(0, "mix", h_lo, h_hi)

            dve.memset(reset[:], 1.0)
            dve.wait_ge(s_spe, 2)
            link(ts_(sp[1][:], sp[2][:], 2.0, None, ALU.add))
            link(dve.reciprocal(sp[1][:], sp[1][:]))
            link(tt_(sp[1][:], sp[1][:], sp[2][:], ALU.mult))
            link(tt_(sp[2][:], sp[1][:], sp[1][:], ALU.mult))
            link(ts_(sp[3][:], sp[2][:], 2.0 / 17, 2.0 / 15, ALU.mult, ALU.add))
            for k in (13, 11, 9, 7, 5, 3, 1):
                link(tt_(sp[3][:], sp[3][:], sp[2][:], ALU.mult))
                link(ts_(sp[3][:], sp[3][:], 2.0 / k, None, ALU.add))
            link(tt_(sp[3][:], sp[3][:], sp[1][:], ALU.mult))
            dve.memset(reset[:, 0:1], 0.0)
            dve.memset(reset[:, N_META:TP:P], 0.0)
            dve.memset(reset[:, TP:T:DEC_L], 0.0)
            link(stt(dq[32:64, :], sp[0][:], 0.0, sp[3][:], ALU.max, ALU.add))
            link(ts_(sp[1][:], dq[32:64, :], hd[:, 2:3], -1.0, ALU.mult, ALU.mult))
            link(dve.tensor_tensor_scan(dq[0:32, :], reset[:], sp[1][:], 0.0, ALU.mult, ALU.add))
            dve.tensor_copy(fold[0:HEADS, :], ident[0:HEADS, 0:HEADS])
            dve.tensor_copy(fold[HEADS:, :], ident[HEADS:2 * HEADS, HEADS:2 * HEADS])
            for c, (t0, n) in enumerate(CHUNKS[:-1]):
                last_c = dq[0:32, t0 + n - 1:t0 + n]
                ts_(sp[2][:, t0:t0 + n], dq[0:32, t0:t0 + n], last_c, -1.0, ALU.subtract, ALU.mult)
            cs = sample_view(dq[0:32, TP:T])
            tt_(sample_view(sp[2][:, TP:T]), cs[:, :, DEC_L - 1:DEC_L].to_broadcast([HEADS, DEC_B, DEC_L]), cs,
                ALU.subtract).then_inc(s_sp, 1)
            dve.wait_ge(s_de, 2)
            link(dve.tensor_copy(sp[1][:], dq[32:64, :]))
            tt_(dq[96:128, :], sp[3][:], sp[1][:], ALU.mult)
            link(dve.tensor_copy(sp[0][:, 0:1], dq[64:96, N_META - 1:N_META]))
            dve.tensor_copy(sp[0][:, 1:NC - 1], dq[64:96, N_META + P - 1:TP:P])
            link(dve.tensor_copy(sp[0][:, NC - 1:NE], dq[64:96, TP + DEC_L - 1:T:DEC_L]))
            link(tt_(bde[:], ident[0:HEADS, 0:HEADS].unsqueeze(2).to_broadcast([HEADS, HEADS, NE]),
                     sp[0][:, 0:NE].unsqueeze(1).to_broadcast([HEADS, HEADS, NE]), ALU.mult))
            link(dve.tensor_copy(cum2[0:HEADS, :], dq[0:HEADS, :]))
            tt_(cum2[HEADS:, :], dq[0:HEADS, :], cum2[0:HEADS, :].bitcast(F32), ALU.subtract)
            dve.memset(line_s[0][:, 0:HS], 0.0)
            dve.memset(line_s[1][:, 0:HS], 0.0)
            link(dve.memset(cm[:], 0.0))
            dve.sem_inc(s_ds, 1)
            dve.sem_inc(s_sp, 1)

            for j in range(CT):
                line, cv = line_s[j % 2], cv_s[j % 2]
                W = LS - HS
                dve.wait_ge(s_accf[(U_XBC + j) % 2], (U_XBC + j) // 2 + 1)
                if j >= 2:
                    dve.wait_ge(s_xbc, j - 1)
                link(ts_(cv[:, 0:W], line[:, 0:W], c_("cs", 4 * j), None, ALU.mult))
                link(stt(cv[:, 0:W], line[:, 1:W + 1], c_("cs", 4 * j + 1), cv[:, 0:W], ALU.mult, ALU.add))
                link(stt(cv[:, 0:W], line[:, 2:W + 2], c_("cs", 4 * j + 2), cv[:, 0:W], ALU.mult, ALU.add))
                dve.tensor_copy(news[:, j, 0, :], line[:, TP:HS + TP])
                dve.tensor_copy(news[:, j, 1:, :], sample_view(line[:, HS + TP:])[:, :, DEC_L:])
                stt(cv[:, 0:W], line[:, 3:W + 3], c_("cs", 4 * j + 3), cv[:, 0:W], ALU.mult, ALU.add)\
                    .then_inc(s_cv, 1)

            def head_rows(s):
                t0, n = CHUNKS[s // GROUPS]
                h0 = s % GROUPS * HPG
                tt_(bd[:, :, 0:n], fold[:, h0:h0 + HPG].unsqueeze(2).to_broadcast([2 * HEADS, HPG, n]),
                    cum2[:, t0:t0 + n].bitcast(F32).unsqueeze(1).to_broadcast([2 * HEADS, HPG, n]), ALU.mult)\
                    .then_inc(s_bd, 1)

            dve.wait_ge(s_dTs, NC + 1)
            dve.wait_ge(s_xbc, CT)
            head_rows(GROUPS)
            for c, (t0, n) in enumerate(CHUNKS):
                sample = c == NC - 1
                mask = smask[:].rearrange("p b r -> p (b r)") if sample else causal[0:n, 0:n]
                for g in range(GROUPS):
                    s = c * GROUPS + g
                    hs = slice(g * HPG, (g + 1) * HPG)

                    def per_head(i, w):
                        return dqT[0:n, c, i * 32 + g * HPG:i * 32 + (g + 1) * HPG].unsqueeze(2)\
                            .to_broadcast([n, HPG, w])

                    if c == 0:
                        dve.wait_ge(s_pre, s + 1)
                        dve.tensor_copy(bT[0:n, :], S0[0:n, P:2 * P])
                        tt_(xde[0:n, :].rearrange("p (h w) -> p h w", h=HPG),
                            S3[0:n, :].rearrange("p (h w) -> p h w", h=HPG), per_head(3, HEADDIM), ALU.mult)\
                            .then_inc(s_wT, 1)
                        dve.wait_ge(s_st, s + 1)
                        dve.tensor_copy(state[:, g, :], S3).then_inc(s_state, 1)
                        continue
                    ys = s - GROUPS
                    if sample:
                        dve.tensor_copy(cm[:, :, 0:DEC_L], sample_view(bc[:, GROUPS + g, TP:T]))
                    dve.wait_ge(s_pre, s + 1)
                    cq = ps[0:n, 6:8, 0:4 * n].rearrange("p a (h q) -> p a h q", h=4)
                    ck = dqT[0:n, c, g * HPG:(g + 1) * HPG].rearrange("p (a h) -> p a h", a=2)\
                        .unsqueeze(3).to_broadcast([n, 2, 4, n])
                    tt_(seg[0:n, :, 0:n].rearrange("p (a h) q -> p a h q", a=2), cq, ck, ALU.subtract)\
                        .then_inc(s_seg, 1)
                    tt_(cbm[0:n, 0:n], S0[0:n, 0:n], mask, ALU.mult)
                    xg = S3[0:n, :].rearrange("p (h w) -> p h w", h=HPG)
                    tt_(xdt[0:n, :].rearrange("p (h w) -> p h w", h=HPG), xg, per_head(1, HEADDIM), ALU.mult)
                    if sample:
                        tt_(bTm[:], S0[0:n, P:2 * P].unsqueeze(1).to_broadcast([n, DEC_B, P]),
                            rowmask[:].unsqueeze(2).to_broadcast([n, DEC_B, P]), ALU.mult)
                    else:
                        dve.tensor_copy(bT[0:n, :], S0[0:n, P:2 * P])
                    link(tt_(xde[0:n, :].rearrange("p (h w) -> p h w", h=HPG), xg, per_head(3, HEADDIM), ALU.mult))
                    dve.wait_ge(s_exp, ys + 1)
                    tt_(wT[0:n, :, 0:n], seg[0:n, :, 0:n],
                        cbm[0:n, 0:n].unsqueeze(1).to_broadcast([n, HPG, n]), ALU.mult).then_inc(s_wT, 1)
                    if s + 1 < NC * GROUPS:
                        head_rows(s + 1)
                    dve.wait_ge(s_y, ys + 1)
                    link(tt_(ysb[0:n, :].rearrange("p (h w) -> p h w", h=HPG),
                             S2[0:n, :].rearrange("p (h w) -> p h w", h=HPG), per_head(2, HEADDIM), ALU.mult))
                    tt_(ysb[0:n, :], ysb[0:n, :], S1[0:n, :], ALU.add).then_inc(s_ysb, 1)

                    if sample:
                        for hb in range(2):
                            k = 2 * g + hb
                            e0 = NC - 1 + 4 * hb
                            dve.wait_ge(s_pl[k % 3], 16 * (k // 3 + 1))
                            pv = prev[:, k % 3].rearrange("p b (h w) -> p b h w", h=HPG)
                            link(tt_(pv, pv, dend[:, hs, e0:e0 + 4].rearrange("p h e -> p e h").unsqueeze(3)
                                     .to_broadcast([P, 4, HPG, HEADDIM]), ALU.mult))
                    else:
                        st = state[:, g, :]
                        sv = st.rearrange("p (h w) -> p h w", h=HPG)
                        link(tt_(sv, sv, dend[:, hs, c:c + 1].to_broadcast([P, HPG, HEADDIM]), ALU.mult))
                        dve.wait_ge(s_st, s + 1)
                        tt_(st, st, S3, ALU.add).then_inc(s_state, 1)
                    dve.wait_ge(s_yT, ys + 1)
                    for j in range(4):
                        xj = xs[:, 4 * g + j, t0:t0 + n]
                        last = stt(xj, xj, c_("dd", 4 * g + j), S0[:, j * n:(j + 1) * n], ALU.mult, ALU.add)
                    last.then_inc(s_y2, 1)
                    if sample:
                        for q_ in range(4):
                            pq = prev[:, (2 * g + q_ // 2) % 3, q_ % 2 * 2:q_ % 2 * 2 + 2, :]
                            dve.wait_ge(s_sst, 4 * g + q_ + 1)
                            tt_(pq, pq, pair_banks[q_ % 2], ALU.add).then_inc(s_snew, 1)
                        dve.wait_ge(s_snew, 4 * (g + 1))
                        dve.sem_inc(s_state, 1)

            dve.wait_ge(s_y2, (NC - 1) * GROUPS)
            dve.wait_ge(s_cxb[0], 16)
            dve.memset(line_a[:, 0:HA], 0.0)

            def v_low(i):
                dve.wait_ge(s_vhi, i + 1)
                tt_(v_lo[:, i, :], v_f[i % 2][:], v_hi[:, i, :].bitcast(F32), ALU.subtract).then_inc(s_v, 1)

            for i in range(KT):
                W = LA - HA
                if i:
                    dve.wait_ge(s_vf, i)
                dve.tensor_copy(sample_view(line_a[:, HA + TP:])[:, :, 0:HA], hista[:, i])
                C, X, B = (cxb[i % 2][:, a, :] for a in range(3))
                dve.wait_ge(s_cxb[i % 2], 16 * (i // 2 + 1))
                tt_(line_a[:, HA:HA + TP], C[:, 0:TP], X[:, 0:TP], ALU.mult)
                link(tt_(sample_view(line_a[:, HA + TP:])[:, :, HA:], sample_view(C[:, TP:]),
                         sample_view(X[:, TP:]), ALU.mult))
                if i:
                    v_low(i - 1)
                link(ts_(cv_a[:, 0:W], line_a[:, 0:W], c_("ca", 3 * i), None, ALU.mult))
                link(stt(cv_a[:, 0:W], line_a[:, 1:W + 1], c_("ca", 3 * i + 1), cv_a[:, 0:W], ALU.mult, ALU.add))
                link(stt(cv_a[:, 0:W], line_a[:, 2:W + 2], c_("ca", 3 * i + 2), cv_a[:, 0:W], ALU.mult, ALU.add))
                dve.tensor_copy(newa[:, i, 0, :], line_a[:, TP:HA + TP])
                dve.tensor_copy(newa[:, i, 1:, :], sample_view(line_a[:, HA + TP:])[:, :, DEC_L:])
                f = v_f[i % 2]
                tt_(f[:, 0:TP], B[:, 0:TP], cv_a[:, 0:TP], ALU.mult)
                tt_(sample_view(f[:, TP:]), sample_view(B[:, TP:]), line_out(cv_a, HA), ALU.mult)\
                    .then_inc(s_vf, 1)
            v_low(KT - 1)

            def gate_group(g):
                dve.wait_ge(s_zl[g % 2], 16 * (g // 2 + 1))
                for j in range(4):
                    xj = kept(xs[:, 4 * g + j, :])
                    tt_(xj, xj, zb[g % 2][:, j, :], ALU.mult).then_inc(s_gz, 1)

            def branch_a_out(i):
                dve.wait_ge(s_unit, U_AO + i + 1)
                tt_(halves(ma[:, i, :]), halves(ma[:, i, :]), acck[(U_AO + i) % 2], ALU.mult)\
                    .then_inc(s_accf[(U_AO + i) % 2], 1)

            def group_root(g):
                rsqrt(1 + g, 1.0 / GW, KT + 4 * g + 4, (lambda: gate_group(g + 1)) if g + 1 < GROUPS else None)

            gate_group(0)
            branch_a_out(0)
            group_root(0)
            for g in range(GROUPS):
                dve.wait_ge(s_inv, 2 + g)
                for j in range(4 * g, 4 * g + 4):
                    if j % 4 == 2 and g + 1 < GROUPS:
                        branch_a_out(2 * g + 1)
                        group_root(g + 1)
                    if j > 4 * g + 1:
                        dve.wait_ge(s_n, j - 1)
                    stt(halves(hf[j % 2][:, 0:TK]), halves(kept(xs[:, j, :])), c_("sn", j), inv[:, :, 0:HK],
                        ALU.mult, ALU.mult).then_inc(s_nf, 1)
                    dve.wait_ge(s_nhi, j + 1)
                    tt_(kept(n_lo[:, j, :]), hf[j % 2][:, 0:TK], kept(n_hi[:, j, :]).bitcast(F32),
                        ALU.subtract).then_inc(s_n, 1)
                branch_a_out(2 * g + 2 if g + 1 < GROUPS else 2 * g + 1)

            for j in range(KT):
                L = U_SO + j
                if j % 4 == 0:
                    dve.wait_ge(s_gbl[j // 4], 16)
                dve.wait_ge(s_unit, U_SO + 2 * j + 2)
                link(tt_(halves(mt[j % 2][:]), acck[L % 2], halves(sgb[:, j, :]), ALU.mult))
                dve.sem_inc(s_accf[L % 2], 1)
                tt_(ma[:, j, :], ma[:, j, :], mt[j % 2][:], ALU.add).then_inc(s_mf, 1)
                dve.wait_ge(s_mhi, j + 1)
                tt_(m_lo[:, j, :], ma[:, j, :], m_hi[:, j, :].bitcast(F32), ALU.subtract).then_inc(s_m, 1)
            dve.wait_ge(s_xr, 16)

            def add_squares(r, k):
                a = KT * (r - GROUPS - 1) + k
                dve.wait_ge(s_sq, KT + XT + a + 1)
                if k == 1:
                    tt_(sqa[:, 0:TK], squares_of(0)[:, 0:TK], squares_of(1)[:, 0:TK], ALU.add).then_inc(s_sqa, 2)
                else:
                    dve.wait_ge(s_sqa, a)
                    tt_(sqa[:, 0:TK], sqa[:, 0:TK], squares_of(k % 2)[:, 0:TK], ALU.add).then_inc(s_sqa, 1)

            for j in range(KT):
                L = L_WO + j
                dve.wait_ge(s_unit, U_WO + j + 1)
                xj = halves(kept(x[:, j, :]))
                link(tt_(xj, xj, acck[L % 2], ALU.add))
                dve.sem_inc(s_accf[L % 2], 1)
                dve.sem_inc(s_x1, 1)
                if j >= 2:
                    add_squares(1 + GROUPS, j - 1)
            add_squares(1 + GROUPS, KT - 1)
            rsqrt(1 + GROUPS, 1.0 / D, KT + XT + 1)
            dve.wait_ge(s_inv, 2 + GROUPS)
            normed(1, "ffn", g_lo, g_hi)

            def top16(vals, idx, src, src2, rows):
                for i in range(rows):
                    last = dve.max(vals[:, i, 0:8], src[:, i, :])
                link(last)
                for i in range(rows):
                    dve.max_index(idx[:, i, 0:8], vals[:, i, 0:8], src[:, i, :])
                    last = dve.match_replace(src2[:, i, :], vals[:, i, 0:8], src[:, i, :], LOWEST)
                link(last)
                for i in range(rows):
                    last = dve.max(vals[:, i, 8:16], src2[:, i, :])
                link(last)
                for i in range(rows):
                    last = dve.max_index(idx[:, i, 8:16], vals[:, i, 8:16], src2[:, i, :])
                link(last)

            def weight_parts(tt):
                t0, n = TT[tt]
                w = pickT[:, 2, t0:t0 + n]
                dve.wait_ge(s_pks, tt + 1)
                for i in range(3):
                    b, f = wb[:, i, 0:n], wpart[:, i, t0:t0 + n]
                    link(dve.tensor_copy(b, w))
                    link(dve.tensor_copy(f, b))
                    if i < 2:
                        link(tt_(w, w, f, ALU.subtract))

            for tt, (t0, n) in enumerate(TT):
                dve.wait_ge(s_scs, tt + 1)
                top16(top[0:n], topi[0:n], sc[0:n], sc2[0:n], 2 * PH)
                dve.sem_inc(s_scf, 1)
                if tt:
                    weight_parts(tt - 1)
                pair = top[0:n].rearrange("p (h i) k -> p h i k", i=2)
                shape = [n, PH, TOPK, TOPK]
                link(tt_(cand[0:n].rearrange("p h (j k) -> p h j k", j=TOPK),
                         pair[:, :, 0, :].unsqueeze(3).to_broadcast(shape),
                         pair[:, :, 1, :].unsqueeze(2).to_broadcast(shape), ALU.add))
                top16(best[0:n], besti[0:n].rearrange("p (h k) -> p h k", h=PH), cand[0:n], cand2[0:n], PH)
                link(dve.tensor_copy(sm[0:n, 0, :], best[0:n, :, 0]))
                tt_(best[0:n], best[0:n], sm[0:n, 0, :].unsqueeze(2).to_broadcast([n, PH, TOPK]),
                    ALU.subtract).then_inc(s_be, 1)
                ts_(bsel[0:n, 0, :], besti[0:n], 4, None, ALU.logical_shift_right)
                ts_(bsel[0:n, 1, :], besti[0:n], 15, None, ALU.bitwise_and)
                link(dve.tensor_copy(topf[0:n], topi[0:n]))
                link(dve.tensor_copy(bself[0:n], bsel[0:n]))
                keyf = topf[0:n].rearrange("p (h i) k -> p h i k", i=2)
                for i, eq in enumerate((cand, cand2)):
                    e3 = eq[0:n].rearrange("p h (k j) -> p (h k) j", j=TOPK)
                    tt_(e3, bself[0:n, i, :].unsqueeze(2).to_broadcast([n, PH * TOPK, TOPK]),
                        iota[0:n, 0:TOPK].unsqueeze(1).to_broadcast([n, PH * TOPK, TOPK]), ALU.is_equal)\
                        .then_inc(s_dc, 1)
                    chain[0] += 1
                dve.wait_ge(s_dc, chain[0])
                for i, eq in enumerate((cand, cand2)):
                    e4 = eq[0:n].rearrange("p h (k j) -> p h k j", j=TOPK)
                    tt_(e4, e4, keyf[:, :, i, :].unsqueeze(2).to_broadcast(shape), ALU.mult).then_inc(s_dc, 1)
                    chain[0] += 1
                dve.wait_ge(s_dc, chain[0])
                if tt:
                    dve.wait_ge(s_pkT, tt)
                for i, eq in enumerate((cand, cand2)):
                    dve.tensor_reduce(pick[0:n, i, :], eq[0:n].rearrange("p h (k j) -> p (h k) j", j=TOPK),
                                      AX.X, ALU.add)
                dve.wait_ge(s_bx, tt + 1)
                link(dve.tensor_reduce(sm[0:n, 0, :], best[0:n], AX.X, ALU.add))
                link(dve.reciprocal(sm[0:n, 1, :], sm[0:n, 0, :]))
                tt_(pick[0:n, 2, :].rearrange("p (h k) -> p h k", h=PH), best[0:n],
                    sm[0:n, 1, :].unsqueeze(2).to_broadcast([n, PH, TOPK]), ALU.mult).then_inc(s_pk, 1)

            def one_hots(b, par, first, t):
                if not first:
                    dve.wait_ge(s_gm, b - 1)
                tt_(oh_2[:, par], iota_b[:].unsqueeze(1).to_broadcast([P, TB, P]),
                    pickT[:, 1, t(0, TB)].unsqueeze(2).to_broadcast([P, TB, P]), ALU.is_equal)
                for j in range(TB):
                    for i in range(3):
                        last = ts_(oh_g[:, par, i, j, :], iota_b[:], pickT[:, 0, t(j, 1)], wpart[:, i, t(j, 1)],
                                   ALU.is_equal, ALU.mult)
                last.then_inc(s_oh, 1)

            dve.wait_ge(s_pks, len(TT))
            weight_parts(len(TT) - 1)
            link(dve.tensor_copy(iota_b[:], iota[:]))
            for b in range(2):
                one_hots(b, b, True, lambda j, w: slice(b * TB + j, b * TB + j + w))
            with dve.Fori(1, NB // 2) as i:
                for par in range(2):
                    one_hots(i * 2 + par, par, False, lambda j, w: bass.ds(i * 2 * TB + (par * TB + j), w))
            for b in range(NB // 2 * 2, NB):
                one_hots(b, b % 2, False, lambda j, w: slice(b * TB + j, b * TB + j + w))

            L0 = U_PEER - L_SHIFT + NKEYS

            def group(g, par, add):
                for u in range(GI):
                    a = abuf[:, u // 4, u % 4, :]
                    if u % 4 == 0:
                        dve.wait_ge(s_al[u // 4], g * 16 + 16)
                        dve.wait_ge(s_gl[u // 4], g * 16 + 16)
                    v = a.rearrange("p (n t) -> p n t", t=TB)
                    tt_(v, v, gbuf[:, u // 4, :, u % 4, :], ALU.mult).then_inc(s_pm, 1)
                    dve.wait_ge(s_phi, g * GI + u + 1)
                    tt_(p_lo[par][:, u, :], a, p_hi[par][:, u, :].bitcast(F32), ALU.subtract).then_inc(s_p, 1)
                    if add:
                        add_tile(g - 1, u)

            def add_tile(g, u):
                p_ = (L0 + u) % 2
                dve.wait_ge(s_unit, g * KT + (U_PEER + NKEYS + u + 1))
                xu = halves(kept(x[:, u, :]))
                tt_(xu, xu, acck[p_], ALU.add).then_inc(s_x2, 1)
                dve.wait_ge(s_x2, g * KT + u + 1)
                dve.sem_inc(s_accf[p_], 1)

            group(0, 0, False)
            group(1, 1, True)
            with dve.Fori(1, NG // 2) as i:
                group(i * 2, 0, True)
                group(i * 2 + 1, 1, True)
            for u in range(KT):
                add_tile(NG - 1, u)
                if u >= 2:
                    add_squares(2 + GROUPS, u - 1)
            add_squares(2 + GROUPS, KT - 1)

            rsqrt(2 + GROUPS, 1.0 / D, KT + XT + 2)
            dve.wait_ge(s_inv, 3 + GROUPS)
            for k in range(KT):
                if k >= 2:
                    dve.wait_ge(s_yd[k % 2], 16 * (k // 2))
                stt(halves(yo[k % 2][:]), halves(kept(x[:, k, :])), c_("fin", k), inv[:, :, 0:HK],
                    ALU.mult, ALU.mult).then_inc(s_yo, 1)


def inputs_of(x_prompt, x_sample, state_conv_a, state_conv_ssd, state_ssm, meta_tokens, norm_mix_w, w_in,
              conv_a_w, w_a_out, ssd_conv_w, ssd_conv_b, ssd_dt_bias, ssd_a_log, ssd_d, ssd_norm_w,
              w_ssd_out, w_o, norm_ffn_w, peer_w_q, peer_sub_keys, peer_u, peer_v, norm_final_w):
    import numpy as np
    A = lambda a: np.asarray(a)
    tokens = np.concatenate([A(meta_tokens), A(x_prompt)[0], A(x_sample).reshape(TS, D)], 0)
    xT = np.ascontiguousarray(tokens.reshape(T, KT, P).transpose(2, 1, 0))

    def tiles(w):
        return w.reshape(KT, P, -1, P).transpose(2, 1, 0, 3).reshape(-1, P, D)

    wi = A(w_in)[0]
    o = np.cumsum([0, D, D, D, 2 * D, CT * P, HEADS, D, D])
    aB, aC, aX, z, xbc, dt, ga, gb = (wi[:, o[i]:o[i + 1]] for i in range(8))
    dt_p = np.zeros((D, P), wi.dtype)
    dt_p[:, :HEADS] = dt
    units = np.empty((UNITS, P, D), wi.dtype)
    units[U_DT:U_PRE] = tiles(dt_p)
    units[U_XBC:U_PARK] = tiles(xbc)
    for i, w in enumerate((aC, aX, aB)):
        units[PARKED[i:N_A:3]] = tiles(w)
    units[PARKED[N_A:N_A + N_Z]] = tiles(z)
    units[PARKED[N_A + N_Z:]] = tiles(gb)
    units[U_AO:U_SO] = tiles(A(w_a_out)[0])
    units[U_GA:U_AO] = tiles(ga)
    so = A(w_ssd_out)[0].reshape(2, KT, P, KT, P).transpose(3, 0, 2, 1, 4).reshape(2 * KT, P, D)
    units[U_SO:U_WO] = so
    units[U_WO:U_WQ] = tiles(A(w_o)[0])
    units[U_WQ:U_PEER] = tiles(A(peer_w_q)[0])
    uu = A(peer_u)[0].reshape(NKEYS, NKEYS, KT, P).transpose(1, 3, 2, 0).reshape(NG, GI, P, D)
    vv = A(peer_v)[0].reshape(NKEYS, NG, GI, KT, P).transpose(1, 3, 0, 2, 4).reshape(NG, KT, P, D)
    e = units[U_PEER:].reshape(2 * NG, GI, P, D)
    e[:NG], e[NG:] = uu, vv
    keys = np.ascontiguousarray(A(peer_sub_keys)[0].transpose(3, 0, 1, 2).reshape(P, 2 * PH, NKEYS))
    colp = lambda a: A(a).reshape(-1, P).T
    cols = np.ascontiguousarray(np.concatenate([
        colp(norm_mix_w), colp(norm_ffn_w), colp(norm_final_w),
        A(conv_a_w)[0].reshape(3, KT, P).transpose(2, 1, 0).reshape(P, 3 * KT),
        A(ssd_conv_w)[0].reshape(4, CT, P).transpose(2, 1, 0).reshape(P, 4 * CT),
        colp(ssd_conv_b), colp(ssd_norm_w), colp(np.repeat(A(ssd_d)[0], HEADDIM))], 1))
    heads = np.ascontiguousarray(np.stack([A(ssd_dt_bias)[0], A(ssd_a_log)[0]], 1))
    hist = lambda a, n: np.ascontiguousarray(A(a)[0].reshape(DEC_B, -1, n, P).transpose(3, 2, 0, 1))
    ssm = np.ascontiguousarray(A(state_ssm)[0].reshape(DEC_B, GROUPS, GW, STATE).transpose(3, 1, 0, 2))
    return dict(xT=xT, units=units, keys=keys, cols=cols, heads=heads, hist_a=hist(state_conv_a, KT),
                hist_s=hist(state_conv_ssd, CT), ssm_in=ssm)


OUTS = dict(yT=(P, KT, TK), new_a=(P, KT, 1 + DEC_B, HA), new_s=(P, CT, 1 + DEC_B, HS),
            ssm_p=(P, GROUPS, GW), ssm_s=(P, GROUPS, DEC_B, GW))


def outputs_of(yT, new_a, new_s, ssm_p, ssm_s):
    import numpy as np
    y = yT.transpose(2, 1, 0).reshape(TK, D)
    conv = lambda a: np.ascontiguousarray(a.transpose(2, 3, 1, 0)).reshape(1, 1 + DEC_B, a.shape[3], -1)
    na, ns = conv(new_a), conv(new_s)
    sp = ssm_p.transpose(1, 2, 0).reshape(1, 1, HEADS, HEADDIM, STATE)
    ss = ssm_s.transpose(2, 1, 3, 0).reshape(1, DEC_B, HEADS, HEADDIM, STATE)
    c = np.ascontiguousarray
    return (c(y[:SEQ])[None], c(y[SEQ:]).reshape(DEC_B, DEC_L, D), c(na[:, :1]), c(ns[:, :1]), c(sp),
            c(na[:, 1:]), c(ns[:, 1:]), c(ss))


def kernel(**inputs):
    import numpy as np
    import concourse.bacc as bacc
    from concourse.bass_utils import run_bass_kernel_spmd

    nc = bacc.Bacc("TRN2", target_bir_lowering=False, num_devices=1)
    arrays = inputs_of(**inputs)
    args = [nc.dram_tensor(k, a.shape, mybir.dt.from_np(a.dtype), kind="ExternalInput").ap()
            for k, a in arrays.items()]
    args += [nc.dram_tensor(k, s, F32, kind="ExternalOutput").ap() for k, s in OUTS.items()]
    trunk(nc, *args)
    r = run_bass_kernel_spmd(nc, [arrays], core_ids=[0])
    return outputs_of(**{k: r.results[0][k] for k in OUTS})
```
